# Optimizing a Trainium2 kernel written in Bass

```python
import math
import jax
import jax.numpy as jnp
from jax import lax
import numpy as np

D_MODEL = 1024
BATCH = 1
SEQ = 256
DEPTH = 2

MEM_LEN = 256
HEAD_DIM = 64
MIX_WIDTH = 2 * D_MODEL
SSD_WIDTH = MIX_WIDTH // 2
RWKV_WIDTH = MIX_WIDTH - SSD_WIDTH
SSD_HEADS = SSD_WIDTH // HEAD_DIM
SSD_GROUPS = 2
SSD_STATE = 128
SSD_CONV = 4
SSD_CHUNK = 128
SSD_XBC = SSD_WIDTH + 2 * SSD_GROUPS * SSD_STATE
SSD_IN = SSD_WIDTH + SSD_XBC + SSD_HEADS
RWKV_HEADS = RWKV_WIDTH // HEAD_DIM
RWKV_DECAY_LORA = 64
RWKV_ICLR_LORA = 64
RWKV_GATE_LORA = 128
RWKV_IN = 3 * RWKV_WIDTH + RWKV_DECAY_LORA + RWKV_ICLR_LORA + RWKV_GATE_LORA
EVEN_IN = SSD_IN + RWKV_IN
MOBA_HEADS = D_MODEL // HEAD_DIM
MOBA_BLOCK = 256
MOBA_TOPK = 3
MOBA_QBLOCK = 128
XATTN_HEADS = 4
XATTN_HEAD_DIM = D_MODEL // XATTN_HEADS
FFN_RAW = -(-8 * D_MODEL // 3)
FFN_HIDDEN = -(-FFN_RAW // 256) * 256
N_EVEN = (DEPTH + 1) // 2
N_ODD = DEPTH // 2
DEEPNORM_ALPHA = (2 * DEPTH) ** 0.25
DEEPNORM_BETA = (8 * DEPTH) ** -0.25
LN_EPS = 1e-5
RMS_EPS = 1e-5
RWKV_LNX_EPS = 64e-5


F32 = jnp.float32

def _layer_norm(x, g, b):
    xf = x.astype(F32)
    mu = jnp.mean(xf, axis=-1, keepdims=True)
    var = jnp.mean(jnp.square(xf - mu), axis=-1, keepdims=True)
    return ((xf - mu) * lax.rsqrt(var + LN_EPS) * g + b).astype(x.dtype)

def _token_shift(s):
    return jnp.pad(s, ((0, 0), (1, 0), (0, 0)))[:, :-1]

def _causal_dwconv(u, w, b):
    k = w.shape[0]
    out = lax.conv_general_dilated(
        u, w.astype(u.dtype)[:, None, :], window_strides=(1,), padding=[(k - 1, 0)],
        dimension_numbers=("NWC", "WIO", "NWC"), feature_group_count=u.shape[-1])
    return out + b

def _ssd_chunked(xs, dt, a_neg, bm, cm):
    bsz, l, h, p = xs.shape
    g, n = bm.shape[2], bm.shape[3]
    rep = h // g
    nc = l // SSD_CHUNK
    bh = jnp.repeat(bm, rep, axis=2).reshape(bsz, nc, SSD_CHUNK, h, n)
    ch = jnp.repeat(cm, rep, axis=2).reshape(bsz, nc, SSD_CHUNK, h, n)
    xdt = (xs.astype(F32) * dt[..., None]).reshape(bsz, nc, SSD_CHUNK, h, p)
    a = (dt * a_neg).reshape(bsz, nc, SSD_CHUNK, h).transpose(0, 3, 1, 2)
    a_cum = jnp.cumsum(a, axis=-1)
    causal = jnp.tril(jnp.ones((SSD_CHUNK, SSD_CHUNK), dtype=bool))
    seg = a_cum[..., :, None] - a_cum[..., None, :]
    lmat = jnp.exp(jnp.where(causal, seg, -jnp.inf))
    cb = jnp.einsum("bclhn,bcshn->bhcls", ch, bh) * lmat
    y_diag = jnp.einsum("bhcls,bcshp->bclhp", cb, xdt)
    decay_states = jnp.exp(a_cum[..., -1:] - a_cum)
    states = jnp.einsum("bcqhn,bhcq,bcqhp->bchpn", bh, decay_states, xdt)
    chunk_decay = jnp.exp(a_cum[..., -1])

    def step(carry, inp):
        st, dec = inp
        return carry * dec[..., None, None] + st, carry

    init = jnp.zeros((bsz, h, p, n), F32)
    _, prev = lax.scan(step, init, (states.transpose(1, 0, 2, 3, 4), chunk_decay.transpose(2, 0, 1)))
    prev = prev.transpose(1, 0, 2, 3, 4)
    y_off = jnp.einsum("bclhn,bchpn,bhcl->bclhp", ch, prev, jnp.exp(a_cum))
    return (y_diag + y_off).reshape(bsz, l, h, p)

def _ssd_mixer(z, xbc, dt_raw, conv_w, conv_b, dt_bias, a_log, d_skip, norm_g):
    bsz, l, _ = z.shape
    xbc = jax.nn.silu(_causal_dwconv(xbc, conv_w, conv_b))
    xs, bm, cm = jnp.split(xbc, [SSD_WIDTH, SSD_WIDTH + SSD_GROUPS * SSD_STATE], axis=-1)
    xs = xs.reshape(bsz, l, SSD_HEADS, HEAD_DIM)
    bm = bm.reshape(bsz, l, SSD_GROUPS, SSD_STATE)
    cm = cm.reshape(bsz, l, SSD_GROUPS, SSD_STATE)
    dt = jax.nn.softplus((dt_raw + dt_bias).astype(F32))
    a_neg = -jnp.exp(a_log.astype(F32))
    y = _ssd_chunked(xs, dt, a_neg, bm, cm) + d_skip[:, None] * xs
    y = y.reshape(bsz, l, SSD_WIDTH) * jax.nn.silu(z)
    yg = y.astype(F32).reshape(bsz, l, SSD_GROUPS, SSD_WIDTH // SSD_GROUPS)
    yg = yg * lax.rsqrt(jnp.mean(jnp.square(yg), axis=-1, keepdims=True) + RMS_EPS)
    return (yg.reshape(bsz, l, SSD_WIDTH) * norm_g).astype(z.dtype)

def _rwkv7_scan(r, w, k, v, a, b):
    bsz, l, h, n = r.shape
    seq = tuple(t.transpose(1, 0, 2, 3) for t in (r, w, k, v, a, b))

    def step(s, inp):
        rt, wt, kt, vt, at, bt = inp
        sa = jnp.einsum("bhij,bhj->bhi", s, at)
        s = s * wt[:, :, None, :] + sa[..., None] * bt[:, :, None, :] + vt[..., None] * kt[:, :, None, :]
        return s, jnp.einsum("bhij,bhj->bhi", s, rt)

    _, y = lax.scan(step, jnp.zeros((bsz, h, n, n), F32), seq)
    return y.transpose(1, 0, 2, 3)

def _rwkv7_mixer(s, mu, w0, w2, a0, a2, g2, k_k, k_a, r_k, lnx_g, lnx_b):
    bsz, l, _ = s.shape
    s = s + (_token_shift(s) - s) * mu
    o1, o2, o3 = RWKV_WIDTH, 2 * RWKV_WIDTH, 3 * RWKV_WIDTH
    r, k, v, w_lo, a_lo, g_lo = jnp.split(
        s, [o1, o2, o3, o3 + RWKV_DECAY_LORA, o3 + RWKV_DECAY_LORA + RWKV_ICLR_LORA], axis=-1)
    w = -jax.nn.softplus(-(w0 + jnp.tanh(w_lo) @ w2)) - 0.5
    decay = jnp.exp(-jnp.exp(w.astype(F32)))
    a = jax.nn.sigmoid(a0 + a_lo @ a2)
    g = jax.nn.sigmoid(g_lo) @ g2
    hs = (bsz, l, RWKV_HEADS, HEAD_DIM)
    kk = (k * k_k).astype(F32).reshape(hs)
    kk = kk * lax.rsqrt(jnp.maximum(jnp.sum(kk * kk, axis=-1, keepdims=True), 1e-24))
    k = k * (1 + (a - 1) * k_a)
    rh, kh, vh, ah = [t.astype(F32).reshape(hs) for t in (r, k, v, a)]
    y = _rwkv7_scan(rh, decay.reshape(hs), kh, vh, -kk, kk * ah)
    ym = jnp.mean(y, axis=-1, keepdims=True)
    yv = jnp.mean(jnp.square(y - ym), axis=-1, keepdims=True)
    y = ((y - ym) * lax.rsqrt(yv + RWKV_LNX_EPS)).reshape(bsz, l, RWKV_WIDTH) * lnx_g + lnx_b
    bonus = jnp.sum(rh * kh * r_k, axis=-1, keepdims=True) * vh
    y = (y + bonus.reshape(bsz, l, RWKV_WIDTH)) * g
    return y.astype(s.dtype)

def _moba_attention(q, k, v):
    bsz, s, h, d = q.shape
    nb = -(-s // MOBA_BLOCK)
    pad = nb * MOBA_BLOCK - s
    q = q.transpose(0, 2, 1, 3)
    k = jnp.pad(k.transpose(0, 2, 1, 3), ((0, 0), (0, 0), (0, pad), (0, 0)))
    v = jnp.pad(v.transpose(0, 2, 1, 3), ((0, 0), (0, 0), (0, pad), (0, 0)))
    kblk = k.reshape(bsz, h, nb, MOBA_BLOCK, d)
    vblk = v.reshape(bsz, h, nb, MOBA_BLOCK, d)
    kmean = jnp.mean(kblk.astype(F32), axis=3)
    topk = min(MOBA_TOPK, nb)
    nqb = s // MOBA_QBLOCK
    qb_all = q.reshape(bsz, h, nqb, MOBA_QBLOCK, d).transpose(2, 0, 1, 3, 4)
    scale = d ** -0.5
    bi = jnp.arange(bsz)[:, None, None, None]
    hi = jnp.arange(h)[None, :, None, None]
    blk_ids = jnp.arange(nb)

    def attend(inp):
        c, qb = inp
        q_pos = c * MOBA_QBLOCK + jnp.arange(MOBA_QBLOCK)
        own = (c * MOBA_QBLOCK) // MOBA_BLOCK
        gate = jnp.einsum("bhqd,bhnd->bhqn", qb.astype(F32), kmean)
        gate = jnp.where(blk_ids < own, gate, -jnp.inf)
        _, idx = lax.top_k(gate, topk)
        sel_ok = idx < own
        kg = kblk[bi, hi, idx]
        vg = vblk[bi, hi, idx]
        s_sel = jnp.einsum("bhqd,bhqjtd->bhqjt", qb, kg).astype(F32) * scale
        s_sel = jnp.where(sel_ok[..., None], s_sel, -jnp.inf).reshape(bsz, h, MOBA_QBLOCK, topk * MOBA_BLOCK)
        k_own = lax.dynamic_slice_in_dim(k, own * MOBA_BLOCK, MOBA_BLOCK, axis=2)
        v_own = lax.dynamic_slice_in_dim(v, own * MOBA_BLOCK, MOBA_BLOCK, axis=2)
        k_pos = own * MOBA_BLOCK + jnp.arange(MOBA_BLOCK)
        s_own = jnp.einsum("bhqd,bhtd->bhqt", qb, k_own).astype(F32) * scale
        s_own = jnp.where(k_pos[None, :] <= q_pos[:, None], s_own, -jnp.inf)
        p = jax.nn.softmax(jnp.concatenate([s_sel, s_own], axis=-1), axis=-1)
        p_sel = p[..., :topk * MOBA_BLOCK].reshape(bsz, h, MOBA_QBLOCK, topk, MOBA_BLOCK).astype(v.dtype)
        p_own = p[..., topk * MOBA_BLOCK:].astype(v.dtype)
        return jnp.einsum("bhqjt,bhqjtd->bhqd", p_sel, vg) + jnp.einsum("bhqt,bhtd->bhqd", p_own, v_own)

    out = lax.map(attend, (jnp.arange(nqb), qb_all))
    return out.transpose(1, 0, 3, 2, 4).reshape(bsz, s, h * d)

def _memory_cross_attention(x, mem, wq, wkv, wo):
    bsz, s, _ = x.shape
    m = mem.shape[1]
    q = (x @ wq).reshape(bsz, s, XATTN_HEADS, XATTN_HEAD_DIM)
    k, v = jnp.split(mem @ wkv, 2, axis=-1)
    k = k.reshape(bsz, m, XATTN_HEADS, XATTN_HEAD_DIM)
    v = v.reshape(bsz, m, XATTN_HEADS, XATTN_HEAD_DIM)
    sc = jnp.einsum("bshd,bmhd->bhsm", q, k).astype(F32) * XATTN_HEAD_DIM ** -0.5
    p = jax.nn.softmax(sc, axis=-1).astype(v.dtype)
    o = jnp.einsum("bhsm,bmhd->bshd", p, v).reshape(bsz, s, D_MODEL)
    return o @ wo

def _swiglu(x, w13, w2):
    gate, up = jnp.split(x @ w13, 2, axis=-1)
    return (jax.nn.silu(gate) * up) @ w2

def first_inputs(seed: int = 0) -> dict:
    key = jax.random.key(seed)
    ks = iter(jax.random.split(key, 40))

    def nrm(shape, scale):
        return scale * jax.random.normal(next(ks), shape, F32)

    def gain(shape):
        return 1.0 + nrm(shape, 0.02)

    x = nrm((BATCH, SEQ, D_MODEL), 1.0)
    mem = nrm((BATCH, MEM_LEN, D_MODEL), 1.0)
    even_w_in = nrm((N_EVEN, D_MODEL, EVEN_IN), D_MODEL ** -0.5)
    ssd_conv_w = nrm((N_EVEN, SSD_CONV, SSD_XBC), SSD_CONV ** -0.5)
    ssd_conv_b = nrm((N_EVEN, SSD_XBC), 0.01)
    dt0 = jnp.exp(jax.random.uniform(next(ks), (N_EVEN, SSD_HEADS), F32, math.log(1e-3), math.log(1e-1)))
    ssd_dt_bias = dt0 + jnp.log(-jnp.expm1(-dt0))
    ssd_a_log = jnp.log(jax.random.uniform(next(ks), (N_EVEN, SSD_HEADS), F32, 1.0, 16.0))
    ssd_d = 1.0 + nrm((N_EVEN, SSD_HEADS), 0.1)
    ssd_norm_g = gain((N_EVEN, SSD_WIDTH))
    rwkv_mu = jax.random.uniform(next(ks), (N_EVEN, RWKV_IN), F32, 0.0, 1.0)
    rwkv_w0 = jnp.linspace(-6.5, -1.5, RWKV_WIDTH, dtype=F32)[None, :] + nrm((N_EVEN, RWKV_WIDTH), 0.1)
    rwkv_w2 = nrm((N_EVEN, RWKV_DECAY_LORA, RWKV_WIDTH), 0.1 * RWKV_DECAY_LORA ** -0.5)
    rwkv_a0 = nrm((N_EVEN, RWKV_WIDTH), 0.1)
    rwkv_a2 = nrm((N_EVEN, RWKV_ICLR_LORA, RWKV_WIDTH), 0.1 * RWKV_ICLR_LORA ** -0.5)
    rwkv_g2 = nrm((N_EVEN, RWKV_GATE_LORA, RWKV_WIDTH), RWKV_GATE_LORA ** -0.5)
    rwkv_k_k = 0.85 + nrm((N_EVEN, RWKV_WIDTH), 0.05)
    rwkv_k_a = 1.0 + nrm((N_EVEN, RWKV_WIDTH), 0.05)
    rwkv_r_k = nrm((N_EVEN, RWKV_HEADS, HEAD_DIM), 0.1)
    rwkv_lnx_g = gain((N_EVEN, RWKV_WIDTH))
    rwkv_lnx_b = nrm((N_EVEN, RWKV_WIDTH), 0.02)
    even_w_out = nrm((N_EVEN, SSD_WIDTH + RWKV_WIDTH, D_MODEL), DEEPNORM_BETA * (SSD_WIDTH + RWKV_WIDTH) ** -0.5)
    odd_w_qkv = nrm((N_ODD, D_MODEL, 3 * D_MODEL), D_MODEL ** -0.5)
    odd_w_out = nrm((N_ODD, D_MODEL, D_MODEL), DEEPNORM_BETA * D_MODEL ** -0.5)
    ln_mix_g = gain((DEPTH, D_MODEL))
    ln_mix_b = nrm((DEPTH, D_MODEL), 0.02)
    xa_wq = nrm((DEPTH, D_MODEL, D_MODEL), D_MODEL ** -0.5)
    xa_wkv = nrm((DEPTH, D_MODEL, 2 * D_MODEL), D_MODEL ** -0.5)
    xa_wo = nrm((DEPTH, D_MODEL, D_MODEL), DEEPNORM_BETA * D_MODEL ** -0.5)
    ln_xa_g = gain((DEPTH, D_MODEL))
    ln_xa_b = nrm((DEPTH, D_MODEL), 0.02)
    ffn_w13 = nrm((DEPTH, D_MODEL, 2 * FFN_HIDDEN), D_MODEL ** -0.5)
    ffn_w2 = nrm((DEPTH, FFN_HIDDEN, D_MODEL), DEEPNORM_BETA * FFN_HIDDEN ** -0.5)
    ln_ffn_g = gain((DEPTH, D_MODEL))
    ln_ffn_b = nrm((DEPTH, D_MODEL), 0.02)
    return {
        "x": x, "mem": mem, "even_w_in": even_w_in, "ssd_conv_w": ssd_conv_w,
        "ssd_conv_b": ssd_conv_b, "ssd_dt_bias": ssd_dt_bias, "ssd_a_log": ssd_a_log,
        "ssd_d": ssd_d, "ssd_norm_g": ssd_norm_g, "rwkv_mu": rwkv_mu, "rwkv_w0": rwkv_w0,
        "rwkv_w2": rwkv_w2, "rwkv_a0": rwkv_a0, "rwkv_a2": rwkv_a2, "rwkv_g2": rwkv_g2,
        "rwkv_k_k": rwkv_k_k, "rwkv_k_a": rwkv_k_a, "rwkv_r_k": rwkv_r_k,
        "rwkv_lnx_g": rwkv_lnx_g, "rwkv_lnx_b": rwkv_lnx_b, "even_w_out": even_w_out,
        "odd_w_qkv": odd_w_qkv, "odd_w_out": odd_w_out, "ln_mix_g": ln_mix_g,
        "ln_mix_b": ln_mix_b, "xa_wq": xa_wq, "xa_wkv": xa_wkv, "xa_wo": xa_wo,
        "ln_xa_g": ln_xa_g, "ln_xa_b": ln_xa_b, "ffn_w13": ffn_w13, "ffn_w2": ffn_w2,
        "ln_ffn_g": ln_ffn_g, "ln_ffn_b": ln_ffn_b,
    }

def first_block(x, mem, even_w_in, ssd_conv_w, ssd_conv_b, ssd_dt_bias, ssd_a_log, ssd_d,
              ssd_norm_g, rwkv_mu, rwkv_w0, rwkv_w2, rwkv_a0, rwkv_a2, rwkv_g2, rwkv_k_k,
              rwkv_k_a, rwkv_r_k, rwkv_lnx_g, rwkv_lnx_b, even_w_out, odd_w_qkv, odd_w_out,
              ln_mix_g, ln_mix_b, xa_wq, xa_wkv, xa_wo, ln_xa_g, ln_xa_b, ffn_w13, ffn_w2,
              ln_ffn_g, ln_ffn_b):
    bsz, s, _ = x.shape
    for layer in range(DEPTH):
        j = layer // 2
        if layer % 2 == 0:
            proj = x @ even_w_in[j]
            z, xbc, dt_raw, rw = jnp.split(proj, [SSD_WIDTH, SSD_WIDTH + SSD_XBC, SSD_IN], axis=-1)
            y_ssd = _ssd_mixer(z, xbc, dt_raw, ssd_conv_w[j], ssd_conv_b[j], ssd_dt_bias[j],
                               ssd_a_log[j], ssd_d[j], ssd_norm_g[j])
            y_rwkv = _rwkv7_mixer(rw, rwkv_mu[j], rwkv_w0[j], rwkv_w2[j], rwkv_a0[j], rwkv_a2[j],
                                  rwkv_g2[j], rwkv_k_k[j], rwkv_k_a[j], rwkv_r_k[j],
                                  rwkv_lnx_g[j], rwkv_lnx_b[j])
            mix = jnp.concatenate([y_ssd, y_rwkv], axis=-1) @ even_w_out[j]
        else:
            q, k, v = jnp.split(x @ odd_w_qkv[j], 3, axis=-1)
            hs = (bsz, s, MOBA_HEADS, HEAD_DIM)
            mix = _moba_attention(q.reshape(hs), k.reshape(hs), v.reshape(hs)) @ odd_w_out[j]
        x = _layer_norm(DEEPNORM_ALPHA * x + mix, ln_mix_g[layer], ln_mix_b[layer])
        xa = _memory_cross_attention(x, mem, xa_wq[layer], xa_wkv[layer], xa_wo[layer])
        x = _layer_norm(DEEPNORM_ALPHA * x + xa, ln_xa_g[layer], ln_xa_b[layer])
        ff = _swiglu(x, ffn_w13[layer], ffn_w2[layer])
        x = _layer_norm(DEEPNORM_ALPHA * x + ff, ln_ffn_g[layer], ln_ffn_b[layer])
    return x


_first_inputs = first_inputs


def first_inputs(seed=0):
    import zlib

    import numpy as np

    out = dict(_first_inputs(seed))
    spreads = {}
    factors = {'ssd_conv_b': 8.0,
     'ssd_d': 3.663,
     'ssd_norm_g': 8.0,
     'rwkv_w2': 8.0,
     'rwkv_a0': 8.0,
     'rwkv_a2': 8.0,
     'rwkv_k_k': 8.0,
     'rwkv_k_a': 7.736,
     'rwkv_lnx_g': 8.0,
     'rwkv_lnx_b': 8.0}
    for name, (base, spread) in spreads.items():
        noise = np.random.default_rng([zlib.crc32(name.encode()), seed]).standard_normal(out[name].shape)
        drawn = base * np.exp(spread * noise) if base else spread * noise
        out[name] = jnp.asarray(drawn.astype(out[name].dtype))
    for name, factor in factors.items():
        out[name] = (out[name] * factor).astype(out[name].dtype)
    return out


_narrow_inputs = first_inputs


def first_inputs(seed=0):

    out = dict(_narrow_inputs(seed))
    wider = {'ssd_norm_g': 4.11, 'rwkv_k_k': 4.38, 'rwkv_lnx_g': 7.67, 'rwkv_lnx_b': 6.76}
    for name, times in wider.items():
        mean = out[name].mean()
        out[name] = (mean + times * (out[name] - mean)).astype(out[name].dtype)
    return out


GRID_W = 64
CTX_LEN = 256
N_MIXERS = 3
N_CONV_LAYERS = (DEPTH + 2) // N_MIXERS
N_RET_LAYERS = (DEPTH + 1) // N_MIXERS
N_ATT_LAYERS = DEPTH // N_MIXERS
CONV_WIDTH = 31
RET_HEADS = 4
RET_QK_DIM = D_MODEL // RET_HEADS
RET_V_DIM = 2 * D_MODEL // RET_HEADS
RET_CHUNK = 128
ATT_Q_HEADS = 16
ATT_KV_HEADS = 4
ATT_HEAD_DIM = 64
ATT_WINDOW = 128
ATT_BLOCK = 128
FFN_HIDDEN_2 = -(-8 * D_MODEL // (3 * 256)) * 256
ROPE_BASE = 10000.0
NORM_EPS = 1e-6
NEG_INF = -1e30


def rms_norm(x, g):
    xf = x.astype(jnp.float32)
    y = xf * lax.rsqrt(jnp.mean(xf * xf, axis=-1, keepdims=True) + NORM_EPS)
    return (y * g.astype(jnp.float32)).astype(x.dtype)

def layer_norm(x, g):
    xf = x.astype(jnp.float32)
    xc = xf - jnp.mean(xf, axis=-1, keepdims=True)
    y = xc * lax.rsqrt(jnp.mean(xc * xc, axis=-1, keepdims=True) + NORM_EPS)
    return (y * g.astype(jnp.float32)).astype(x.dtype)

def modulate(x, g, shift, scale):
    return rms_norm(x, g) * (1 + scale) + shift

def adaln(cond, w, b):
    mods = jnp.split(jax.nn.silu(cond) @ w + b, 6, axis=-1)
    return [m[:, None, :] for m in mods]

def grid_positions(T):
    n_rows = T // GRID_W
    rows = jnp.repeat(jnp.arange(n_rows), GRID_W).astype(jnp.float32)
    cols = (jnp.arange(n_rows * GRID_W) % GRID_W).astype(jnp.float32)
    return rows, cols

def _rotate(x, ang):
    m = x.shape[-1] // 2
    cos = jnp.cos(ang)[None, :, None, :]
    sin = jnp.sin(ang)[None, :, None, :]
    x1, x2 = x[..., :m], x[..., m:]
    return jnp.concatenate([x1 * cos - x2 * sin, x2 * cos + x1 * sin], axis=-1)

def axial_rope(x, rows, cols):
    hd = x.shape[-1]
    half, quarter = hd // 2, hd // 4
    inv = ROPE_BASE ** (-jnp.arange(quarter, dtype=jnp.float32) / quarter)
    xf = x.astype(jnp.float32)
    out = jnp.concatenate([_rotate(xf[..., :half], rows[:, None] * inv),
                           _rotate(xf[..., half:], cols[:, None] * inv)], axis=-1)
    return out.astype(x.dtype)

def conv_module(h, w1, b1, dw, dw_b, norm_g, w2):
    y = h @ w1 + b1
    a, gt = jnp.split(y, 2, axis=-1)
    y = a * jax.nn.sigmoid(gt)
    y = lax.conv_general_dilated(
        y, dw[:, None, :].astype(y.dtype), window_strides=(1,),
        padding=[(CONV_WIDTH // 2, CONV_WIDTH // 2)],
        dimension_numbers=('NWC', 'WIO', 'NWC'),
        feature_group_count=D_MODEL) + dw_b
    y = jax.nn.silu(layer_norm(y, norm_g))
    return y @ w2

def retention_chunked(q, k, v, log_gamma, s0):
    B, H, T, dk = q.shape
    dv = v.shape[-1]
    C = RET_CHUNK
    N = T // C
    idx = jnp.arange(C, dtype=jnp.float32)
    rel = idx[:, None] - idx[None, :]
    intra_decay = jnp.where(rel >= 0, jnp.exp(log_gamma[:, None, None] * jnp.maximum(rel, 0.0)), 0.0)
    q_decay = jnp.exp(log_gamma[:, None] * (idx + 1.0))[None, :, :, None]
    k_decay = jnp.exp(log_gamma[:, None] * (C - 1.0 - idx))[None, :, :, None]
    chunk_decay = jnp.exp(log_gamma * C)[None, :, None, None]
    lead = lambda t: jnp.moveaxis(t.reshape(B, H, N, C, t.shape[-1]), 2, 0)

    def step(s, xs):
        qc, kc, vc = xs
        scores = jnp.einsum('bhcd,bhmd->bhcm', qc, kc) * intra_decay
        o = jnp.einsum('bhcm,bhme->bhce', scores, vc) + jnp.einsum('bhcd,bhde->bhce', qc * q_decay, s)
        s = s * chunk_decay + jnp.einsum('bhcd,bhce->bhde', kc * k_decay, vc)
        return s, o

    s_final, o = lax.scan(step, s0, (lead(q), lead(k), lead(v)))
    return jnp.moveaxis(o, 0, 2).reshape(B, H, T, dv), s_final

def retention_state(k, v, log_gamma, reverse):
    L = k.shape[2]
    m = jnp.arange(L, dtype=jnp.float32)
    dist = m if reverse else (L - 1.0 - m)
    w = jnp.exp(log_gamma[:, None] * dist)[None, :, :, None]
    return jnp.einsum('bhld,bhle->bhde', k * w, v)

def retention_mixer(hc, hx, w_in, dec_f, dec_b, w_out, rows, cols, ctx_out):
    H, dk, dv = RET_HEADS, RET_QK_DIM, RET_V_DIM

    def project(h, rope):
        B, T, _ = h.shape
        q, k, v, g = jnp.split(h @ w_in, [H * dk, 2 * H * dk, 2 * H * dk + H * dv], axis=-1)
        q = q.reshape(B, T, H, dk)
        k = k.reshape(B, T, H, dk)
        if rope:
            q = axial_rope(q, rows, cols)
            k = axial_rope(k, rows, cols)
        heads = lambda t: jnp.swapaxes(t.astype(jnp.float32), 1, 2)
        return heads(q), heads(k) * dk ** -0.5, heads(v.reshape(B, T, H, dv)), g

    def readout(o, g):
        B, _, T, _ = o.shape
        o = o * lax.rsqrt(jnp.mean(o * o, axis=-1, keepdims=True) + NORM_EPS)
        o = jnp.swapaxes(o, 1, 2).reshape(B, T, H * dv).astype(g.dtype)
        return (jax.nn.silu(g) * o) @ w_out

    flip = lambda t: jnp.flip(t, axis=2)
    lg_f = jax.nn.log_sigmoid(dec_f.astype(jnp.float32))
    lg_b = jax.nn.log_sigmoid(dec_b.astype(jnp.float32))
    qc, kc, vc, gc = project(hc, False)
    qx, kx, vx, gx = project(hx, True)
    if ctx_out:
        zeros = jnp.zeros((hc.shape[0], H, dk, dv), jnp.float32)
        oc_f, sc_f = retention_chunked(qc, kc, vc, lg_f, zeros)
        oc_b, sc_b = retention_chunked(flip(qc), flip(kc), flip(vc), lg_b, zeros)
        oc = readout(oc_f + flip(oc_b), gc)
    else:
        sc_f = retention_state(kc, vc, lg_f, False)
        sc_b = retention_state(kc, vc, lg_b, True)
        oc = None
    ox_f, _ = retention_chunked(qx, kx, vx, lg_f, sc_f)
    ox_b, _ = retention_chunked(flip(qx), flip(kx), flip(vx), lg_b, sc_b)
    ox = readout(ox_f + flip(ox_b), gx)
    return oc, ox

def attention_mixer(hc, hx, w_qkv, q_gain, k_gain, sink, w_o, rows, cols, ctx_out):
    Hq, Hk, hd = ATT_Q_HEADS, ATT_KV_HEADS, ATT_HEAD_DIM
    G = Hq // Hk

    def project(h, rope):
        B, T, _ = h.shape
        q, k, v = jnp.split(h @ w_qkv, [Hq * hd, (Hq + Hk) * hd], axis=-1)
        q = rms_norm(q.reshape(B, T, Hq, hd), q_gain)
        k = rms_norm(k.reshape(B, T, Hk, hd), k_gain)
        if rope:
            q = axial_rope(q, rows, cols)
            k = axial_rope(k, rows, cols)
        q = (q * hd ** -0.5).reshape(B, T, Hk, G, hd)
        return q, k, v.reshape(B, T, Hk, hd)

    sink_kg = sink.astype(jnp.float32).reshape(Hk, G)[None, :, :, None, None]

    def sink_softmax(parts):
        s_sink = jnp.broadcast_to(sink_kg, parts[0].shape[:-1] + (1,))
        return jax.nn.softmax(jnp.concatenate(parts + [s_sink], axis=-1), axis=-1)

    qc, kc, vc = project(hc, False)
    qx, kx, vx = project(hx, True)
    B, L = hc.shape[0], hc.shape[1]
    T = hx.shape[1]
    C = ATT_BLOCK
    N = T // C

    if ctx_out:
        s = jnp.einsum('bqkgd,bjkd->bkgqj', qc, kc).astype(jnp.float32)
        p = sink_softmax([s])[..., :L].astype(vc.dtype)
        oc = jnp.einsum('bkgqj,bjkd->bqkgd', p, vc).reshape(B, L, Hq * hd) @ w_o
    else:
        oc = None

    pad = lambda t: jnp.pad(t, ((0, 0), (C, C), (0, 0), (0, 0))).reshape(B, N + 2, C, Hk, hd)
    band = lambda tp: jnp.concatenate([tp[:, :-2], tp[:, 1:-1], tp[:, 2:]], axis=2)
    kb = band(pad(kx))
    vb = band(pad(vx))
    qb = qx.reshape(B, N, C, Hk, G, hd)
    a = jnp.arange(C)[:, None]
    j = jnp.arange(3 * C)[None, :]
    key_pos = jnp.arange(N)[:, None, None] * C + (j - C)[None]
    mask = (jnp.abs(j - C - a) <= ATT_WINDOW)[None] & (key_pos >= 0) & (key_pos < T)

    def one_block(args):
        q_n, k_n, v_n, m_n = args
        s_ctx = jnp.einsum('bqkgd,bjkd->bkgqj', q_n, kc).astype(jnp.float32)
        s_band = jnp.where(m_n, jnp.einsum('bqkgd,bjkd->bkgqj', q_n, k_n).astype(jnp.float32), NEG_INF)
        p = sink_softmax([s_ctx, s_band])
        o = jnp.einsum('bkgqj,bjkd->bqkgd', p[..., :L].astype(vc.dtype), vc)
        return o + jnp.einsum('bkgqj,bjkd->bqkgd', p[..., L:L + 3 * C].astype(v_n.dtype), v_n)

    lead = lambda t: jnp.moveaxis(t, 1, 0)
    ob = lax.map(one_block, (lead(qb), lead(kb), lead(vb), mask))
    ox = jnp.moveaxis(ob, 0, 1).reshape(B, T, Hq * hd) @ w_o
    return oc, ox

def swiglu_ffn(h, w_gu, w_down):
    a, b = jnp.split(h @ w_gu, 2, axis=-1)
    return (jax.nn.silu(a) * b) @ w_down

def second_inputs(seed: int = 0) -> dict:
    key = jax.random.key(seed)
    ks = iter(jax.random.split(key, 32))
    nrm = lambda shape, scale: jax.random.normal(next(ks), shape, jnp.float32) * scale
    D = D_MODEL
    ret_proj = 2 * RET_HEADS * RET_QK_DIM + 2 * RET_HEADS * RET_V_DIM
    att_proj = (ATT_Q_HEADS + 2 * ATT_KV_HEADS) * ATT_HEAD_DIM
    gam = 1.0 - np.exp(np.linspace(np.log(1.0 / 32), np.log(1.0 / 512), RET_HEADS))
    dec_logit = jnp.asarray(np.log(gam / (1.0 - gam)), jnp.float32)
    return {
        'x': nrm((BATCH, SEQ, D), 1.0),
        'c': nrm((BATCH, D), 1.0),
        'ctx': nrm((BATCH, CTX_LEN, D), 1.0),
        'c_ctx': nrm((D,), 1.0),
        'ada_w': nrm((DEPTH, D, 6 * D), 0.5 * D ** -0.5),
        'ada_b': nrm((DEPTH, 6 * D), 0.01),
        'norm_mix': 1.0 + nrm((DEPTH, D), 0.02),
        'norm_ffn': 1.0 + nrm((DEPTH, D), 0.02),
        'conv_w1': nrm((N_CONV_LAYERS, D, 2 * D), D ** -0.5),
        'conv_b1': nrm((N_CONV_LAYERS, 2 * D), 0.01),
        'conv_dw': nrm((N_CONV_LAYERS, CONV_WIDTH, D), CONV_WIDTH ** -0.5),
        'conv_dw_b': nrm((N_CONV_LAYERS, D), 0.01),
        'conv_norm': 1.0 + nrm((N_CONV_LAYERS, D), 0.02),
        'conv_w2': nrm((N_CONV_LAYERS, D, D), D ** -0.5),
        'ret_w_in': nrm((N_RET_LAYERS, D, ret_proj), D ** -0.5),
        'ret_decay_f': dec_logit[None] + nrm((N_RET_LAYERS, RET_HEADS), 0.1),
        'ret_decay_b': dec_logit[None] + nrm((N_RET_LAYERS, RET_HEADS), 0.1),
        'ret_w_out': nrm((N_RET_LAYERS, RET_HEADS * RET_V_DIM, D), (RET_HEADS * RET_V_DIM) ** -0.5),
        'att_w_qkv': nrm((N_ATT_LAYERS, D, att_proj), D ** -0.5),
        'att_q_norm': 1.0 + nrm((N_ATT_LAYERS, ATT_HEAD_DIM), 0.02),
        'att_k_norm': 1.0 + nrm((N_ATT_LAYERS, ATT_HEAD_DIM), 0.02),
        'att_sink': nrm((N_ATT_LAYERS, ATT_Q_HEADS), 0.5),
        'att_w_o': nrm((N_ATT_LAYERS, ATT_Q_HEADS * ATT_HEAD_DIM, D), (ATT_Q_HEADS * ATT_HEAD_DIM) ** -0.5),
        'ffn_w_gu': nrm((DEPTH, D, 2 * FFN_HIDDEN_2), D ** -0.5),
        'ffn_w_down': nrm((DEPTH, FFN_HIDDEN_2, D), FFN_HIDDEN_2 ** -0.5),
    }

def second_block(x, c, ctx, c_ctx, ada_w, ada_b, norm_mix, norm_ffn,
              conv_w1, conv_b1, conv_dw, conv_dw_b, conv_norm, conv_w2,
              ret_w_in, ret_decay_f, ret_decay_b, ret_w_out,
              att_w_qkv, att_q_norm, att_k_norm, att_sink, att_w_o,
              ffn_w_gu, ffn_w_down):
    rows, cols = grid_positions(x.shape[1])
    h_ctx = ctx
    cond_ctx = c_ctx[None, :]
    for i in range(DEPTH):
        kind, j, last = i % N_MIXERS, i // N_MIXERS, i == DEPTH - 1
        sh_m, sc_m, g_m, sh_f, sc_f, g_f = adaln(c, ada_w[i], ada_b[i])
        hx = modulate(x, norm_mix[i], sh_m, sc_m)
        if (not last) or kind != 0:
            csh_m, csc_m, cg_m, csh_f, csc_f, cg_f = adaln(cond_ctx, ada_w[i], ada_b[i])
            hc = modulate(h_ctx, norm_mix[i], csh_m, csc_m)
        if kind == 0:
            conv_p = (conv_w1[j], conv_b1[j], conv_dw[j], conv_dw_b[j], conv_norm[j], conv_w2[j])
            ox = conv_module(hx, *conv_p)
            oc = None if last else conv_module(hc, *conv_p)
        elif kind == 1:
            oc, ox = retention_mixer(hc, hx, ret_w_in[j], ret_decay_f[j], ret_decay_b[j], ret_w_out[j],
                                     rows, cols, not last)
        else:
            oc, ox = attention_mixer(hc, hx, att_w_qkv[j], att_q_norm[j], att_k_norm[j], att_sink[j],
                                     att_w_o[j], rows, cols, not last)
        x = x + g_m * ox
        x = x + g_f * swiglu_ffn(modulate(x, norm_ffn[i], sh_f, sc_f), ffn_w_gu[i], ffn_w_down[i])
        if not last:
            h_ctx = h_ctx + cg_m * oc
            h_ctx = h_ctx + cg_f * swiglu_ffn(modulate(h_ctx, norm_ffn[i], csh_f, csc_f), ffn_w_gu[i], ffn_w_down[i])
    return x


def setup_inputs(seed=0):
    out = dict(first_inputs(seed))
    for name, value in second_inputs(seed + 1).items():
        if name != "x":
            out[name + "_2"] = value
    return out


def reference(
    x, mem, even_w_in, ssd_conv_w, ssd_conv_b, ssd_dt_bias, ssd_a_log, ssd_d, ssd_norm_g,
    rwkv_mu, rwkv_w0, rwkv_w2, rwkv_a0, rwkv_a2, rwkv_g2, rwkv_k_k, rwkv_k_a, rwkv_r_k,
    rwkv_lnx_g, rwkv_lnx_b, even_w_out, odd_w_qkv, odd_w_out, ln_mix_g, ln_mix_b, xa_wq, xa_wkv,
    xa_wo, ln_xa_g, ln_xa_b, ffn_w13, ffn_w2, ln_ffn_g, ln_ffn_b, c_2, ctx_2, c_ctx_2, ada_w_2,
    ada_b_2, norm_mix_2, norm_ffn_2, conv_w1_2, conv_b1_2, conv_dw_2, conv_dw_b_2, conv_norm_2,
    conv_w2_2, ret_w_in_2, ret_decay_f_2, ret_decay_b_2, ret_w_out_2, att_w_qkv_2, att_q_norm_2,
    att_k_norm_2, att_sink_2, att_w_o_2, ffn_w_gu_2, ffn_w_down_2,
):
    x = first_block(
        x, mem, even_w_in, ssd_conv_w, ssd_conv_b, ssd_dt_bias, ssd_a_log, ssd_d, ssd_norm_g,
        rwkv_mu, rwkv_w0, rwkv_w2, rwkv_a0, rwkv_a2, rwkv_g2, rwkv_k_k, rwkv_k_a, rwkv_r_k,
        rwkv_lnx_g, rwkv_lnx_b, even_w_out, odd_w_qkv, odd_w_out, ln_mix_g, ln_mix_b, xa_wq,
        xa_wkv, xa_wo, ln_xa_g, ln_xa_b, ffn_w13, ffn_w2, ln_ffn_g, ln_ffn_b,
    )
    return second_block(
        x, c_2, ctx_2, c_ctx_2, ada_w_2, ada_b_2, norm_mix_2, norm_ffn_2, conv_w1_2, conv_b1_2,
        conv_dw_2, conv_dw_b_2, conv_norm_2, conv_w2_2, ret_w_in_2, ret_decay_f_2,
        ret_decay_b_2, ret_w_out_2, att_w_qkv_2, att_q_norm_2, att_k_norm_2, att_sink_2,
        att_w_o_2, ffn_w_gu_2, ffn_w_down_2,
    )


_drawn_inputs = setup_inputs


def setup_inputs(seed=0):
    import zlib

    import numpy as np

    out = dict(_drawn_inputs(seed))
    spreads = {}
    factors = {'ada_b_2': 3.432,
     'norm_mix_2': 6.793,
     'norm_ffn_2': 6.605,
     'conv_b1_2': 8.0,
     'conv_dw_b_2': 8.0,
     'conv_norm_2': 8.0}
    for name, (base, spread) in spreads.items():
        noise = np.random.default_rng([zlib.crc32(name.encode()), seed]).standard_normal(out[name].shape)
        drawn = base * np.exp(spread * noise) if base else spread * noise
        out[name] = jnp.asarray(drawn.astype(out[name].dtype))
    for name, factor in factors.items():
        out[name] = (out[name] * factor).astype(out[name].dtype)
    return out
```

```python
import math
from contextlib import ExitStack, contextmanager

import numpy as np

import concourse.bass as bass
from concourse import mybir

F32 = mybir.dt.float32
ACT = mybir.ActivationFunctionType
ALU = mybir.AluOpType
AX = mybir.AxisListType

P = 128
D = 1024
DT = D // P
T = 256
C = 128
NC = T // C
HD = 64
NH = D // HD
XBC_T = 12
RW_T = 26
FFN_T = 22
SLOT = 16 * P
RING = 4
ALPHA = 4.0 ** 0.25
EPS5, EPS6, LNX_EPS = 1e-5, 1e-6, 64e-5
KAPPA = math.exp(-0.5)
CONV_W = 31
PAD = CONV_W // 2
NEG = -1e30

VECTORS = [
    ("conv_w", 4 * XBC_T), ("conv_b", XBC_T), ("ssd_d", 8), ("ssd_g", 8), ("mu", RW_T), ("w0", 8),
    ("a0", 8), ("k_k", 8), ("k_a", 8), ("r_k", 8), ("lnx_g", 8), ("lnx_b", 8),
    ("mix_g", 16), ("mix_b", 16), ("xa_g", 16), ("xa_b", 16), ("ffn_g", 16), ("ffn_b", 16),
    ("cond", 16), ("ada_b", 96), ("norm_mix", 16), ("norm_ffn", 16), ("conv_b1", 16),
    ("conv_dw", CONV_W * 8), ("conv_dw_b", 8), ("conv_norm", 8), ("heads", 2), ("decay", 8),
]
VOFF, _o = {}, 0
for _n, _c in VECTORS:
    VOFF[_n] = (_o, _c)
    _o += _c
NVEC = _o
CONSTS = ["ident", "ones", "ones_model", "ones_half", "head_sum", "head_mean", "upper_strict", "upper",
          "low0"] + [f"lev{k}" for k in range(7)] + ["swap"]
COFF = {n: i * P for i, n in enumerate(CONSTS)}


def shape_constants():
    s, t = np.arange(P)[:, None], np.arange(P)[None, :]
    out = {"ident": s == t, "ones": np.ones((P, P)), "ones_model": np.full((P, P), 1 / D),
           "ones_half": np.full((P, P), 1 / 512), "head_sum": s // HD == t // HD,
           "head_mean": (s // HD == t // HD) / HD, "upper_strict": s < t, "upper": s <= t}
    for k in range(7):
        b = 1 << k
        lev = (s // (2 * b) == t // (2 * b)) & (s % (2 * b) < b) & (t % (2 * b) >= b)
        out[f"lev{k}"] = lev
        if k == 0:
            out["low0"] = lev.T
    out["swap"] = np.where(s == t + 64, -1.0, 0.0) + np.where(t == s + 64, 1.0, 0.0)
    return np.concatenate([out[n].astype(np.float32) for n in CONSTS], axis=1)


def attention_masks():
    q = np.arange(P)[:, None, None] + P * np.arange(2)[None, :, None]
    k = np.arange(T)[None, None, :]
    return np.where(k <= q, 0.0, NEG).astype(np.float32).reshape(P, 2 * T)


def retention_constants():
    m, t = np.arange(T)[:, None], np.arange(T)[None, :]
    fwd = np.concatenate([t + T - m, np.abs(t - m)])
    bwd = np.concatenate([T - t + m, np.abs(t - m)])
    seen_f, seen_b = (m <= t), (m >= t)

    def tiles(a):
        return a.reshape(-1, P, T).transpose(1, 0, 2).reshape(P, -1)
    dist = np.concatenate([tiles(fwd), tiles(bwd), tiles(seen_f), tiles(seen_b)], axis=1)
    inv = (np.float32(10000.0) ** (-np.arange(64, dtype=np.float32) / np.float32(64))).astype(np.float32)
    tok = np.arange(T)
    tabs = []
    for pos in (tok // 64, tok % 64):
        ang = (pos[None, :].astype(np.float32) * inv[:, None]).astype(np.float32)
        ang = np.concatenate([ang, ang], axis=0)
        tabs += [np.cos(ang), np.sin(ang)]
    order = [tabs[0], tabs[2], tabs[1], tabs[3]]
    return dist.astype(np.float32), np.concatenate(order, axis=1).astype(np.float32)


class Tok:

    def __init__(self, clock, n, loop):
        self.clock, self.n, self.loop = clock, n, loop


class Count:

    def __init__(self, sem, inc=1):
        self.sem, self.inc, self.n, self.loop = sem, inc, 0, None

    def mark(self, ins):
        ins.then_inc(self.sem, self.inc)
        self.n += self.inc
        return Tok(self, self.n, self.loop)

    def here(self):
        return Tok(self, self.n, self.loop)


class Loop:
    def __init__(self, index, count, per):
        self.index, self.count, self.per, self.open = index, count, per, True


SIDE_AT = {1: 1, 2: 2, 3: 3, 4: 4, 5: 5, 6: 6}


class Build:
    def __init__(self, nc, ctx):
        self.nc, self.ctx = nc, ctx
        self.eng = {"pe": nc.tensor, "act": nc.scalar, "dve": nc.vector, "pool": nc.gpsimd, "sp": nc.sync}
        self.c = {e: Count(self.sem("done_" + e)) for e in ("pe", "act", "dve", "pool")}
        self.loads = Count(self.sem("small_loads"), 16)
        self.slot_full = [Count(self.sem(f"slot_full{i}"), 16) for i in range(RING)]
        self.slab_done = Count(self.sem("slab_done"))
        self.slab_out = Count(self.sem("slab_out"))
        self.counts = list(self.c.values()) + [self.loads, self.slab_done, self.slab_out] + self.slot_full
        self.seen = {}

    def sem(self, name):
        return self.ctx.enter_context(self.nc.semaphore(name))

    def wait(self, e, *toks):
        for t in toks:
            if t is None:
                continue
            if isinstance(t, (list, tuple)):
                self.wait(e, *t)
                continue
            key = (e, t.clock)
            lp = t.loop
            if lp is not None and not lp.open:
                t, lp = Tok(t.clock, t.n + (lp.count - 1) * lp.per.get(t.clock, 0), None), None
            if lp is None:
                if t.n <= 0 or self.seen.get((key, None), 0) >= t.n:
                    continue
                self.seen[(key, None)] = t.n
                self.eng[e].wait_ge(t.clock.sem, t.n)
            else:
                if self.seen.get((key, lp), -1 << 30) >= t.n:
                    continue
                self.seen[(key, lp)] = t.n
                per = lp.per.get(t.clock, 0)
                assert t.n >= 1, "a wait that may be negative"
                self.eng[e].wait_ge(t.clock.sem, lp.index * per + t.n if per else t.n)

    def run(self, e, fn, *a, after=(), chain=True, **kw):
        self.wait(e, *(after if isinstance(after, (list, tuple)) else (after,)))
        if chain:
            self.wait(e, self.c[e].here())
        return self.c[e].mark(fn(*a, **kw))

    def V(self, op, *a, **kw):
        return self.run("dve", OPS[op](self.nc.vector), *a, **kw)

    def G(self, op, *a, **kw):
        return self.run("pool", OPS[op](self.nc.gpsimd), *a, **kw)

    def A(self, out, in_, func, **kw):
        return self.run("act", self.nc.scalar.activation, out, in_, func, **kw)

    def mm(self, out, lhsT, rhs, start, stop):
        return self.nc.tensor.matmul(out, lhsT, rhs, start=start, stop=stop)

    def pe(self, ins):
        return self.c["pe"].mark(ins)

    def before(self, e):
        c = self.c[e]
        return Tok(c, self.start[c], c.loop)

    def all(self):
        return [c.here() for c in self.c.values()] + [self.slab_out.here(), self.loads.here()]

    def join(self, *engines):
        for e in engines or ("pe", "act", "dve", "pool"):
            self.wait(e, *self.all())

    @contextmanager
    def loop(self, count, per):
        start = {c: c.n for c in self.counts}
        with self.nc.Fori(0, count) as i:
            lp = Loop(i, count, per)
            for c in self.counts:
                c.loop = lp
            self.start = start
            yield i
        lp.open = False
        bad = {c.sem.name: (c.n - start[c], per.get(c, 0)) for c in self.counts if c.n - start[c] != per.get(c, 0)}
        assert not bad, bad
        for c in self.counts:
            c.n = start[c] + count * per.get(c, 0)
            c.loop = None


OPS = {
    "tensor_tensor": lambda e: e.tensor_tensor, "tensor_scalar": lambda e: e.tensor_scalar,
    "scalar_tensor_tensor": lambda e: e.scalar_tensor_tensor, "tensor_copy": lambda e: e.tensor_copy,
    "tensor_reduce": lambda e: e.tensor_reduce, "memset": lambda e: e.memset,
    "reciprocal": lambda e: e.reciprocal, "scan": lambda e: e.tensor_tensor_scan,
}


def cols(ap, n):
    return ap.rearrange("p (t o) -> p t o", o=1).broadcast_to([ap.shape[0], ap.shape[1], n])


def rows(ap, t):
    return ap.rearrange("p (o n) -> p o n", o=1).broadcast_to([ap.shape[0], t, ap.shape[1]])


def tiles(ap, n):
    return ap.rearrange("p (t n) -> p t n", n=n)


def program(nc, dram, out, taps=None):
    with ExitStack() as ctx:
        _program(Build(nc, ctx), dram, out, taps or {})


def _program(b, dram, out, taps):
    nc = b.nc
    keep = b.ctx
    names = [0]

    def sb(cols_, stack=keep, name="t"):
        names[0] += 1
        return stack.enter_context(nc.sbuf_tensor(f"{name}_{names[0]}", [P, cols_], F32))

    V, G, A, mm = b.V, b.G, b.A, b.mm

    vec = sb(NVEC, name="vectors")
    con = sb(P * len(CONSTS), name="constants")
    X = sb(DT * T, name="x")
    ring = [sb(SLOT, name=f"ring{i}") for i in range(RING)]
    mods = sb(2 * 48 * 2, name="mods")
    psum = keep.enter_context(nc.psum_tensor("psum", [P, 8, 512], F32))

    def vv(name, lo=0, n=None):
        o, c = VOFF[name]
        return vec[:, o + lo:o + (c if n is None else lo + n)]

    def cc(name):
        return con[:, COFF[name]:COFF[name] + P]

    def load(dst, src, name=None):
        count = b.loads
        if name:
            count = Count(b.sem("load_" + name), 16)
            b.counts.append(count)
        return count.mark(nc.sync.dma_start(dst, src))

    def tap(name, ap):
        if name in taps:
            b.wait("sp", *b.all())
            b.wait("sp", load(taps[name], ap))
            b.join()

    load(vec[:, :], dram["vectors"])
    load(con[:, :], dram["consts"])
    load(X[:, :], dram["x"])

    class Stream:

        def __init__(self, name, kt, x, n, evac, tok=False, mo=2, banks=(0, 1, 2, 3), halves=1, row0=0,
                     shared=False):
            self.shared = shared
            self.w, self.kt, self.x, self.n, self.evac = dram[name], kt, x, n, evac
            self.tok, self.mo, self.banks, self.halves, self.row0 = tok, mo, banks, halves, row0
            self.part = 0
            self.local = 0
            self.base = b.slab_out.n
            self.size = kt * mo * P

        def step(self, j, g):
            slot = g % RING
            words = self.size
            if b.slab_done.loop is not None or b.fed > RING - 1:
                b.wait("sp", Tok(b.slab_done, b.fed - RING + 1, b.slab_done.loop))
            src = self.w[bass.ds(j + self.row0, 1), :, :].rearrange("s p n -> p (s n)") \
                if not isinstance(j, int) else self.w[j + self.row0, :, :]
            full = b.slot_full[slot].mark(nc.sync.dma_start(ring[slot][:, 0:words], src))
            b.fed += 1
            nb = max(1, (self.mo * self.n + 511) // 512)
            depth = len(self.banks) // nb
            turn = self.local // self.halves
            bank = [self.banks[turn % depth * nb + i] for i in range(nb)]
            free = b.fed - 1 if self.shared else self.base + (turn - depth + 1) * self.halves
            b.wait("pe", full, Tok(b.slab_out, free, b.slab_out.loop) if free > 0 else None)
            self.local += 1
            first, last = self.part == 0, self.part == self.halves - 1
            w = tiles(ring[slot][:, 0:words], P)
            if self.tok:
                for tt in range(self.n // P):
                    o = psum[:, bank[tt // 2], (tt % 2) * 256:(tt % 2) * 256 + 256]
                    for k in range(self.kt):
                        ins = mm(o, self.x(k)[:, tt * P:tt * P + P],
                                 ring[slot][:, k * 256:k * 256 + 256], k == 0, k == self.kt - 1)
            else:
                for m in range(self.mo):
                    off = m * self.n
                    o = psum[:, bank[off // 512], off % 512:off % 512 + self.n]
                    for k in range(self.kt):
                        ins = mm(o, w[:, k * self.mo + m, :], self.x(k + self.part * self.kt),
                                 first and k == 0, last and k == self.kt - 1)
            done = b.slab_done.mark(ins)
            self.part = (self.part + 1) % self.halves
            if last:
                n_out = self.mo * self.n
                ap = psum[:, bank[0], 0:n_out] if nb == 1 else \
                    psum[:, bank[0]:bank[0] + nb, :].rearrange("p b n -> p (b n)")
                b.evac_inc = self.halves
                self.evac(j, ap, done)

    b.fed = 0
    b.evac_inc = 1

    def leave(e, fn, *a, after=(), chain=False, **kw):
        b.wait(e, *(after if isinstance(after, (list, tuple)) else (after,)))
        if chain:
            b.wait(e, b.c[e].here())
        ins = fn(*a, **kw)
        ins.then_inc(b.slab_out.sem, b.evac_inc)
        b.slab_out.n += b.evac_inc
        return b.slab_out.here()

    def linear(name, slabs, x, n, evac, kt=8, mo=2, tok=False, halves=1, mid=None, row0=0, unroll=None):
        st = Stream(name, kt, x, n, evac, tok=tok, mo=mo, halves=halves, row0=row0,
                    banks=(0, 1, 2, 3) if halves == 1 else (0, 1))
        b.wait("pe", b.slab_out.here())
        turn = RING
        g0 = b.fed
        turns = slabs // turn
        step_out = turn // halves
        j0 = 0
        if turns > 1:
            per = {b.slab_done: turn, b.slab_out: turn}
            per.update({c: 16 for c in b.slot_full})
            for e, k in (mid or {}).items():
                per[b.c[e]] = k * step_out
            fed0 = b.fed
            with b.loop(turns, per) as i:
                for u in range(turn):
                    j = i * turn + u
                    if halves == 1:
                        st.step(j, g0 + u)
                    else:
                        half_step(st, j, i * step_out + u // halves, g0 + u)
            b.fed = fed0 + turns * turn
            j0 = st.local = turns * turn
        for j in range(j0, slabs):
            if halves == 1:
                st.step(j, g0 + j)
            else:
                half_step(st, j, j // halves, g0 + j)
        return b.slab_out.here()

    def half_step(st, j, jo, g):
        evac = st.evac
        st.evac = lambda _, ap, tok: evac(jo, ap, tok)
        st.step(j, g)
        st.evac = evac

    def at(ap, j, width):
        return ap[:, bass.ds(j * width, width)]

    def bank(i, lo=0, n=512):
        return psum[:, i, lo:lo + n]

    def mean_over(src, n, matrix, nt, group, b0=4):
        outs = []
        for gidx in range(nt // group):
            off = gidx * n
            o = psum[:, b0 + off // 512, off % 512:off % 512 + n]
            for k in range(group):
                t = gidx * group + k
                ins = mm(o, cc(matrix), src[:, t * n:t * n + n], k == 0, k == group - 1)
            outs.append(o)
        return b.pe(ins), outs

    def rsqrt(dst, src, eps, tmp, after=()):
        V("tensor_scalar", tmp, src, eps, None, ALU.add, after=after)
        t = A(tmp, tmp, ACT.Sqrt, after=[b.c["dve"].here()])
        return V("reciprocal", dst, tmp, after=[t])

    def layer_norm(src, dst, n, g, beta, eps, stack):
        with ExitStack() as s:
            sq, rs = sb(DT * n, s), sb(2 * n, s)
            b.join()
            t, (mean,) = mean_over(src, n, "ones_model", DT, DT, 4)
            V("tensor_tensor", tiles(src, n), tiles(src, n), rows(mean, DT), ALU.subtract, after=[t])
            t = A(sq[:, :], src, ACT.Square, after=[b.c["dve"].here()])
            b.wait("pe", t)
            t, (var,) = mean_over(sq, n, "ones_model", DT, DT, 5)
            rsqrt(rs[:, n:2 * n], var, eps, rs[:, 0:n], after=[t])
            V("tensor_tensor", tiles(src, n), tiles(src, n), rows(rs[:, n:2 * n], DT), ALU.mult)
            if beta is None:
                V("tensor_tensor", tiles(dst, n), tiles(src, n), cols(g, n), ALU.mult)
            else:
                V("tensor_tensor", tiles(src, n), tiles(src, n), cols(g, n), ALU.mult)
                V("tensor_tensor", tiles(dst, n), tiles(src, n), cols(beta, n), ALU.add)
            b.join()

    def residual_linear(name, slabs, x, kt, mo, halves=1):
        width = mo * T

        def evac(j, ap, tok):
            xs = at(X, j, width)
            leave("dve", nc.vector.scalar_tensor_tensor, xs, xs, ALPHA, ap, ALU.mult, ALU.add, after=[tok])
        linear(name, slabs, x, T, evac, kt=kt, mo=mo, halves=halves)
        b.join()

    def copy_out(dst, width=512, e="act"):
        def evac(j, ap, tok):
            if e == "act":
                leave("act", nc.scalar.activation, at(dst, j, width), ap, ACT.Copy, after=[tok])
            else:
                leave("dve", nc.vector.tensor_copy, at(dst, j, width), ap, after=[tok])
        return evac

    def copy_tokens(dst, nt, total):
        def evac(j, ap, tok):
            d = dst.rearrange("p (t c) -> p t c", c=total)[:, :, bass.ds(j * 256, 256)]
            leave("act", nc.scalar.activation, d, ap.rearrange("p (t c) -> p t c", c=256), ACT.Copy, after=[tok])
        return evac

    def feature(ap, n):
        return lambda k: ap[:, k * n:k * n + n]

    def softmax_rows(S, n_rows, width, scale, mx, sm, after):
        V("tensor_reduce", mx, S, AX.X, ALU.max, after=after)
        t = V("tensor_scalar", mx, mx, -scale, None, ALU.mult)
        for r in range(n_rows):
            t2 = A(S[:, r, :], S[:, r, :], ACT.Exp, bias=mx[:, r:r + 1], scale=scale,
                   accum_out=sm[:, r:r + 1], after=[t], chain=False)
        V("reciprocal", sm, sm, after=[t2])
        return V("tensor_tensor", S, S, cols(sm, width), ALU.mult)

    def ffn(layer, w13, w2, xin, n, res_evac):
        with ExitStack() as s:
            h = sb(FFN_T * n, s, "hidden")
            gate = sb(4 * n, s, "gate")

            def evac(j, ap, tok):
                ph = (b.fed - 1) % 4
                gt = gate[:, ph * n:ph * n + n]
                prev = b.slab_out.here()
                t = b.run("act", nc.scalar.activation, gt, ap[:, 0:n], ACT.Silu,
                          after=[tok, Tok(b.slab_out, prev.n - 3, prev.loop) if prev.n > 3 else None], chain=False)
                leave("dve", nc.vector.tensor_tensor, at(h, j, n), gt, ap[:, n:2 * n], ALU.mult, after=[t])
            linear(w13, FFN_T, feature(xin, n), n, evac, mid={"act": 1})
            res_evac(w2, h)

    FB = ExitStack()
    Kall = sb(16 * T, FB, "mem_k")
    Vall = sb(2 * 2048, FB, "mem_v")
    with ExitStack() as L0:
        Mm = sb(DT * T, L0, "mem")
        mix = sb(16 * T, L0, "mix")
        load(Mm[:, :], dram["mem"])
        scond = sb(16, L0, "silu_cond")
        wdt = sb(DT * 16, L0, "w_dt")
        load(wdt[:, :], dram["w_dt"])
        lora = sb(2 * D, L0, "lora")
        load(lora[:, :], dram["lora"])
        rs_ = sb(RW_T * T, L0, "shifted")
        with ExitStack() as S1:
            Z = sb(DT * T, S1, "z")
            XBC = sb(XBC_T * (T + 3), S1, "xbc")
            RW = S1.enter_context(ExitStack())
            rw = sb(RW_T * (T + 1), RW, "rw")
            b.join()
            zero = V("memset", tiles(XBC[:, :], T + 3)[:, :, 0:3], 0.0)
            zero = V("memset", tiles(rw[:, :], T + 1)[:, :, 0:1], 0.0)
            A(scond[:, :], vv("cond"), ACT.Silu)

            for k in range(DT):
                ins = mm(psum[0:16, 4, 0:T], wdt[:, k * 16:k * 16 + 16], X[:, k * T:k * T + T], k == 0, k == DT - 1)
            t_dt = b.pe(ins)

            def ev_z(j, ap, tok):
                leave("act", nc.scalar.activation, at(Z, j, 512), ap, ACT.Silu, after=[tok])

            def padded(dst, pad):
                def evac(j, ap, tok):
                    d = tiles(dst[:, :], T + pad)[:, bass.ds(j * 2, 2), pad:T + pad]
                    leave("act", nc.scalar.activation, d, tiles(ap, T), ACT.Copy, after=[tok])
                return evac
            b.wait("act", zero)
            linear("w_in", 4, feature(X, T), T, ev_z)
            linear("w_in", 6, feature(X, T), T, padded(XBC, 3), row0=4)
            linear("w_in", 13, feature(X, T), T, padded(rw, 1), row0=10)
            b.join()
            cur, prv = tiles(rw[:, :], T + 1)[:, :, 1:T + 1], tiles(rw[:, :], T + 1)[:, :, 0:T]
            R3 = tiles(rs_[:, :], T)
            V("tensor_tensor", R3, prv, cur, ALU.subtract)
            V("tensor_tensor", R3, R3, cols(vv("mu"), T), ALU.mult)
            V("tensor_tensor", R3, R3, cur, ALU.add)
            b.join()
            RW.close()
            tap("z", Z[:, :]), tap("rs", rs_[:, :])

            XC = sb(XBC_T * T, S1, "xc")
            tmp = sb(XBC_T * T, S1, "tmp")
            xc3, tmp3, xb3 = tiles(XC[:, :], T), tiles(tmp[:, :], T), tiles(XBC[:, :], T + 3)
            for w in range(4):
                dst = xc3 if w == 0 else tmp3
                V("tensor_tensor", dst, xb3[:, :, w:w + T], cols(vv("conv_w", w * XBC_T, XBC_T), T), ALU.mult)
                if w:
                    V("tensor_tensor", xc3, xc3, tmp3, ALU.add)
            t = V("tensor_tensor", xc3, xc3, cols(vv("conv_b"), T), ALU.add)
            A(XC[:, :], XC[:, :], ACT.Silu, after=[t])
            sm = sb(5 * T, S1, "dt_work")
            d16 = [sm[0:16, i * T:i * T + T] for i in range(5)]
            heads = vec[0:16, VOFF["heads"][0]:VOFF["heads"][0] + 2]
            V("tensor_scalar", d16[0], psum[0:16, 4, 0:T], heads[:, 0:1], None, ALU.add, after=[t_dt])

            def log1p_exp_neg_abs(x, w1, w2, w3):
                V("tensor_scalar", w1, x, -1.0, None, ALU.mult)
                V("tensor_tensor", w1, w1, x, ALU.min)
                t = A(w1, w1, ACT.Exp, after=[b.c["dve"].here()])
                t = V("tensor_scalar", w2, w1, 1.0, None, ALU.add, after=[t])
                t = A(w3, w2, ACT.Ln, after=[t])
                V("tensor_scalar", w2, w2, -1.0, 1e-30, ALU.add, ALU.max, after=[t])
                V("reciprocal", w2, w2)
                V("tensor_tensor", w2, w2, w1, ALU.mult)
                return V("tensor_tensor", w3, w3, w2, ALU.mult, after=[t])
            log1p_exp_neg_abs(d16[0], d16[1], d16[2], d16[3])
            V("tensor_scalar", d16[0], d16[0], 0.0, None, ALU.max)
            t = V("tensor_tensor", d16[0], d16[0], d16[3], ALU.add)
            an = sb(1, S1, "a_neg")
            t = A(an[0:16, :], heads[:, 1:2], ACT.Exp)
            V("tensor_scalar", d16[1], d16[0], an[0:16, 0:1], -1.0, ALU.mult, ALU.mult, after=[t])
            V("memset", d16[2], 1.0)
            for c in range(NC):
                s_ = slice(c * C, c * C + C)
                V("scan", d16[4][:, s_], d16[2][:, s_], d16[1][:, s_], 0.0, ALU.mult, ALU.add)
            tap("dt", sm[0:16, 0:T]), tap("acum", sm[0:16, 4 * T:5 * T]), tap("xc", XC[:, :])
            YD = mix[:, 0:DT * T]
            V("tensor_tensor", tiles(YD, T), tiles(XC[:, 0:DT * T], T), cols(vv("ssd_d"), T), ALU.mult)
            b.join()
            AE, EA = tmp[:, 0:16 * C], XBC[:, 0:16 * C]
            SEG = Kall[:, 0:16 * C]
            XDT, XDD = Kall[:, 16 * C:16 * C + D], tmp[:, 16 * C:16 * C + D]
            CBm, Bt, S0 = sb(2 * C, S1, "cb"), sb(2 * C, S1, "b_tok"), Kall[:, 16 * C + D:16 * C + 2 * D]
            dT, dec = sb(2 * NH, S1, "dt_tok"), sb(NH, S1, "decay")
            one16 = con[0:16, COFF["ones"]:COFF["ones"] + P]
            id16 = con[0:16, COFF["ident"]:COFF["ident"] + 16]
            for c in range(NC):
                s_ = slice(c * C, c * C + C)
                V("tensor_tensor", tiles(AE[0:16, :], C), rows(d16[4][:, s_], NH), cols(id16, C), ALU.mult)
                b.join()
                for q in range(4):
                    mm(bank(q), one16, AE[0:16, q * 512:q * 512 + 512], True, True)
                nc.tensor.transpose(psum[:, 4, 0:16], d16[0][:, s_], id16)
                nc.tensor.transpose(psum[:, 4, 16:32], d16[4][:, s_], id16)
                for g in range(2):
                    mm(bank(5, g * C, C), XC[:, (8 + g) * T + c * C:(8 + g) * T + c * C + C],
                       XC[:, (10 + g) * T + c * C:(10 + g) * T + c * C + C], True, True)
                for k in range(DT):
                    ins = nc.tensor.transpose(psum[:, 6 + k // 4, (k % 4) * P:(k % 4) * P + P],
                                              XC[:, k * T + c * C:k * T + c * C + C], cc("ident"))
                t = b.pe(ins)
                V("tensor_copy", dT[:, :], psum[:, 4, 0:32], after=[t])
                V("tensor_tensor", tiles(CBm[:, :], C), tiles(bank(5, 0, 2 * C), C), rows(cc("upper"), 2), ALU.mult)
                V("tensor_tensor", tiles(XDT[:, :], HD), psum[:, 6:8, :].rearrange("p b (h d) -> p (b h) d", d=HD),
                  cols(dT[:, 0:16], HD), ALU.mult)
                abc = psum[:, 0:4, :].rearrange("p b (h l) -> p (b h) l", l=C)
                V("tensor_tensor", tiles(SEG[:, :], C), abc, cols(dT[:, 16:32], C), ALU.subtract)
                t = V("tensor_scalar", SEG[:, :], SEG[:, :], 0.0, None, ALU.min)
                if c == 0:
                    V("tensor_tensor", dec[:, :], abc[:, :, C - 1], dT[:, 16:32], ALU.subtract)
                    td = V("tensor_scalar", dec[:, :], dec[:, :], 0.0, None, ALU.min)
                    A(dec[:, :], dec[:, :], ACT.Exp, after=[td])
                else:
                    A(EA[:, :], psum[:, 0:4, :].rearrange("p b n -> p (b n)"), ACT.Exp, after=[t])
                t = A(SEG[:, :], SEG[:, :], ACT.Exp, after=[t])
                for g in range(2):
                    w = slice(g * 8 * C, (g + 1) * 8 * C)
                    V("tensor_tensor", tiles(SEG[:, w], C), tiles(SEG[:, w], C),
                      rows(CBm[:, g * C:g * C + C], 8), ALU.mult, after=[t])
                    if c == 1:
                        V("tensor_tensor", tiles(EA[:, w], C), tiles(EA[:, w], C),
                          rows(XC[:, (10 + g) * T + C:(10 + g) * T + 2 * C], 8), ALU.mult)
                if c == 0:
                    V("tensor_tensor", tiles(XDD[:, :], HD), tiles(XDT[:, :], HD), cols(dec[:, :], HD), ALU.mult)
                b.join()
                for pr in range(8):
                    o = bank(pr // 2, (pr % 2) * 256, 256)
                    ins = mm(o, XDT[:, pr * P:pr * P + P], SEG[:, pr * 256:pr * 256 + 256], True, c == 0)
                    if c:
                        ins = mm(o, S0[:, pr * P:pr * P + P], EA[:, pr * 256:pr * 256 + 256], False, True)
                ty = b.pe(ins)
                if c == 0:
                    for g in range(2):
                        ins = nc.tensor.transpose(bank(4, g * P, P), XC[:, (8 + g) * T:(8 + g) * T + C], cc("ident"))
                    t = A(Bt[:, :], bank(4, 0, 256), ACT.Copy, after=[b.pe(ins)])
                    b.wait("pe", t)
                    for g in range(2):
                        ins = mm(bank(5 + g), Bt[:, g * P:g * P + P], XDD[:, g * 512:g * 512 + 512], True, True)
                    A(S0[:, :], psum[:, 5:7, :].rearrange("p b n -> p (b n)"), ACT.Copy, after=[b.pe(ins)])
                for hh in range(2):
                    p_ = slice(64 * hh, 64 * hh + 64)
                    o = tiles(YD, T)[p_, :, s_]
                    y = psum[p_, 0:4, :].rearrange("p b (q e l) -> p (b q) e l", q=2, e=2)[:, :, hh, :]
                    V("tensor_tensor", o, o, y, ALU.add, after=[ty])
                b.join()
            V("tensor_tensor", YD, YD, Z[:, :], ALU.mult)
            tap("yz", YD)
            sq = tmp[:, 0:DT * T]
            t = A(sq, YD, ACT.Square, after=[b.c["dve"].here()])
            b.wait("pe", t)
            t, _ = mean_over(sq, T, "ones_half", DT, 4, 4)
            rsd = sb(4 * T, S1, "rstd")
            rsqrt(rsd[:, 2 * T:], bank(4), EPS5, rsd[:, 0:2 * T], after=[t])
            for g in range(2):
                v = tiles(YD[:, g * 4 * T:(g + 1) * 4 * T], T)
                V("tensor_tensor", v, v, rows(rsd[:, (2 + g) * T:(3 + g) * T], 4), ALU.mult)
            V("tensor_tensor", tiles(YD, T), tiles(YD, T), cols(vv("ssd_g"), T), ALU.mult)
            tap("yssd", YD)
            b.join()

        with ExitStack() as S2:
            N8 = DT * T
            Rr, Kr, Vr = rs_[:, 0:N8], rs_[:, N8:2 * N8], rs_[:, 2 * N8:3 * N8]
            lo, gl = rs_[:, 24 * T:25 * T], rs_[:, 25 * T:26 * T]
            SG, CS, KK, BV = (sb(N8, S2, n) for n in ("sig_w", "cum", "kk", "b_vec"))
            t = A(lo[0:64, :], lo[0:64, :], ACT.Tanh)
            t = A(gl, gl, ACT.Sigmoid)
            b.wait("pe", t)
            for half, dst, bias in ((0, SG, "w0"), (1, BV, "a0")):
                p_ = slice(64 * half, 64 * half + 64)
                for k in range(DT):
                    ins = mm(bank(half * 4 + k // 2, (k % 2) * T, T), lora[p_, k * P:k * P + P], lo[p_, :], True, True)
                t = b.pe(ins)
                for k in range(DT):
                    A(dst[:, k * T:k * T + T], bank(half * 4 + k // 2, (k % 2) * T, T), ACT.Sigmoid,
                      bias=vv(bias, k, 1), after=[t], chain=False)
            t_sg = b.c["act"].here()
            V("tensor_tensor", tiles(KK[:, :], T), tiles(Kr, T), cols(vv("k_k"), T), ALU.mult)
            t = A(CS[:, :], KK[:, :], ACT.Square, after=[b.c["dve"].here()])
            b.wait("pe", t)
            for half in range(2):
                sl = slice(half * 4 * T, (half + 1) * 4 * T)
                t, _ = mean_over(CS[:, sl], T, "head_sum", 4, 1, half * 2)
                src = psum[:, half * 2:half * 2 + 2, :].rearrange("p b n -> p (b n)")
                t = V("tensor_scalar", CS[:, sl], src, 1e-24, None, ALU.max, after=[t])
            t = A(CS[:, :], CS[:, :], ACT.Sqrt, after=[t])
            V("reciprocal", CS[:, :], CS[:, :], after=[t])
            V("tensor_tensor", KK[:, :], KK[:, :], CS[:, :], ALU.mult)
            CS3 = tiles(CS[:, :], T)
            V("tensor_scalar", CS[:, :], BV[:, :], -1.0, None, ALU.add, after=[t_sg])
            V("tensor_tensor", CS3, CS3, cols(vv("k_a"), T), ALU.mult)
            V("scalar_tensor_tensor", Kr, CS[:, :], 1.0, Kr, ALU.add, ALU.mult)
            V("tensor_tensor", BV[:, :], BV[:, :], KK[:, :], ALU.mult)
            on = sb(C, S2, "ones_row")
            G("memset", on[:, :], 1.0)
            b.wait("dve", b.c["pool"].here())
            for q in range(DT * NC):
                V("scan", CS[:, q * C:q * C + C], on[:, :], SG[:, q * C:q * C + C], 0.0, ALU.mult, ALU.add, chain=q == 0)
            edge = sb(2 * DT * NC, S2, "mid")
            q3 = tiles(CS[:, :], C)
            V("tensor_copy", edge[:, 0:16], q3[:, :, C // 2 - 1])
            V("tensor_tensor", q3, q3, cols(edge[:, 0:16], C), ALU.subtract)
            e3 = edge[:, :].rearrange("p (w t c) -> p w t c", w=2, c=2)
            V("tensor_tensor", e3[:, 1, :, 0], q3.rearrange("p (t c) n -> p t c n", c=2)[:, :, 0, C - 1],
              e3[:, 0, :, 1], ALU.add)
            fac = sb(DT, S2, "carry")
            A(fac[:, :], e3[:, 1, :, 0], ACT.Exp, scale=-KAPPA, after=[b.c["dve"].here()])
            tap("kk", KK[:, :]), tap("cs", CS[:, :]), tap("kr", Kr), tap("bv", BV[:, :])

            EX = sb(3 * T, S2, "exps")
            AR = sb(2 * 2 * C, S2, "a_r")
            KB = sb(2 * T, S2, "k_b")
            VP = sb(T, S2, "v_pair")
            TR = sb(4 * P, S2, "by_token")
            GB, GK = sb(4 * 2 * C, S2, "gram_b"), sb(4 * 2 * C, S2, "gram_k")
            ML = sb(2 * 4 * C, S2, "level")
            XI, XT, T1 = (sb(4 * C, S2, n) for n in ("inv", "inv_t", "prod"))
            R0, SA, ST = sb(P, S2, "rhs"), sb(P, S2, "sa"), sb(P, S2, "state")
            diff = sb(T, S2, "diff")
            up2 = con[:, COFF["upper_strict"]:COFF["upper_strict"] + 2 * C]
            b.join()

            def ev_k(j, ap, tok):
                leave("act", nc.scalar.activation, at(Kall, j, 512), ap, ACT.Copy, after=[tok])

            def ev_v(j, ap, tok):
                d = tiles(Vall[:, :], 2048)[:, :, bass.ds(j * 256, 256)]
                leave("act", nc.scalar.activation, d, tiles(ap, 256), ACT.Copy, after=[tok])

            def ev_ada(j, ap, tok):
                bias = cols(vv("ada_b")[:, bass.ds(j * 2, 2)], 2)
                leave("dve", nc.vector.tensor_tensor, tiles(at(mods, j, 4), 2), tiles(ap, 2), bias, ALU.add, after=[tok])

            s_k = Stream("w_memk", 8, feature(Mm, T), T, ev_k, banks=(7,), shared=True)
            s_v = Stream("w_memv", 8, feature(Mm, T), T, ev_v, tok=True, banks=(7,), shared=True)
            s_ada = Stream("w_ada", 8, lambda k: scond[:, k * 2:k * 2 + 2], 2, ev_ada, banks=(7,), shared=True)
            per = {b.c["pe"]: 27, b.c["act"]: 19, b.c["dve"]: 24, b.c["pool"]: 6, b.slab_done: 8, b.slab_out: 8}
            per.update({c: 32 for c in b.slot_full})
            fed0, g0 = b.fed, b.fed
            ar4 = AR[:, :].rearrange("p (c w n) -> p c w n", c=2, w=2)
            gb4, gk4 = (tiles(g[:, :], C).rearrange("p (q w) n -> p q w n", w=2) for g in (GB, GK))
            with b.loop(DT, per) as i:
                side = [lambda: s_k.step(i, g0), lambda: s_v.step(i, g0 + 1)] + \
                       [(lambda u=u: s_ada.step(i * 6 + u, g0 + 2 + u)) for u in range(6)]
                old = [b.before(e) for e in ("pe", "act", "dve", "pool")]
                cs_i, sg_i = at(CS, i, T), at(SG, i, T)
                t_d = V("tensor_tensor", diff[:, :], cs_i, sg_i, ALU.subtract, after=old)
                A(EX[:, 0:T], cs_i, ACT.Exp, scale=-KAPPA, after=old, chain=False)
                t_e = A(EX[:, 2 * T:], cs_i, ACT.Exp, scale=KAPPA, chain=False)
                t_e2 = A(EX[:, T:2 * T], diff[:, :], ACT.Exp, scale=-KAPPA, after=[t_d], chain=False)
                t_v = A(VP[:, :], at(Vr, i, T), ACT.Copy, chain=False)
                V("tensor_tensor", KB[:, 0:T], at(Kr, i, T), EX[:, 2 * T:], ALU.mult, after=[t_e], chain=False)
                V("tensor_tensor", KB[:, T:2 * T], at(BV, i, T), EX[:, 2 * T:], ALU.mult, chain=False)
                V("tensor_tensor", ar4[:, :, 1, :], tiles(at(Rr, i, T), C), tiles(EX[:, 0:T], C), ALU.mult, chain=False)
                t = V("scalar_tensor_tensor", ar4[:, :, 0, :], tiles(at(KK, i, T), C), -1.0, tiles(EX[:, T:2 * T], C),
                      ALU.mult, ALU.mult, after=[t_e2], chain=False)
                b.wait("pe", t, t_v)
                for e in range(2):
                    p_ = slice(64 * e, 64 * e + 64)
                    for c in range(NC):
                        mm(bank(1 + e, c * 256, 256), KB[p_, T + c * C:T + c * C + C], AR[p_, c * 256:c * 256 + 256], True, True)
                        ins = mm(bank(5 + e, c * C, C), AR[p_, c * 256:c * 256 + C], KB[p_, T + c * C:T + c * C + C], True, True)
                t_gb = b.pe(ins)
                for e in range(2):
                    p_ = slice(64 * e, 64 * e + 64)
                    for c in range(NC):
                        ins = mm(bank(3 + e, c * 256, 256), KB[p_, c * C:c * C + C], AR[p_, c * 256:c * 256 + 256], True, True)
                t_gk = b.pe(ins)
                for q, src in enumerate((VP[:, 0:C], VP[:, C:T], KB[:, 0:C], KB[:, T:T + C])):
                    ins = nc.tensor.transpose(bank(0, q * P, P), src, cc("ident"))
                t_tr = b.pe(ins)
                two = lambda lo: psum[:, lo:lo + 2, :].rearrange("p b (c n) -> p (b c) n", n=256)
                t_m = V("tensor_tensor", tiles(GB[:, :], 256), two(1), rows(up2, 4), ALU.mult, after=[t_gb])
                x4, t4 = tiles(XI[:, :], C), tiles(XT[:, :], C)
                t_l = G("tensor_tensor", tiles(ML[:, 4 * C:], C), gb4[:, :, 0, :], rows(cc("lev1"), 4), ALU.mult, after=[t_m])
                t_i1 = V("tensor_tensor", x4, psum[:, 5:7, 0:2 * C].rearrange("p b (c n) -> p b c n", n=C),
                         rows(cc("low0"), 4).rearrange("p (b c) n -> p b c n", b=2), ALU.mult, chain=False) if False else \
                    [V("tensor_tensor", tiles(XI[:, e * 2 * C:(e + 1) * 2 * C], C), tiles(psum[:, 5 + e, 0:2 * C], C),
                       rows(cc("low0"), 2), ALU.mult, chain=False) for e in range(2)][-1]
                V("tensor_tensor", t4, gb4[:, :, 0, :], rows(cc("lev0"), 4), ALU.mult)
                V("tensor_tensor", x4, x4, rows(cc("ident"), 4), ALU.add, chain=False, after=[t_i1])
                t_x = V("tensor_tensor", t4, t4, rows(cc("ident"), 4), ALU.add)
                t_tb = A(TR[:, :], bank(0), ACT.Copy, after=[t_tr], chain=False)
                side[0]()
                t_t = t_gkm = V("tensor_tensor", tiles(GK[:, :], 256), two(3), rows(up2, 4), ALU.mult, after=[t_gk], chain=False)
                for lev in range(1, 7):
                    m = ML[:, (lev % 2) * 4 * C:(lev % 2 + 1) * 4 * C]
                    b.wait("pe", t_l, t_x, t_t, t_tb)
                    for q in range(4):
                        ins = mm(bank(0, q * C, C), m[:, q * C:q * C + C], XI[:, q * C:q * C + C], True, True)
                    t_p = b.pe(ins)
                    t_c = A(T1[:, :], bank(0), ACT.Copy, after=[t_p], chain=False)
                    if lev < 6:
                        t_l = G("tensor_tensor", tiles(ML[:, ((lev + 1) % 2) * 4 * C:((lev + 1) % 2 + 1) * 4 * C], C),
                                gb4[:, :, 0, :], rows(cc(f"lev{lev + 1}"), 4), ALU.mult, after=[t_p], chain=False)
                    if lev in SIDE_AT:
                        side[SIDE_AT[lev]]()
                    b.wait("pe", t_c)
                    for q in range(4 if lev < 6 else 0):
                        ins = mm(bank(5, q * C, C), XT[:, q * C:q * C + C], T1[:, q * C:q * C + C], True, True)
                    t_p1 = b.pe(ins) if lev < 6 else None
                    for q in range(4):
                        ins = mm(bank(6, q * C, C), T1[:, q * C:q * C + C], XT[:, q * C:q * C + C], True, True)
                    t_p2 = b.pe(ins)
                    if lev < 6:
                        t_x = V("tensor_tensor", XI[:, :], XI[:, :], bank(5), ALU.add, after=[t_p1], chain=False)
                    t_t = V("tensor_tensor", XT[:, :], XT[:, :], bank(6), ALU.add, after=[t_p2], chain=False)
                t_s = t_y = None
                for c in range(NC):
                    rb = 0 if c == 0 else 4
                    v_c = TR[:, c * P:c * P + P]
                    b.wait("pe", t_t, t_s, t_gkm)
                    if c:
                        mm(bank(rb, 0, P), AR[:, 256:256 + C], ST[:, :], True, False)
                    for e in range(2):
                        ins = mm(bank(rb, e * 64, 64), gk4[:, 2 * e + c, 0, :], v_c[:, e * 64:e * 64 + 64], c == 0, e == 1 or c == 0)
                    t = A(R0[:, :], bank(rb, 0, P), ACT.Copy, after=[b.pe(ins)], chain=False)
                    for e in range(2):
                        mm(bank(1 + c, e * P, P), v_c, gk4[:, 2 * e + c, 1, :], e == 0, False)
                        if c:
                            mm(bank(1 + c, e * P, P), ST[:, :], AR[:, 256 + C:256 + 2 * C], False, False)
                    if c == 0:
                        mm(bank(3, 0, P), TR[:, 256:384], v_c, True, False)
                    b.wait("pe", t)
                    for e in range(2):
                        ins = mm(bank(rb, 128 + e * 64, 64), XT[:, (2 * e + c) * C:(2 * e + c) * C + C],
                                 R0[:, e * 64:e * 64 + 64], True, True)
                    t = A(SA[:, :], bank(rb, 128, P), ACT.Copy, after=[b.pe(ins)], chain=False)
                    if c == 0:
                        side[7]()
                    b.wait("pe", t)
                    if c == 0:
                        ins = mm(bank(3, 0, P), TR[:, 384:512], SA[:, :], False, True)
                        t_s = V("scalar_tensor_tensor", ST[:, :], bank(3, 0, P), fac[:, bass.ds(i, 1)], cc("head_sum"),
                                ALU.mult, ALU.mult, after=[b.pe(ins)], chain=False)
                    for e in range(2):
                        ins = mm(bank(1 + c, e * P, P), SA[:, :], gb4[:, 2 * e + c, 1, :], False, e == 1)
                    t_y = b.pe(ins)
                    for e in range(2):
                        p_ = slice(64 * e, 64 * e + 64)
                        A(mix[p_, bass.ds(N8 + i * T + c * C, C)], psum[p_, 1 + c, e * P:e * P + P], ACT.Copy,
                          after=[t_y], chain=False)
            b.fed = fed0 + 8 * DT
            tap("ywkv", mix[:, N8:2 * N8]), tap("mods", mods[:, :])
            Y = mix[:, N8:2 * N8]
            b.join()

            def head_stat(src, matrix):
                t, _ = mean_over(src, T, matrix, DT, 1, 0)
                return t, psum[:, 0:4, :].rearrange("p b n -> p (b n)")
            t, m_ = head_stat(Y, "head_mean")
            t = V("tensor_tensor", Y, Y, m_, ALU.subtract, after=[t])
            t = A(SG[:, :], Y, ACT.Square, after=[t])
            b.wait("pe", t)
            t, m_ = head_stat(SG, "head_mean")
            rsqrt(CS[:, :], m_, LNX_EPS, SG[:, :], after=[t])
            V("tensor_tensor", Y, Y, CS[:, :], ALU.mult)
            V("tensor_tensor", tiles(Y, T), tiles(Y, T), cols(vv("lnx_g"), T), ALU.mult)
            V("tensor_tensor", tiles(Y, T), tiles(Y, T), cols(vv("lnx_b"), T), ALU.add)
            V("tensor_tensor", KK[:, :], Rr, Kr, ALU.mult)
            t = V("tensor_tensor", tiles(KK[:, :], T), tiles(KK[:, :], T), cols(vv("r_k"), T), ALU.mult)
            b.wait("pe", t)
            t, m_ = head_stat(KK, "head_sum")
            V("tensor_tensor", KK[:, :], Vr, m_, ALU.mult, after=[t])
            V("tensor_tensor", Y, Y, KK[:, :], ALU.add)
            b.join()
            for k in range(DT):
                ins = mm(bank(k // 2, (k % 2) * T, T), lora[:, D + k * P:D + k * P + P], gl, True, True)
            V("tensor_tensor", Y, Y, psum[:, 0:4, :].rearrange("p b n -> p (b n)"), ALU.mult, after=[b.pe(ins)])
            tap("yrwkv", Y)
            b.join()
        residual_linear("w_mix0", 8, feature(mix, T), 16, 1)

    def after_mix(layer):
        layer_norm(X[:, :], X[:, :], T, vv("mix_g", 8 * layer, 8), vv("mix_b", 8 * layer, 8), EPS5, None)
        tap(f"mix{layer}", X[:, :])
        with ExitStack() as s:
            Q, O = sb(DT * T, s, "q"), sb(DT * T, s, "o")
            linear(f"w_xq{layer}", 4, feature(X, T), T, copy_out(Q))
            b.join()
            S = sb(8 * T, s, "probs")
            PT = sb(8 * T, s, "probs_t")
            st = sb(16, s, "stats")
            for h in range(4):
                for qt in range(2):
                    for dd in range(2):
                        k = 2 * h + dd
                        ins = mm(bank(h, qt * T, T), Q[:, k * T + qt * P:k * T + qt * P + P],
                                 Kall[:, (8 * layer + k) * T:(8 * layer + k + 1) * T], dd == 0, dd == 1)
            t = b.pe(ins)
            t = A(S[:, :], psum[:, 0:4, :].rearrange("p b n -> p (b n)"), ACT.Copy, after=[t])
            t = softmax_rows(tiles(S[:, :], T), 8, T, 256 ** -0.5, st[:, 0:8], st[:, 8:16], [t])
            b.wait("pe", t)
            for h in range(4):
                for qt in range(2):
                    for kt in range(2):
                        ins = nc.tensor.transpose(bank(4 + h, kt * T + qt * P, P),
                                                  S[:, (2 * h + qt) * T + kt * P:(2 * h + qt) * T + kt * P + P], cc("ident"))
            t = A(PT[:, :], psum[:, 4:8, :].rearrange("p b n -> p (b n)"), ACT.Copy, after=[b.pe(ins)])
            b.wait("pe", t)
            for k in range(DT):
                for kt in range(2):
                    v = Vall[:, kt * 2048 + layer * D + k * P:kt * 2048 + layer * D + k * P + P]
                    ins = mm(bank(k // 2, (k % 2) * T, T), v, PT[:, (2 * (k // 2) + kt) * T:(2 * (k // 2) + kt + 1) * T],
                             kt == 0, kt == 1)
            A(O[:, :], psum[:, 0:4, :].rearrange("p b n -> p (b n)"), ACT.Copy, after=[b.pe(ins)])
            b.join()
            residual_linear(f"w_xo{layer}", 4, feature(O, T), 8, 2)
        layer_norm(X[:, :], X[:, :], T, vv("xa_g", 8 * layer, 8), vv("xa_b", 8 * layer, 8), EPS5, None)
        tap(f"xa{layer}", X[:, :])
        ffn(layer, f"w13_{layer}", f"w2_{layer}", X, T,
            lambda w2, h: (b.join(), residual_linear(w2, 16, feature(h, T), 11, 1, halves=2)))
        layer_norm(X[:, :], X[:, :], T, vv("ffn_g", 8 * layer, 8), vv("ffn_b", 8 * layer, 8), EPS5, None)
        tap(f"ffn{layer}", X[:, :])

    after_mix(0)

    with ExitStack() as s:
        Q, K, O = (sb(DT * T, s, n) for n in ("q", "k", "o"))
        Vt = sb(2 * D, s, "v_tok")
        am = sb(2 * T, s, "causal")
        b.join()
        b.wait("sp", *b.all())
        tm = load(am[:, :], dram["causal"], "causal")
        linear("w_qkv", 4, feature(X, T), T, copy_out(Q))
        linear("w_qkv", 4, feature(X, T), T, copy_out(K), row0=4)
        linear("w_qkv", 4, feature(X, T), T, copy_tokens(Vt[:, :], 2, D), tok=True, row0=8)
        b.join()
        Qs, Ks, Vs = sb(2 * T, s, "q_heads"), sb(2 * T, s, "k_heads"), sb(2 * 2 * P, s, "v_heads")
        S, PT = sb(8 * T, s, "probs"), sb(8 * T, s, "probs_t")
        st = sb(16, s, "stats")
        b.wait("dve", tm)
        S3 = S[:, :].rearrange("p (h q k) -> p h q k", h=4, q=2)
        with b.loop(4, {b.c["pe"]: 3, b.c["act"]: 12, b.c["dve"]: 10}) as i:
            t1 = A(Qs[:, :], at(Q, i, 2 * T), ACT.Copy, chain=False, after=[b.before("pe")])
            t2 = A(tiles(Vs[:, :], 256), tiles(Vt[:, :], D)[:, :, bass.ds(i * 256, 256)], ACT.Copy, chain=False)
            t3 = V("tensor_copy", Ks[:, :], at(K, i, 2 * T), after=[b.before("pe")], chain=False)
            b.wait("pe", t1, t2, t3, b.before("dve"))
            for h in range(4):
                p_ = slice(64 * (h % 2), 64 * (h % 2) + 64)
                for qt in range(2):
                    ins = mm(bank(h, qt * T, T), Qs[p_, (h // 2) * T + qt * P:(h // 2) * T + qt * P + P],
                             Ks[p_, (h // 2) * T:(h // 2) * T + T], True, True)
            t = b.pe(ins)
            for h in range(4):
                t = V("tensor_tensor", S[:, h * 2 * T:(h + 1) * 2 * T], bank(h), am[:, :], ALU.add, after=[t, t2], chain=False)
            t = softmax_rows(tiles(S[:, :], T), 8, T, HD ** -0.5, st[:, 0:8], st[:, 8:16], [t])
            b.wait("pe", t)
            for h in range(4):
                for qt in range(2):
                    for kt in range(2):
                        ins = nc.tensor.transpose(bank(4 + h, kt * T + qt * P, P),
                                                  S[:, (2 * h + qt) * T + kt * P:(2 * h + qt) * T + kt * P + P], cc("ident"))
            t = A(PT[:, :], psum[:, 4:8, :].rearrange("p b n -> p (b n)"), ACT.Copy, after=[b.pe(ins)], chain=False)
            b.wait("pe", t)
            for h in range(4):
                for kt in range(2):
                    ins = mm(bank(h, 0, T), Vs[:, kt * 256 + (h // 2) * P:kt * 256 + (h // 2) * P + P],
                             PT[:, (2 * h + kt) * T:(2 * h + kt + 1) * T], kt == 0, kt == 1)
            t = b.pe(ins)
            Oi = tiles(at(O, i, 2 * T), T)
            for hh in range(2):
                p_ = slice(64 * hh, 64 * hh + 64)
                src = psum[p_, 0:4, 0:T].rearrange("p (a e) n -> p a e n", e=2)[:, :, hh, :]
                if hh == 0:
                    t_o = V("tensor_copy", Oi[p_, :, :], src, after=[t], chain=False)
                else:
                    A(Oi[p_, :, :], src, ACT.Copy, after=[t, t_o], chain=False)
        b.join()
        residual_linear("w_aout", 4, feature(O, T), 8, 2)
    after_mix(1)

    FB.close()
    R = sb(DT * 2 * T, name="streams")
    r4 = R[:, :].rearrange("p (t s n) -> p t s n", s=2, n=T)
    b.wait("sp", *b.all())
    t = load(r4[:, :, 0, :], dram["ctx"].rearrange("p (t n) -> p t n", n=T), "ctx")
    V("tensor_copy", r4[:, :, 1, :], tiles(X[:, :], T))
    for e in ("act", "dve"):
        b.wait(e, t)
    b.join()

    def mod(layer, part, lo=0, n=16):
        o = layer * 96 + part * 16 + lo
        return mods[:, o:o + n]

    def modulate(src, dst, ns, layer, gain, part):
        n = ns * T
        with ExitStack() as s:
            sq, rs, gm = sb(DT * n, s), sb(2 * n, s), sb(16, s)
            b.join()
            t = A(sq[:, :], src, ACT.Square)
            b.wait("pe", t)
            t, (ms,) = mean_over(sq, n, "ones_model", DT, DT, 4)
            rsqrt(rs[:, n:2 * n], ms, EPS6, rs[:, 0:n], after=[t])
            V("tensor_scalar", gm[:, :], mod(layer, part + 1), 1.0, None, ALU.add)
            V("tensor_tensor", tiles(gm[:, :], 2), tiles(gm[:, :], 2), cols(vv(gain, 8 * layer, 8), 2), ALU.mult)
            V("tensor_tensor", tiles(dst, n), tiles(src, n), rows(rs[:, n:2 * n], DT), ALU.mult)
            if ns == 2:
                g, h, v = gm[:, :], mod(layer, part), tiles(dst, T)
            else:
                g, h, v = tiles(gm[:, :], 2)[:, :, 1], tiles(mod(layer, part), 2)[:, :, 1], tiles(dst, T)
            V("tensor_tensor", v, v, cols(g, T), ALU.mult)
            V("tensor_tensor", v, v, cols(h, T), ALU.add)
            b.join()

    def gated_linear(name, slabs, x, kt, mo, layer, part, halves=1):
        width = mo * 2 * T
        with ExitStack() as s:
            tmp = sb(4 * width, s)

            def evac(j, ap, tok):
                tm = tmp[:, 0:width]
                gates = mods[:, bass.ds(layer * 96 + part * 16 + j * (2 * mo), 2 * mo)]
                t = V("tensor_tensor", tiles(tm, T), tiles(ap, T), cols(gates, T), ALU.mult,
                      after=[tok, b.slab_out.here()], chain=False)
                leave("dve", nc.vector.tensor_tensor, at(R, j, width), at(R, j, width), tm, ALU.add, after=[t])
            linear(name, slabs, x, 2 * T, evac, kt=kt, mo=mo, halves=halves, mid={"dve": 1})
            b.join()

    with ExitStack() as s:
        W2 = 2 * T
        PW = T + 2 * PAD
        hm = sb(DT * W2, s, "modulated")
        YP = sb(DT * 2 * PW, s, "glu_padded")
        sg = sb(4 * W2, s, "sig")
        acc = sb(DT * W2, s, "conv")
        yp3 = tiles(YP[:, :], PW)
        V("memset", YP[:, :], 0.0)
        modulate(R[:, :], hm[:, :], 2, 0, "norm_mix", 0)
        ob = VOFF["conv_b1"][0]

        def ev_glu(j, ap, tok):
            ph = (b.fed - 1) % 4
            gt = sg[:, ph * W2:ph * W2 + W2]
            n = b.slab_out.n
            t = A(gt, ap[:, W2:2 * W2], ACT.Sigmoid, bias=vec[:, bass.ds(j + (ob + 8), 1)], chain=False,
                  after=[tok, Tok(b.slab_out, n - 3, b.slab_out.loop)])
            leave("dve", nc.vector.scalar_tensor_tensor, yp3[:, bass.ds(j * 2, 2), PAD:PAD + T],
                  tiles(ap[:, 0:W2], T), vec[:, bass.ds(j + ob, 1)], tiles(gt, T), ALU.add, ALU.mult, after=[t])
        linear("w_c1", 8, feature(hm, W2), W2, ev_glu, mid={"act": 1})
        b.join()
        od = VOFF["conv_dw"][0]
        with b.loop(DT, {b.c["dve"]: CONV_W}) as i:
            a_i = tiles(at(acc, i, W2), T)
            for k in range(CONV_W):
                src = yp3[:, bass.ds(i * 2, 2), k:k + T]
                wk = vec[:, bass.ds(i + (od + 8 * k), 1)]
                if k == 0:
                    V("tensor_scalar", a_i, src, wk, vec[:, bass.ds(i + VOFF["conv_dw_b"][0], 1)], ALU.mult, ALU.add)
                else:
                    V("scalar_tensor_tensor", a_i, src, wk, a_i, ALU.mult, ALU.add)
        b.join()
        tap("dwconv", acc[:, :])
        layer_norm(acc[:, :], acc[:, :], W2, vv("conv_norm"), None, EPS6, None)
        A(acc[:, :], acc[:, :], ACT.Silu)
        b.join()
        gated_linear("w_c2", 4, feature(acc, W2), 8, 2, 0, 2)
    tap("convout", R[:, :])
    with ExitStack() as s:
        hm = sb(DT * 2 * T, s, "modulated")
        modulate(R[:, :], hm[:, :], 2, 0, "norm_ffn", 3)
        ffn(0, "gu_0", "down_0", hm, 2 * T,
            lambda w2, h: (b.join(), gated_linear(w2, 16, feature(h, 2 * T), 11, 1, 0, 5, halves=2)))
    tap("l0out", R[:, :])

    def gated_x(name, slabs, x, kt, mo, layer, part, halves=1):
        def evac(j, ap, tok):
            gate = mods[:, bass.ds(j * 2 + (layer * 96 + part * 16 + 1), 1)]
            leave("dve", nc.vector.scalar_tensor_tensor, at(X, j, T), ap, gate, at(X, j, T), ALU.mult, ALU.add, after=[tok])
        linear(name, slabs, x, T, evac, kt=kt, mo=mo, halves=halves)
        b.join()

    with ExitStack() as s:
        V("tensor_copy", tiles(X[:, :], T), r4[:, :, 1, :])
        QX, KX = sb(DT * T, s, "q"), sb(DT * 2 * T, s, "k")
        Vt = sb(4 * 2048, s, "v_tok")
        Gt, O = sb(16 * T, s, "gate"), sb(16 * T, s, "o")
        with ExitStack() as s2:
            hm = sb(DT * 2 * T, s2, "modulated")
            modulate(R[:, :], hm[:, :], 2, 1, "norm_mix", 0)
            xs = lambda k: hm[:, k * 2 * T + T:(k + 1) * 2 * T]

            def ev_g(j, ap, tok):
                leave("act", nc.scalar.activation, at(Gt, j, 512), ap, ACT.Silu, after=[tok])
            linear("w_ret", 4, xs, T, copy_out(QX))
            linear("w_ret", 4, feature(hm, 2 * T), 2 * T, copy_out(KX, 1024), row0=4)
            linear("w_ret", 8, feature(hm, 2 * T), 2 * T, copy_tokens(Vt[:, :], 4, 2048), tok=True, row0=8)
            linear("w_ret", 8, xs, T, ev_g, row0=16)
            b.join()
        with ExitStack() as s2:
            dist, rope = sb(12 * T, s2, "dist"), sb(4 * T, s2, "rope")
            b.wait("sp", *b.all())
            t = [load(dist[:, :], dram["dist"], "dist"), load(rope[:, :], dram["rope"], "rope")]
            b.wait("dve", t)
            b.wait("act", t)
            tmp = sb(DT * T, s2)
            tab = rope[:, :].rearrange("p (w m n) -> p w m n", w=2, m=2)
            kx4 = KX[:, :].rearrange("p (h m s n) -> p h m s n", m=2, s=2, n=T)
            for dst, src, width in ((QX[:, :].rearrange("p (h m n) -> p h m n", m=2, n=T), QX, T),
                                    (kx4[:, :, :, 1, :], KX, 2 * T)):
                for k in range(DT):
                    ins = mm(bank(k // 2, (k % 2) * T, T), cc("swap"), src[:, k * width + width - T:(k + 1) * width], True, True)
                t = b.pe(ins)
                tp = tmp[:, :].rearrange("p (h m n) -> p h m n", m=2, n=T)
                tb = lambda w: tab[:, w:w + 1, :, :].broadcast_to([P, 4, 2, T])
                V("tensor_tensor", tp, psum[:, 0:4, :].rearrange("p b (m n) -> p b m n", m=2), tb(1), ALU.mult, after=[t])
                V("tensor_tensor", dst, dst, tb(0), ALU.mult)
                V("tensor_tensor", dst, dst, tp, ALU.add)
                b.join()
            dw = sb(5 * 8, s2)
            w_ = [dw[:, i * 8:i * 8 + 8] for i in range(5)]
            log1p_exp_neg_abs(vv("decay"), w_[0], w_[1], w_[2])
            V("tensor_scalar", w_[3], vv("decay"), 0.0, None, ALU.min)
            lg = w_[3]
            t_lg = V("tensor_tensor", lg, lg, w_[2], ALU.subtract)
            WF, WB, SW = sb(4 * T, s2, "w_fwd"), sb(4 * T, s2, "w_bwd"), sb(4 * T, s2, "weights")
            for h in range(4):
                t = A(WF[:, :], dist[:, 0:4 * T], ACT.Exp, scale=lg[:, h:h + 1], after=[b.c["dve"].here()])
                t2 = A(WB[:, :], dist[:, 4 * T:8 * T], ACT.Exp, scale=lg[:, 4 + h:5 + h])
                for st_ in range(4):
                    for dd in range(2):
                        k = 2 * h + dd
                        ins = mm(bank(st_ // 2, (st_ % 2) * T, T), KX[:, k * 512 + st_ * P:k * 512 + st_ * P + P],
                                 QX[:, k * T:k * T + T], dd == 0, dd == 1)
                tq = b.pe(ins)
                V("tensor_tensor", WF[:, 2 * T:], WF[:, 2 * T:], dist[:, 8 * T:10 * T], ALU.mult, after=[t])
                V("tensor_tensor", WB[:, 2 * T:], WB[:, 2 * T:], dist[:, 10 * T:12 * T], ALU.mult, after=[t2])
                V("tensor_tensor", WF[:, :], WF[:, :], WB[:, :], ALU.add)
                t = V("scalar_tensor_tensor", SW[:, :], psum[:, 0:2, :].rearrange("p b n -> p (b n)"), 256 ** -0.5, WF[:, :],
                      ALU.mult, ALU.mult, after=[tq])
                b.wait("pe", t)
                for m in range(4):
                    for st_ in range(4):
                        ins = mm(bank(2 + m // 2, (m % 2) * T, T), Vt[:, st_ * 2048 + h * 512 + m * P:st_ * 2048 + h * 512 + m * P + P],
                                 SW[:, st_ * T:st_ * T + T], st_ == 0, st_ == 3)
                A(O[:, h * 4 * T:(h + 1) * 4 * T], psum[:, 2:4, :].rearrange("p b n -> p (b n)"), ACT.Copy, after=[b.pe(ins)])
                b.join()
        tap("reto", O[:, :])
        with ExitStack() as s2:
            sq, rs = sb(16 * T, s2), sb(8 * T, s2)
            t = A(sq[:, :], O[:, :], ACT.Square)
            b.wait("pe", t)
            t, _ = mean_over(sq, T, "ones_half", 16, 4, 4)
            rsqrt(rs[:, 4 * T:], psum[:, 4:6, :].rearrange("p b n -> p (b n)"), EPS6, rs[:, 0:4 * T], after=[t])
            for h in range(4):
                v = tiles(O[:, h * 4 * T:(h + 1) * 4 * T], T)
                V("tensor_tensor", v, v, rows(rs[:, (4 + h) * T:(5 + h) * T], 4), ALU.mult)
            V("tensor_tensor", O[:, :], O[:, :], Gt[:, :], ALU.mult)
            b.join()
        gated_x("w_rout", 8, feature(O, T), 16, 1, 1, 2)
    tap("retout", X[:, :])
    with ExitStack() as s:
        hm = sb(DT * T, s, "modulated")
        modulate(X[:, :], hm[:, :], 1, 1, "norm_ffn", 3)
        ffn(1, "gu_1", "down_1", hm, T,
            lambda w2, h: (b.join(), gated_x(w2, 16, feature(h, T), 11, 1, 1, 5, halves=2)))
    b.wait("sp", *b.all())
    done = load(out, X[:, :], "out")
    b.wait("sp", done)


def slabs(w, kt, groups):
    t = w.reshape(-1, P, w.shape[1] // P, P)
    out = []
    for g in groups:
        for lo in range(0, t.shape[0], kt):
            out.append(t[lo:lo + kt][:, :, list(g), :].transpose(1, 0, 2, 3).reshape(P, -1))
    return np.ascontiguousarray(np.stack(out))


def arrange(inp):
    def feat(x):
        return np.ascontiguousarray(x.T.reshape(DT, P, -1).transpose(1, 0, 2).reshape(P, -1))

    def col(v):
        return np.asarray(v).reshape(-1, P).T
    two = lambda n, o=0: [(o + 2 * i, o + 2 * i + 1) for i in range(n)]
    one = lambda n: [(i,) for i in range(n)]
    pair = lambda n: [(i, n + i) for i in range(n)]
    d = {"x": feat(inp["x"][0]), "mem": feat(inp["mem"][0]), "ctx": feat(inp["ctx_2"][0])}
    w = inp["even_w_in"][0]
    main = np.concatenate([w[:, :2560], w[:, 2576:]], axis=1)
    d["w_in"] = slabs(main, 8, two(23))
    d["w_dt"] = np.ascontiguousarray(w[:, 2560:2576].reshape(DT, P, 16).transpose(1, 0, 2).reshape(P, -1))
    d["lora"] = np.concatenate([np.concatenate([inp["rwkv_w2"][0], inp["rwkv_a2"][0]], axis=0), inp["rwkv_g2"][0]], axis=1)
    d["w_mix0"] = slabs(inp["even_w_out"][0], 16, one(8))
    kv = inp["xa_wkv"]
    d["w_memk"] = np.concatenate([slabs(kv[l][:, :D], 8, two(4)) for l in range(2)])
    d["w_memv"] = np.concatenate([slabs(kv[l][:, D:], 8, two(4)) for l in range(2)])
    d["w_ada"] = np.concatenate([slabs(inp["ada_w_2"][l], 8, two(24)) for l in range(2)])
    for l in range(2):
        d[f"w_xq{l}"] = slabs(inp["xa_wq"][l], 8, two(4))
        d[f"w_xo{l}"] = slabs(inp["xa_wo"][l], 8, two(4))
        d[f"w13_{l}"] = slabs(inp["ffn_w13"][l], 8, pair(FFN_T))
        d[f"w2_{l}"] = slabs(inp["ffn_w2"][l], 11, one(8))
        d[f"gu_{l}"] = slabs(inp["ffn_w_gu_2"][l], 8, pair(FFN_T))
        d[f"down_{l}"] = slabs(inp["ffn_w_down_2"][l], 11, one(8))
    d["w_qkv"] = slabs(inp["odd_w_qkv"][0], 8, two(12))
    d["w_aout"] = slabs(inp["odd_w_out"][0], 8, two(4))
    d["w_c1"] = slabs(inp["conv_w1_2"][0], 8, pair(8))
    d["w_c2"] = slabs(inp["conv_w2_2"][0], 8, two(4))
    d["w_ret"] = slabs(inp["ret_w_in_2"][0], 8, two(24))
    d["w_rout"] = slabs(inp["ret_w_out_2"][0], 16, one(8))
    heads = np.zeros((P, 2), np.float32)
    heads[:NH, 0], heads[:NH, 1] = inp["ssd_dt_bias"][0], inp["ssd_a_log"][0]
    cond = np.stack([col(inp["c_ctx_2"]), col(inp["c_2"][0])], axis=2).reshape(P, -1)
    decay = np.broadcast_to(np.concatenate([inp["ret_decay_f_2"][0], inp["ret_decay_b_2"][0]]), (P, 8))
    v = {
        "conv_w": np.concatenate([col(inp["ssd_conv_w"][0][k]) for k in range(4)], axis=1),
        "conv_b": col(inp["ssd_conv_b"][0]), "ssd_d": col(np.repeat(inp["ssd_d"][0], HD)),
        "ssd_g": col(inp["ssd_norm_g"][0]), "mu": col(inp["rwkv_mu"][0]), "w0": col(inp["rwkv_w0"][0]),
        "a0": col(inp["rwkv_a0"][0]), "k_k": col(inp["rwkv_k_k"][0]), "k_a": col(inp["rwkv_k_a"][0]),
        "r_k": col(inp["rwkv_r_k"][0].reshape(-1)), "lnx_g": col(inp["rwkv_lnx_g"][0]),
        "lnx_b": col(inp["rwkv_lnx_b"][0]), "mix_g": col(inp["ln_mix_g"]), "mix_b": col(inp["ln_mix_b"]),
        "xa_g": col(inp["ln_xa_g"]), "xa_b": col(inp["ln_xa_b"]), "ffn_g": col(inp["ln_ffn_g"]),
        "ffn_b": col(inp["ln_ffn_b"]), "cond": cond, "ada_b": col(inp["ada_b_2"]),
        "norm_mix": col(inp["norm_mix_2"]), "norm_ffn": col(inp["norm_ffn_2"]), "conv_b1": col(inp["conv_b1_2"]),
        "conv_dw": np.concatenate([col(inp["conv_dw_2"][0][k]) for k in range(CONV_W)], axis=1),
        "conv_dw_b": col(inp["conv_dw_b_2"]), "conv_norm": col(inp["conv_norm_2"]), "heads": heads, "decay": decay,
    }
    d["vectors"] = np.concatenate([v[n] for n, _ in VECTORS], axis=1)
    assert d["vectors"].shape[1] == NVEC
    d["consts"] = shape_constants()
    d["causal"] = attention_masks()
    d["dist"], d["rope"] = retention_constants()
    return {k: np.ascontiguousarray(a, dtype=np.float32) if a.dtype == np.float32 else a for k, a in d.items()}


def build(nc, arrays, tap_shapes=None):
    dram = {n: nc.dram_tensor(f"in_{n}", a.shape, F32, kind="ExternalInput").ap() for n, a in arrays.items()}
    out = nc.dram_tensor("out", (P, DT * T), F32, kind="ExternalOutput").ap()
    taps = {n: nc.dram_tensor(f"tap_{n}", s, F32, kind="ExternalOutput").ap() for n, s in (tap_shapes or {}).items()}
    program(nc, dram, out, taps)


def kernel(**inputs):
    import concourse.bacc as _bacc
    from concourse.bass_utils import run_bass_kernel_spmd as _run

    arrays = arrange({k: np.asarray(v) for k, v in inputs.items()})
    nc = _bacc.Bacc("TRN2", target_bir_lowering=False, num_devices=1)
    build(nc, arrays)
    r = _run(nc, [{f"in_{n}": a for n, a in arrays.items()}], core_ids=[0])
    y = r.results[0]["out"]
    return y.reshape(P, DT, T).transpose(1, 0, 2).reshape(D, T).T.reshape(1, T, D)
```

```python
import math
from contextlib import ExitStack, contextmanager

import numpy as np

import concourse.bass as bass
from concourse import mybir

F32 = mybir.dt.float32
F32R = mybir.dt.float32r
ACT = mybir.ActivationFunctionType
ALU = mybir.AluOpType
AX = mybir.AxisListType

P = 128
D = 1024
DT = D // P
T = 256
C = 128
NC = T // C
HD = 64
NH = D // HD
XBC_T = 12
RW_T = 26
FFN_T = 22
SLOT = 16 * P
RING = 4
PIECE = 8 * P
PIECES = 2
ALPHA = 4.0 ** 0.25
EPS5, EPS6, LNX_EPS = 1e-5, 1e-6, 64e-5
KAPPA = math.exp(-0.5)
CONV_W = 31
PAD = CONV_W // 2
NEG = -1e30

VECTORS = [
    ("conv_w", 4 * XBC_T), ("conv_b", XBC_T), ("ssd_d", 8), ("ssd_g", 8), ("mu", RW_T), ("w0", 8),
    ("a0", 8), ("k_k", 8), ("k_a", 8), ("r_k", 8), ("lnx_g", 8), ("lnx_b", 8),
    ("mix_g", 16), ("mix_b", 16), ("xa_g", 16), ("xa_b", 16), ("ffn_g", 16), ("ffn_b", 16),
    ("cond", 16), ("ada_b", 96), ("norm_mix", 16), ("norm_ffn", 16), ("conv_b1", 16),
    ("conv_dw", CONV_W * 8), ("conv_dw_b", 8), ("conv_norm", 8), ("heads", 2), ("decay", 8),
]
VOFF, _o = {}, 0
for _n, _c in VECTORS:
    VOFF[_n] = (_o, _c)
    _o += _c
NVEC = _o
CONSTS = ["ident", "ones", "ones_model", "ones_half", "head_sum", "head_mean", "upper_strict", "upper",
          "low0"] + [f"lev{k}" for k in range(7)] + ["swap", "cond_sum"]
COFF = {n: i * P for i, n in enumerate(CONSTS)}


def shape_constants():
    s, t = np.arange(P)[:, None], np.arange(P)[None, :]
    out = {"ident": s == t, "ones": np.ones((P, P)), "ones_model": np.full((P, P), 1 / D),
           "ones_half": np.full((P, P), 1 / 512), "head_sum": s // HD == t // HD,
           "head_mean": (s // HD == t // HD) / HD, "upper_strict": s < t, "upper": s <= t}
    for k in range(7):
        b = 1 << k
        lev = (s // (2 * b) == t // (2 * b)) & (s % (2 * b) < b) & (t % (2 * b) >= b)
        out[f"lev{k}"] = lev
        if k == 0:
            out["low0"] = lev.T
    out["cond_sum"] = (s % 2 == t) & (s < 4)
    out["swap"] = np.where(s == t + 64, -1.0, 0.0) + np.where(t == s + 64, 1.0, 0.0)
    return np.concatenate([out[n].astype(np.float32) for n in CONSTS], axis=1)


def attention_masks():
    q = np.arange(P)[:, None, None] + P * np.arange(2)[None, :, None]
    k = np.arange(T)[None, None, :]
    return np.where(k <= q, 0.0, NEG).astype(np.float32).reshape(P, 2 * T)


def retention_constants():
    m, t = np.arange(T)[:, None], np.arange(T)[None, :]
    fwd = np.concatenate([t + T - m, np.abs(t - m)])
    bwd = np.concatenate([T - t + m, np.abs(t - m)])
    seen_f, seen_b = (m <= t), (m >= t)

    def tiles(a):
        return a.reshape(-1, P, T).transpose(1, 0, 2).reshape(P, -1)
    dist = np.concatenate([tiles(fwd), tiles(bwd), tiles(seen_f), tiles(seen_b)], axis=1)
    inv = (np.float32(10000.0) ** (-np.arange(64, dtype=np.float32) / np.float32(64))).astype(np.float32)
    tok = np.arange(T)
    tabs = []
    for pos in (tok // 64, tok % 64):
        ang = (pos[None, :].astype(np.float32) * inv[:, None]).astype(np.float32)
        ang = np.concatenate([ang, ang], axis=0)
        tabs += [np.cos(ang), np.sin(ang)]
    order = [tabs[0], tabs[2], tabs[1], tabs[3]]
    return dist.astype(np.float32), np.concatenate(order, axis=1).astype(np.float32)


class Tok:

    def __init__(self, clock, n, loop):
        self.clock, self.n, self.loop = clock, n, loop


class Count:

    def __init__(self, sem, inc=1):
        self.sem, self.inc, self.n, self.loop = sem, inc, 0, None

    def mark(self, ins):
        ins.then_inc(self.sem, self.inc)
        self.n += self.inc
        return Tok(self, self.n, self.loop)

    def here(self):
        return Tok(self, self.n, self.loop)

    def value(self, n):
        return Tok(self, n, self.loop)


class Matrix:

    def __init__(self, name, slabs, kt=8, mo=2, row0=0):
        self.name, self.slabs, self.kt, self.mo, self.row0 = name, slabs, kt, mo, row0
        self.size = kt * mo * P
        self.half = (kt * mo + 1) // 2

    def words(self, part):
        return (0, self.half * P) if part == 0 else (self.half * P, self.size)


class Loop:
    def __init__(self, index, count, per):
        self.index, self.count, self.per, self.open = index, count, per, True


SIDE = 12
M_IN_Z, M_IN_XBC, M_IN_RW = Matrix("w_in", 4), Matrix("w_in", 6, row0=4), Matrix("w_in", 13, row0=10)
M_ADA = Matrix("w_ada", 48)
M_MIX0 = Matrix("w_mix0", 8, 16, 1)
M_KV, M_XQ, M_XO = ([Matrix(f"{w}{l}", n) for l in range(2)] for w, n in (("w_kv", 8), ("w_xq", 4), ("w_xo", 4)))
M_W13 = [Matrix(f"w13_{l}", 22) for l in range(2)]
M_W2 = [Matrix(f"w2_{l}", 16, 11, 1) for l in range(2)]
M_Q, M_K, M_V = (Matrix("w_qkv", 4, row0=4 * i) for i in range(3))
M_AOUT = Matrix("w_aout", 4)
M_C1, M_C2 = Matrix("w_c1", 8), Matrix("w_c2", 4)
M_GU0 = [Matrix("gu_0", 11, row0=11 * i) for i in range(2)]
M_DOWN0 = [Matrix("down_0", 8, 11, 1, row0=8 * i) for i in range(2)]
M_RQ, M_RK, M_RV, M_RG = (Matrix("w_ret", n, row0=r) for n, r in ((4, 0), (4, 4), (8, 8), (8, 16)))
M_ROUT = Matrix("w_rout", 8, 16, 1)
M_GU1, M_DOWN1 = Matrix("gu_1", 22), Matrix("down_1", 16, 11, 1)


class Build:
    def __init__(self, nc, ctx):
        self.nc, self.ctx = nc, ctx
        self.eng = {"pe": nc.tensor, "act": nc.scalar, "dve": nc.vector, "pool": nc.gpsimd, "sp": nc.sync}
        self.c = {e: Count(self.sem("done_" + e)) for e in ("pe", "act", "dve", "pool")}
        self.loads = Count(self.sem("small_loads"), 16)
        self.slot_full = [Count(self.sem(f"slot_full{i}"), 16) for i in range(RING)]
        self.piece_hi = Count(self.sem("piece_hi"))
        self.piece_lo = Count(self.sem("piece_lo"))
        self.piece_done = Count(self.sem("piece_done"))
        self.slab_out = Count(self.sem("slab_out"))
        self.counts = list(self.c.values()) + [self.loads, self.slab_out, self.piece_hi, self.piece_lo,
                                               self.piece_done] + self.slot_full
        self.seen = {}

    def sem(self, name):
        return self.ctx.enter_context(self.nc.semaphore(name))

    def wait(self, e, *toks):
        for t in toks:
            if t is None:
                continue
            if isinstance(t, (list, tuple)):
                self.wait(e, *t)
                continue
            key = (e, t.clock)
            lp = t.loop
            if lp is not None and not lp.open:
                t, lp = Tok(t.clock, t.n + (lp.count - 1) * lp.per.get(t.clock, 0), None), None
            if lp is None:
                if t.n <= 0 or self.seen.get((key, None), 0) >= t.n:
                    continue
                self.seen[(key, None)] = t.n
                self.eng[e].wait_ge(t.clock.sem, t.n)
            else:
                if self.seen.get((key, lp), -1 << 30) >= t.n:
                    continue
                self.seen[(key, lp)] = t.n
                per = lp.per.get(t.clock, 0)
                assert t.n >= 1, "a wait that may be negative"
                self.eng[e].wait_ge(t.clock.sem, lp.index * per + t.n if per else t.n)

    def run(self, e, fn, *a, after=(), chain=True, **kw):
        self.wait(e, *(after if isinstance(after, (list, tuple)) else (after,)))
        if chain:
            self.wait(e, self.c[e].here())
        return self.c[e].mark(fn(*a, **kw))

    def V(self, op, *a, **kw):
        return self.run("dve", OPS[op](self.nc.vector), *a, **kw)

    def G(self, op, *a, **kw):
        return self.run("pool", OPS[op](self.nc.gpsimd), *a, **kw)

    def A(self, out, in_, func, **kw):
        return self.run("act", self.nc.scalar.activation, out, in_, func, **kw)

    def mm(self, out, lhsT, rhs, start, stop):
        return self.nc.tensor.matmul(out, lhsT, rhs, start=start, stop=stop)

    def pe(self, ins):
        return self.c["pe"].mark(ins)

    def fetched(self):
        return sum(c.n for c in self.slot_full) // 16

    def before(self, e):
        c = self.c[e]
        return Tok(c, self.start[c], c.loop)

    def all(self):
        return [c.here() for c in self.c.values()] + [self.slab_out.here(), self.loads.here(), self.piece_done.here()]

    def join(self, *engines):
        for e in engines or ("pe", "act", "dve", "pool"):
            self.wait(e, *self.all())

    @contextmanager
    def loop(self, count, per):
        start = {c: c.n for c in self.counts}
        with self.nc.Fori(0, count) as i:
            lp = Loop(i, count, per)
            for c in self.counts:
                c.loop = lp
            self.start = start
            yield i
        lp.open = False
        bad = {c.sem.name: (c.n - start[c], per.get(c, 0)) for c in self.counts if c.n - start[c] != per.get(c, 0)}
        assert not bad, bad
        for c in self.counts:
            c.n = start[c] + count * per.get(c, 0)
            c.loop = None


OPS = {
    "tensor_tensor": lambda e: e.tensor_tensor, "tensor_scalar": lambda e: e.tensor_scalar,
    "scalar_tensor_tensor": lambda e: e.scalar_tensor_tensor, "tensor_copy": lambda e: e.tensor_copy,
    "tensor_reduce": lambda e: e.tensor_reduce, "memset": lambda e: e.memset,
    "reciprocal": lambda e: e.reciprocal, "scan": lambda e: e.tensor_tensor_scan,
}


def cols(ap, n):
    return ap.rearrange("p (t o) -> p t o", o=1).broadcast_to([ap.shape[0], ap.shape[1], n])


def rows(ap, t):
    return ap.rearrange("p (o n) -> p o n", o=1).broadcast_to([ap.shape[0], t, ap.shape[1]])


def tiles(ap, n):
    return ap.rearrange("p (t n) -> p t n", n=n)


def program(nc, dram, out, taps=None):
    with ExitStack() as ctx:
        _program(Build(nc, ctx), dram, out, taps or {})


def _program(b, dram, out, taps):
    nc = b.nc
    keep = b.ctx
    names = [0]
    V, G, A, mm = b.V, b.G, b.A, b.mm

    def sb(cols_, stack=keep, name="t", dt=F32):
        names[0] += 1
        return stack.enter_context(nc.sbuf_tensor(f"{name}_{names[0]}", [P, cols_], dt))

    class Split:

        def __init__(self, words, stack, name="x"):
            self.hi, self.lo = sb(words, stack, name + "_hi", F32R), sb(words, stack, name + "_lo", F32R)

        def __getitem__(self, sl):
            return self.hi[:, sl], self.lo[:, sl]

        def set(self, src, lo=0, after=()):
            w = src.shape[-1]
            t = A(self.hi[:, lo:lo + w], src, ACT.Copy, after=after, chain=False)
            return V("tensor_tensor", self.lo[:, lo:lo + w], src, self.hi[:, lo:lo + w].bitcast(F32),
                     ALU.subtract, after=[t], chain=False)


    vec = sb(NVEC, name="vectors")
    con = sb(P * len(CONSTS), name="constants")
    X = sb(DT * T, name="x")
    ring = [sb(SLOT, name=f"ring{i}") for i in range(RING)]
    pieces = [Split(PIECE, keep, f"piece{i}") for i in range(PIECES)]
    mods = sb(2 * 48 * 2, name="mods")
    psum = keep.enter_context(nc.psum_tensor("psum", [P, 8, 512], F32))

    def vv(name, lo=0, n=None):
        o, c = VOFF[name]
        return vec[:, o + lo:o + (c if n is None else lo + n)]

    def cc(name):
        return con[:, COFF[name]:COFF[name] + P]

    def load(dst, src, name=None):
        count = b.loads
        if name:
            count = Count(b.sem("load_" + name), 16)
            b.counts.append(count)
        return count.mark((nc.scalar if name else nc.sync).dma_start(dst, src))

    def tap(name, ap):
        if name in taps:
            b.wait("sp", *b.all())
            b.wait("sp", load(taps[name], ap))
            b.join()

    load(vec[:, :], dram["vectors"])
    load(con[:, :], dram["consts"])
    load(X[:, :], dram["x"])

    def fetch(m, j):
        slot = b.fetched() % RING
        src = dram[m.name][m.row0 + j, :, :] if isinstance(j, int) else \
            dram[m.name][bass.ds(j + m.row0, 1), :, :].rearrange("s p n -> p (s n)")
        return b.slot_full[slot].mark(nc.sync.dma_start(ring[slot][:, 0:m.size], src))

    def round_piece(m, part):
        lo, hi = m.words(part)
        h = pieces[b.piece_hi.n % PIECES]
        return b.piece_hi.mark(nc.scalar.activation(h.hi[:, 0:hi - lo], ring[(b.fetched() - 1) % RING][:, lo:hi], ACT.Copy))

    def rest_of_piece(m, part):
        lo, hi = m.words(part)
        h = pieces[b.piece_lo.n % PIECES]
        return b.piece_lo.mark(nc.vector.tensor_tensor(
            h.lo[:, 0:hi - lo], ring[(b.fetched() - 1) % RING][:, lo:hi], h.hi[:, 0:hi - lo].bitcast(F32), ALU.subtract))

    def mm3(out, a, c, start, stop):
        for q, (l, r) in enumerate(((a[0], c[0]), (a[0], c[1]), (a[1], c[0]))):
            ins = mm(out, l, r, start and q == 0, stop and q == 2)
        return ins

    def multiply(m, x, n, part, first_bank, k0=0, start=True, stop=True):
        h = pieces[b.piece_done.n % PIECES]
        for t in range(m.half) if part == 0 else range(m.half, m.kt * m.mo):
            mt, k = t // m.kt, t % m.kt
            at_ = mt * n
            out_ = psum[:, first_bank + at_ // 512, at_ % 512:at_ % 512 + n]
            w = h[slice((t - m.half * part) * P, (t - m.half * part + 1) * P)]
            ins = mm3(out_, w, x(k + k0), start and k == 0, stop and k == m.kt - 1)
        return b.piece_done.mark(ins)

    def multiply_tokens(m, x, n, part, first_bank, **kw):
        h = pieces[b.piece_done.n % PIECES]
        for tt in range(n // P):
            out_ = psum[:, first_bank + tt // 2, (tt % 2) * 256:(tt % 2) * 256 + 256]
            for k in range(4):
                xk = tuple(a[:, tt * P:tt * P + P] for a in x(4 * part + k))
                ins = mm3(out_, xk, h[slice(k * 256, k * 256 + 256)], part == 0 and k == 0 and tt % 2 == 0,
                          part == 1 and k == 3 and tt % 2 == 1)
        return b.piece_done.mark(ins)

    def multiply_kv(m, x, n, part, first_bank, **kw):
        if part == 0:
            return multiply(m, x, n, 0, first_bank, stop=False)
        h = pieces[b.piece_done.n % PIECES]
        for tt in range(T // P):
            for k in range(DT):
                xk = tuple(a[:, tt * P:tt * P + P] for a in x(k))
                ins = mm3(psum[:, first_bank, T + tt * P:T + tt * P + P], xk, h[slice(k * P, k * P + P)],
                          False, tt == T // P - 1 and k == DT - 1)
        return b.piece_done.mark(ins)

    def multiply_conditions(part, bk):
        h = pieces[b.piece_done.n % PIECES]
        for k in range(4):
            c4 = cond4[:, 4 * (4 * part + k):4 * (4 * part + k) + 4]
            for q, w in enumerate((h.hi, h.lo)):
                ins = mm(psum[0:4, bk, 0:256], c4, w[:, k * 256:k * 256 + 256],
                         part == 0 and k == 0 and q == 0, part == 1 and k == 3 and q == 1)
        return b.piece_done.mark(ins)

    def slot_free():
        return b.piece_lo.value(2 * (b.fetched() - RING + 1))

    def piece_free():
        return b.piece_done.value(b.piece_hi.n - PIECES + 1)

    def piece_ready():
        return b.piece_lo.value(b.piece_done.n + 1)

    def leave(e, fn, *a, after=(), chain=False, **kw):
        b.wait(e, *(after if isinstance(after, (list, tuple)) else (after,)))
        if chain:
            b.wait(e, b.c[e].here())
        ins = fn(*a, **kw)
        ins.then_inc(b.slab_out.sem, b.slabs_a_result)
        b.slab_out.n += b.slabs_a_result
        return b.slab_out.here()

    b.slabs_a_result = 1
    b.prepared = None

    def prepare_first(m):
        b.wait("sp", slot_free())
        full = fetch(m, 0)
        for part in range(2):
            b.wait("act", full, piece_free())
            b.wait("dve", round_piece(m, part))
            rest_of_piece(m, part)
        b.prepared = m

    def linear(m, x, n, evac, then=None, product=multiply, halves=1, mid=None):
        nb = max(1, (m.mo * n + 511) // 512)
        depth = (4 if halves == 1 else 2) // nb
        base = b.slab_out.n
        b.wait("pe", b.slab_out.here())
        b.slabs_a_result = halves
        if b.prepared is None:
            prepare_first(m)
        assert b.prepared is m, (b.prepared.name, m.name)

        def turn(j, jo, u, nxt, k):
            bk = (b.slab_out.n - base) // halves % depth * nb
            kpart = u % halves
            for part in range(2):
                b.wait("pe", piece_ready())
                if part == 0 and kpart == 0:
                    b.wait("pe", b.slab_out.value(b.slab_out.n - (depth - 1) * halves))
                done = product(m, x, n, part, bk, k0=kpart * m.kt, start=kpart == 0, stop=kpart == halves - 1)
                if nxt is None:
                    continue
                if part == 0:
                    b.wait("sp", slot_free())
                    full = fetch(nxt, k)
                b.wait("act", full, piece_free())
                b.wait("dve", round_piece(nxt, part))
                rest_of_piece(nxt, part)
            if kpart == halves - 1:
                res = psum[:, bk, 0:m.mo * n] if nb == 1 else psum[:, bk:bk + nb, :].rearrange("p b n -> p (b n)")
                evac(jo, res, done)

        turns = (m.slabs - 1) // RING
        j0 = 0
        if turns > 1:
            per = {b.piece_hi: 2 * RING, b.piece_lo: 2 * RING, b.piece_done: 2 * RING, b.slab_out: RING}
            per.update({c: 16 for c in b.slot_full})
            for e, k in (mid or {}).items():
                per[b.c[e]] = k * RING // halves
            with b.loop(turns, per) as i:
                for u in range(RING):
                    j = i * RING + u
                    turn(j, j if halves == 1 else i * (RING // halves) + u // halves, u, m, i * RING + (u + 1))
            j0 = turns * RING
        for j in range(j0, m.slabs):
            turn(j, j // halves, j, *((m, j + 1) if j + 1 < m.slabs else (then, 0)))
        b.prepared = then
        b.slabs_a_result = 1
        return b.slab_out.here()

    def at(ap, j, width):
        return ap[:, bass.ds(j * width, width)]

    def bank(i, lo=0, n=512):
        return psum[:, i, lo:lo + n]

    def mean_over(src, n, matrix, nt, group, b0=4):
        outs = []
        for gidx in range(nt // group):
            off = gidx * n
            o = psum[:, b0 + off // 512, off % 512:off % 512 + n]
            for k in range(group):
                t = gidx * group + k
                ins = mm(o, cc(matrix), src[:, t * n:t * n + n], k == 0, k == group - 1)
            outs.append(o)
        return b.pe(ins), outs

    def rsqrt(dst, src, eps, tmp, after=()):
        V("tensor_scalar", tmp, src, eps, None, ALU.add, after=after)
        t = A(tmp, tmp, ACT.Sqrt, after=[b.c["dve"].here()])
        return V("reciprocal", dst, tmp, after=[t])

    def layer_norm(src, dst, n, g, beta, eps, stack):
        with ExitStack() as s:
            sq, rs = sb(DT * n, s), sb(2 * n, s)
            b.join()
            t, (mean,) = mean_over(src, n, "ones_model", DT, DT, 4)
            V("tensor_tensor", tiles(src, n), tiles(src, n), rows(mean, DT), ALU.subtract, after=[t])
            t = A(sq[:, :], src, ACT.Square, after=[b.c["dve"].here()])
            b.wait("pe", t)
            t, (var,) = mean_over(sq, n, "ones_model", DT, DT, 5)
            rsqrt(rs[:, n:2 * n], var, eps, rs[:, 0:n], after=[t])
            V("tensor_tensor", tiles(src, n), tiles(src, n), rows(rs[:, n:2 * n], DT), ALU.mult)
            if beta is None:
                V("tensor_tensor", tiles(dst, n), tiles(src, n), cols(g, n), ALU.mult)
            else:
                V("tensor_tensor", tiles(src, n), tiles(src, n), cols(g, n), ALU.mult)
                V("tensor_tensor", tiles(dst, n), tiles(src, n), cols(beta, n), ALU.add)
            b.join()

    def residual_linear(m, x, then, halves=1):
        b.join()
        width = m.mo * T

        def evac(j, ap, tok):
            xs = at(X, j, width)
            leave("dve", nc.vector.scalar_tensor_tensor, xs, xs, ALPHA, ap, ALU.mult, ALU.add, after=[tok])
        linear(m, x, T, evac, then, halves=halves)
        b.join()

    def copy_out(dst, width=512, e="act"):
        def evac(j, ap, tok):
            if e == "act":
                leave("act", nc.scalar.activation, at(dst, j, width), ap, ACT.Copy, after=[tok])
            else:
                leave("dve", nc.vector.tensor_copy, at(dst, j, width), ap, after=[tok])
        return evac

    def copy_tokens(dst, nt, total):
        def evac(j, ap, tok):
            d = dst.rearrange("p (t c) -> p t c", c=total)[:, :, bass.ds(j * 256, 256)]
            leave("act", nc.scalar.activation, d, ap.rearrange("p (t c) -> p t c", c=256), ACT.Copy, after=[tok])
        return evac

    def feature(x, n, lo=0, width=None):
        return lambda k: x[slice(k * n + lo, k * n + lo + (width or n))]

    def softmax_rows(S, n_rows, width, scale, mx, sm, after):
        V("tensor_reduce", mx, S, AX.X, ALU.max, after=after)
        t = V("tensor_scalar", mx, mx, -scale, None, ALU.mult)
        for r in range(n_rows):
            t2 = A(S[:, r, :], S[:, r, :], ACT.Exp, bias=mx[:, r:r + 1], scale=scale,
                   accum_out=sm[:, r:r + 1], after=[t], chain=False)
        V("reciprocal", sm, sm, after=[t2])
        return V("tensor_tensor", S, S, cols(sm, width), ALU.mult)

    def ffn(w13s, xin, n, w2s, down, then):
        for w13, w2, nxt in zip(w13s, w2s, [*w13s[1:], then]):
            tn = w13.slabs
            with ExitStack() as s:
                h = Split(tn * n, s, "hidden")
                gate, prod = sb(2 * n, s, "gate"), sb(2 * n, s, "prod")

                def evac(j, ap, tok):
                    ph = b.piece_done.n // 2 % 2
                    gt, pr = gate[:, ph * n:ph * n + n], prod[:, ph * n:ph * n + n]
                    t = A(gt, ap[:, 0:n], ACT.Silu, chain=False,
                          after=[tok, Tok(b.slab_out, b.slab_out.n - 1, b.slab_out.loop)])
                    t = leave("dve", nc.vector.tensor_tensor, pr, gt, ap[:, n:2 * n], ALU.mult, after=[t])
                    t = A(at(h.hi, j, n), pr, ACT.Copy, after=[t], chain=False)
                    V("tensor_tensor", at(h.lo, j, n), pr, at(h.hi, j, n).bitcast(F32), ALU.subtract,
                      after=[t], chain=False)
                linear(w13, feature(xin, n), n, evac, w2, mid={"act": 2, "dve": 1})
                b.join()
                down(w2, h, nxt)

    cond4 = sb(DT * 4, name="cond_rows", dt=F32R)
    ada_rows = sb(2 * 256, name="ada_rows")
    sel = con[0:4, COFF["cond_sum"]:COFF["cond_sum"] + 2]

    def ev_ada(j, ap, tok):
        bk = 7
        ph = b.piece_done.n // 2 % 2
        row = ada_rows[0:4, ph * 256:ph * 256 + 256]
        t = A(row, ap[0:4, :], ACT.Copy, after=[tok], chain=False)
        b.wait("pe", t)
        for m in range(2):
            ins = mm(bank(bk, 256 + 2 * m, 2), row[:, m * P:m * P + P], sel, True, True)
        bias = cols(vv("ada_b")[:, bass.ds(j * 2, 2)], 2)
        leave("dve", nc.vector.tensor_tensor, tiles(at(mods, j, 4), 2), tiles(bank(bk, 256, 4), 2), bias,
              ALU.add, after=[b.pe(ins)])

    FB = ExitStack()
    with ExitStack() as L0:
        mix = sb(DT * T, L0, "ssd_out")
        scond = sb(16, L0, "silu_cond")
        wdt = sb(DT * 16, L0, "w_dt")
        load(wdt[:, :], dram["w_dt"])
        g2 = sb(D, L0, "g2")
        load(g2[:, :], dram["g2"])
        rs_ = sb(RW_T * T, L0, "shifted")
        with ExitStack() as S1:
            Z = sb(DT * T, S1, "z")
            XBC = sb(XBC_T * (T + 3), S1, "xbc")
            RW = S1.enter_context(ExitStack())
            xs_ = Split(DT * T, RW)
            rw = sb(RW_T * (T + 1), RW, "rw")
            b.join()
            zero = V("memset", tiles(XBC[:, :], T + 3)[:, :, 0:3], 0.0)
            zero = V("memset", tiles(rw[:, :], T + 1)[:, :, 0:1], 0.0)
            t = A(scond[:, :], vv("cond"), ACT.Silu)
            c4 = tiles(cond4[:, :], 4)
            t = A(c4[:, :, 0:2], tiles(scond[:, :], 2), ACT.Copy, after=[t])
            V("tensor_tensor", c4[:, :, 2:4], tiles(scond[:, :], 2), c4[:, :, 0:2].bitcast(F32), ALU.subtract, after=[t])
            xs_.set(X[:, :])
            b.join()

            for k in range(DT):
                ins = mm(psum[0:16, 4, 0:T], wdt[:, k * 16:k * 16 + 16], X[:, k * T:k * T + T], k == 0, k == DT - 1)
            t_dt = b.pe(ins)

            def ev_z(j, ap, tok):
                leave("act", nc.scalar.activation, at(Z, j, 512), ap, ACT.Silu, after=[tok])

            def padded(dst, pad):
                def evac(j, ap, tok):
                    d = tiles(dst[:, :], T + pad)[:, bass.ds(j * 2, 2), pad:T + pad]
                    leave("act", nc.scalar.activation, d, tiles(ap, T), ACT.Copy, after=[tok])
                return evac
            b.wait("act", zero)
            linear(M_IN_Z, feature(xs_, T), T, ev_z, then=M_IN_XBC)
            linear(M_IN_XBC, feature(xs_, T), T, padded(XBC, 3), then=M_IN_RW)
            linear(M_IN_RW, feature(xs_, T), T, padded(rw, 1))
            b.join()
            cur, prv = tiles(rw[:, :], T + 1)[:, :, 1:T + 1], tiles(rw[:, :], T + 1)[:, :, 0:T]
            R3 = tiles(rs_[:, :], T)
            V("tensor_tensor", R3, prv, cur, ALU.subtract)
            V("tensor_tensor", R3, R3, cols(vv("mu"), T), ALU.mult)
            V("tensor_tensor", R3, R3, cur, ALU.add)
            b.join()
            RW.close()
            tap("z", Z[:, :]), tap("rs", rs_[:, :])

            XC = sb(XBC_T * T, S1, "xc")
            XD_ = sb(2 * D, S1, "x_dt")
            tmp = sb(XBC_T * T, S1, "tmp")
            xc3, tmp3, xb3 = tiles(XC[:, :], T), tiles(tmp[:, :], T), tiles(XBC[:, :], T + 3)
            for w in range(4):
                dst = xc3 if w == 0 else tmp3
                V("tensor_tensor", dst, xb3[:, :, w:w + T], cols(vv("conv_w", w * XBC_T, XBC_T), T), ALU.mult)
                if w:
                    V("tensor_tensor", xc3, xc3, tmp3, ALU.add)
            t = V("tensor_tensor", xc3, xc3, cols(vv("conv_b"), T), ALU.add)
            A(XC[:, :], XC[:, :], ACT.Silu, after=[t])
            sm = sb(5 * T, S1, "dt_work")
            d16 = [sm[0:16, i * T:i * T + T] for i in range(5)]
            heads = vec[0:16, VOFF["heads"][0]:VOFF["heads"][0] + 2]
            V("tensor_scalar", d16[0], psum[0:16, 4, 0:T], heads[:, 0:1], None, ALU.add, after=[t_dt])

            def log1p_exp_neg_abs(x, w1, w2, w3):
                V("tensor_scalar", w1, x, -1.0, None, ALU.mult)
                V("tensor_tensor", w1, w1, x, ALU.min)
                t = A(w1, w1, ACT.Exp, after=[b.c["dve"].here()])
                t = V("tensor_scalar", w2, w1, 1.0, None, ALU.add, after=[t])
                t = A(w3, w2, ACT.Ln, after=[t])
                V("tensor_scalar", w2, w2, -1.0, 1e-30, ALU.add, ALU.max, after=[t])
                V("reciprocal", w2, w2)
                V("tensor_tensor", w2, w2, w1, ALU.mult)
                return V("tensor_tensor", w3, w3, w2, ALU.mult, after=[t])
            log1p_exp_neg_abs(d16[0], d16[1], d16[2], d16[3])
            V("tensor_scalar", d16[0], d16[0], 0.0, None, ALU.max)
            t = V("tensor_tensor", d16[0], d16[0], d16[3], ALU.add)
            an = sb(1, S1, "a_neg")
            t = A(an[0:16, :], heads[:, 1:2], ACT.Exp)
            V("tensor_scalar", d16[1], d16[0], an[0:16, 0:1], -1.0, ALU.mult, ALU.mult, after=[t])
            V("memset", d16[2], 1.0)
            for c in range(NC):
                s_ = slice(c * C, c * C + C)
                V("scan", d16[4][:, s_], d16[2][:, s_], d16[1][:, s_], 0.0, ALU.mult, ALU.add)
            tap("dt", sm[0:16, 0:T]), tap("acum", sm[0:16, 4 * T:5 * T]), tap("xc", XC[:, :])
            YD = mix[:, :]
            V("tensor_tensor", tiles(YD, T), tiles(XC[:, 0:DT * T], T), cols(vv("ssd_d"), T), ALU.mult)
            b.join()
            AE, EA = tmp[:, 0:16 * C], XBC[:, 0:16 * C]
            SEG = sb(16 * C, S1, "seg")
            XDT, XDD = XD_[:, 0:D], tmp[:, 16 * C:16 * C + D]
            CBm, Bt, S0 = sb(2 * C, S1, "cb"), sb(2 * C, S1, "b_tok"), XD_[:, D:2 * D]
            dT, dec = sb(2 * NH, S1, "dt_tok"), sb(NH, S1, "decay")
            one16 = con[0:16, COFF["ones"]:COFF["ones"] + P]
            id16 = con[0:16, COFF["ident"]:COFF["ident"] + 16]
            for c in range(NC):
                s_ = slice(c * C, c * C + C)
                V("tensor_tensor", tiles(AE[0:16, :], C), rows(d16[4][:, s_], NH), cols(id16, C), ALU.mult)
                b.join()
                for q in range(4):
                    mm(bank(q), one16, AE[0:16, q * 512:q * 512 + 512], True, True)
                nc.tensor.transpose(psum[:, 4, 0:16], d16[0][:, s_], id16)
                nc.tensor.transpose(psum[:, 4, 16:32], d16[4][:, s_], id16)
                for g in range(2):
                    mm(bank(5, g * C, C), XC[:, (8 + g) * T + c * C:(8 + g) * T + c * C + C],
                       XC[:, (10 + g) * T + c * C:(10 + g) * T + c * C + C], True, True)
                for k in range(DT):
                    ins = nc.tensor.transpose(psum[:, 6 + k // 4, (k % 4) * P:(k % 4) * P + P],
                                              XC[:, k * T + c * C:k * T + c * C + C], cc("ident"))
                t = b.pe(ins)
                V("tensor_copy", dT[:, :], psum[:, 4, 0:32], after=[t])
                V("tensor_tensor", tiles(CBm[:, :], C), tiles(bank(5, 0, 2 * C), C), rows(cc("upper"), 2), ALU.mult)
                V("tensor_tensor", tiles(XDT[:, :], HD), psum[:, 6:8, :].rearrange("p b (h d) -> p (b h) d", d=HD),
                  cols(dT[:, 0:16], HD), ALU.mult)
                abc = psum[:, 0:4, :].rearrange("p b (h l) -> p (b h) l", l=C)
                V("tensor_tensor", tiles(SEG[:, :], C), abc, cols(dT[:, 16:32], C), ALU.subtract)
                t = V("tensor_scalar", SEG[:, :], SEG[:, :], 0.0, None, ALU.min)
                if c == 0:
                    V("tensor_tensor", dec[:, :], abc[:, :, C - 1], dT[:, 16:32], ALU.subtract)
                    td = V("tensor_scalar", dec[:, :], dec[:, :], 0.0, None, ALU.min)
                    A(dec[:, :], dec[:, :], ACT.Exp, after=[td])
                else:
                    A(EA[:, :], psum[:, 0:4, :].rearrange("p b n -> p (b n)"), ACT.Exp, after=[t])
                t = A(SEG[:, :], SEG[:, :], ACT.Exp, after=[t])
                for g in range(2):
                    w = slice(g * 8 * C, (g + 1) * 8 * C)
                    V("tensor_tensor", tiles(SEG[:, w], C), tiles(SEG[:, w], C),
                      rows(CBm[:, g * C:g * C + C], 8), ALU.mult, after=[t])
                    if c == 1:
                        V("tensor_tensor", tiles(EA[:, w], C), tiles(EA[:, w], C),
                          rows(XC[:, (10 + g) * T + C:(10 + g) * T + 2 * C], 8), ALU.mult)
                if c == 0:
                    V("tensor_tensor", tiles(XDD[:, :], HD), tiles(XDT[:, :], HD), cols(dec[:, :], HD), ALU.mult)
                b.join()
                for pr in range(8):
                    o = bank(pr // 2, (pr % 2) * 256, 256)
                    ins = mm(o, XDT[:, pr * P:pr * P + P], SEG[:, pr * 256:pr * 256 + 256], True, c == 0)
                    if c:
                        ins = mm(o, S0[:, pr * P:pr * P + P], EA[:, pr * 256:pr * 256 + 256], False, True)
                ty = b.pe(ins)
                if c == 0:
                    for g in range(2):
                        ins = nc.tensor.transpose(bank(4, g * P, P), XC[:, (8 + g) * T:(8 + g) * T + C], cc("ident"))
                    t = A(Bt[:, :], bank(4, 0, 256), ACT.Copy, after=[b.pe(ins)])
                    b.wait("pe", t)
                    for g in range(2):
                        ins = mm(bank(5 + g), Bt[:, g * P:g * P + P], XDD[:, g * 512:g * 512 + 512], True, True)
                    A(S0[:, :], psum[:, 5:7, :].rearrange("p b n -> p (b n)"), ACT.Copy, after=[b.pe(ins)])
                for hh in range(2):
                    p_ = slice(64 * hh, 64 * hh + 64)
                    o = tiles(YD, T)[p_, :, s_]
                    y = psum[p_, 0:4, :].rearrange("p b (q e l) -> p (b q) e l", q=2, e=2)[:, :, hh, :]
                    V("tensor_tensor", o, o, y, ALU.add, after=[ty])
                b.join()
            V("tensor_tensor", YD, YD, Z[:, :], ALU.mult)
            tap("yz", YD)
            sq = tmp[:, 0:DT * T]
            t = A(sq, YD, ACT.Square, after=[b.c["dve"].here()])
            b.wait("pe", t)
            t, _ = mean_over(sq, T, "ones_half", DT, 4, 4)
            rsd = sb(4 * T, S1, "rstd")
            rsqrt(rsd[:, 2 * T:], bank(4), EPS5, rsd[:, 0:2 * T], after=[t])
            for g in range(2):
                v = tiles(YD[:, g * 4 * T:(g + 1) * 4 * T], T)
                V("tensor_tensor", v, v, rows(rsd[:, (2 + g) * T:(3 + g) * T], 4), ALU.mult)
            V("tensor_tensor", tiles(YD, T), tiles(YD, T), cols(vv("ssd_g"), T), ALU.mult)
            tap("yssd", YD)
            b.join()

        with ExitStack() as S2:
            N8 = DT * T
            Rr, Kr, Vr = rs_[:, 0:N8], rs_[:, N8:2 * N8], rs_[:, 2 * N8:3 * N8]
            lo, gl = rs_[:, 24 * T:25 * T], rs_[:, 25 * T:26 * T]
            SG, CS, KK, BV = (sb(N8, S2, n) for n in ("sig_w", "cum", "kk", "b_vec"))
            t = A(lo[0:64, :], lo[0:64, :], ACT.Tanh)
            t = A(gl, gl, ACT.Sigmoid)
            b.wait("pe", t)
            w2a2 = KK[:, 0:D]
            b.join()
            b.wait("act", *b.all())
            b.wait("pe", load(w2a2, dram["w2a2"], "w2a2"))
            for half, dst, bias in ((0, SG, "w0"), (1, BV, "a0")):
                p_ = slice(64 * half, 64 * half + 64)
                for k in range(DT):
                    ins = mm(bank(half * 4 + k // 2, (k % 2) * T, T), w2a2[p_, k * P:k * P + P], lo[p_, :], True, True)
                t = b.pe(ins)
                for k in range(DT):
                    A(dst[:, k * T:k * T + T], bank(half * 4 + k // 2, (k % 2) * T, T), ACT.Sigmoid,
                      bias=vv(bias, k, 1), after=[t], chain=False)
            t_sg = b.c["act"].here()
            V("tensor_tensor", tiles(KK[:, :], T), tiles(Kr, T), cols(vv("k_k"), T), ALU.mult, after=[t])
            t = A(CS[:, :], KK[:, :], ACT.Square, after=[b.c["dve"].here()])
            b.wait("pe", t)
            for half in range(2):
                sl = slice(half * 4 * T, (half + 1) * 4 * T)
                t, _ = mean_over(CS[:, sl], T, "head_sum", 4, 1, half * 2)
                src = psum[:, half * 2:half * 2 + 2, :].rearrange("p b n -> p (b n)")
                t = V("tensor_scalar", CS[:, sl], src, 1e-24, None, ALU.max, after=[t])
            t = A(CS[:, :], CS[:, :], ACT.Sqrt, after=[t])
            V("reciprocal", CS[:, :], CS[:, :], after=[t])
            V("tensor_tensor", KK[:, :], KK[:, :], CS[:, :], ALU.mult)
            CS3 = tiles(CS[:, :], T)
            V("tensor_scalar", CS[:, :], BV[:, :], -1.0, None, ALU.add, after=[t_sg])
            V("tensor_tensor", CS3, CS3, cols(vv("k_a"), T), ALU.mult)
            V("scalar_tensor_tensor", Kr, CS[:, :], 1.0, Kr, ALU.add, ALU.mult)
            V("tensor_tensor", BV[:, :], BV[:, :], KK[:, :], ALU.mult)
            on = sb(C, S2, "ones_row")
            G("memset", on[:, :], 1.0)
            b.wait("dve", b.c["pool"].here())
            for q in range(DT * NC):
                V("scan", CS[:, q * C:q * C + C], on[:, :], SG[:, q * C:q * C + C], 0.0, ALU.mult, ALU.add, chain=q == 0)
            edge = sb(2 * DT * NC, S2, "mid")
            q3 = tiles(CS[:, :], C)
            V("tensor_copy", edge[:, 0:16], q3[:, :, C // 2 - 1])
            V("tensor_tensor", q3, q3, cols(edge[:, 0:16], C), ALU.subtract)
            e3 = edge[:, :].rearrange("p (w t c) -> p w t c", w=2, c=2)
            V("tensor_tensor", e3[:, 1, :, 0], q3.rearrange("p (t c) n -> p t c n", c=2)[:, :, 0, C - 1],
              e3[:, 0, :, 1], ALU.add)
            fac = sb(DT, S2, "carry")
            A(fac[:, :], e3[:, 1, :, 0], ACT.Exp, scale=-KAPPA, after=[b.c["dve"].here()])
            tap("kk", KK[:, :]), tap("cs", CS[:, :]), tap("kr", Kr), tap("bv", BV[:, :])

            class Pair:

                def __init__(self, p):
                    self.p = p
                    self.EX, self.DE = sb(T, S2, "exp"), sb(T, S2, "decay")
                    self.AR = sb(2 * 2 * C, S2, "a_r")
                    self.KB = sb(2 * T, S2, "k_b")
                    self.VP = sb(T, S2, "v_pair")
                    self.TR = sb(4 * P, S2, "by_token")
                    self.GB, self.GK = sb(4 * 2 * C, S2, "gram_b"), sb(4 * 2 * C, S2, "gram_k")
                    self.ML = sb(2 * 4 * C, S2, "level")
                    self.XI, self.XT, self.T1 = (sb(4 * C, S2, n) for n in ("inv", "inv_t", "prod"))
                    self.R0, self.SA, self.ST = (self.EX[:, 0:P], self.EX[:, P:2 * P], self.VP[:, 0:P])
                    self.banks = ((0, 5, 6), (4, 1, 2))[p]
                    self.bank_tr = (0, 3)[p]
            pairs = [Pair(0), Pair(1)]
            up2 = con[:, COFF["upper_strict"]:COFF["upper_strict"] + 2 * C]
            b.join()

            grams_out = [None]

            def pair_steps(i, w):
                EX, AR, KB, VP, TR, GB, GK, ML, XI, XT, T1, R0, SA, ST = (
                    w.EX, w.AR, w.KB, w.VP, w.TR, w.GB, w.GK, w.ML, w.XI, w.XT, w.T1, w.R0, w.SA, w.ST)
                L0_, L1_, L2_ = w.banks
                tile = lambda a: a[:, bass.ds(i * (2 * T) + w.p * T, T)]
                ar4 = AR[:, :].rearrange("p (c w n) -> p c w n", c=2, w=2)
                gb4, gk4 = (tiles(g[:, :], C).rearrange("p (q w) n -> p q w n", w=2) for g in (GB, GK))
                old = [b.before(e) for e in ("pe", "act", "dve", "pool")]
                DE = w.DE[:, :]
                cs_i, sg_i = tile(CS), tile(SG)
                t_d = V("tensor_tensor", DE, cs_i, sg_i, ALU.subtract, after=old, chain=False)
                t_e = A(EX[:, :], cs_i, ACT.Exp, scale=KAPPA, after=old, chain=False)
                t_e2 = A(DE, DE, ACT.Exp, scale=-KAPPA, after=[t_e, t_d], chain=False)
                t_r = A(cs_i, cs_i, ACT.Exp, scale=-KAPPA, chain=False)
                t_v = A(VP[:, :], tile(Vr), ACT.Copy, chain=False)
                V("tensor_tensor", KB[:, 0:T], tile(Kr), EX[:, :], ALU.mult, after=[t_e], chain=False)
                V("tensor_tensor", KB[:, T:2 * T], tile(BV), EX[:, :], ALU.mult, chain=False)
                V("tensor_tensor", ar4[:, :, 1, :], tiles(tile(Rr), C), tiles(cs_i, C), ALU.mult, after=[t_r], chain=False)
                t = V("scalar_tensor_tensor", ar4[:, :, 0, :], tiles(tile(KK), C), -1.0, tiles(DE, C),
                      ALU.mult, ALU.mult, after=[t_e2], chain=False)
                yield
                b.wait("pe", t, t_v, grams_out[0])
                for e in range(2):
                    p_ = slice(64 * e, 64 * e + 64)
                    for c in range(NC):
                        mm(bank(1 + e, c * 256, 256), KB[p_, T + c * C:T + c * C + C], AR[p_, c * 256:c * 256 + 256], True, True)
                        ins = mm(bank(3 + e, c * C, C), AR[p_, c * 256:c * 256 + C], KB[p_, T + c * C:T + c * C + C], True, True)
                t_gb = b.pe(ins)
                two = lambda lo: psum[:, lo:lo + 2, :].rearrange("p b (c n) -> p (b c) n", n=256)
                t_m = V("tensor_tensor", tiles(GB[:, :], 256), two(1), rows(up2, 4), ALU.mult, after=[t_gb], chain=False)
                x4, t4 = tiles(XI[:, :], C), tiles(XT[:, :], C)
                for e in range(2):
                    t_i1 = V("tensor_tensor", tiles(XI[:, e * 2 * C:(e + 1) * 2 * C], C), tiles(psum[:, 3 + e, 0:2 * C], C),
                             rows(cc("low0"), 2), ALU.mult, chain=False)
                t_l = G("tensor_tensor", tiles(ML[:, 4 * C:], C), gb4[:, :, 0, :], rows(cc("lev1"), 4), ALU.mult,
                        after=[t_m], chain=False)
                yield
                b.wait("pe", t_i1 if w.p else t_m)
                for q, src in enumerate((VP[:, 0:C], VP[:, C:T], KB[:, 0:C], KB[:, T:T + C])):
                    ins = nc.tensor.transpose(bank(w.bank_tr, q * P, P), src, cc("ident"))
                t_tr = b.pe(ins)
                for e in range(2):
                    p_ = slice(64 * e, 64 * e + 64)
                    for c in range(NC):
                        ins = mm(bank(1 + e, c * 256, 256), KB[p_, c * C:c * C + C], AR[p_, c * 256:c * 256 + 256], True, True)
                t_gk = b.pe(ins)
                V("tensor_tensor", t4, gb4[:, :, 0, :], rows(cc("lev0"), 4), ALU.mult, after=[t_m], chain=False)
                V("tensor_tensor", x4, x4, rows(cc("ident"), 4), ALU.add, chain=False, after=[t_i1])
                t_x = V("tensor_tensor", t4, t4, rows(cc("ident"), 4), ALU.add)
                t_tb = A(TR[:, :], bank(w.bank_tr), ACT.Copy, after=[t_tr], chain=False)
                t_t = t_gkm = V("tensor_tensor", tiles(GK[:, :], 256), two(1), rows(up2, 4), ALU.mult, after=[t_gk], chain=False)
                grams_out[0] = t_gkm
                yield
                for lev in range(1, 7):
                    m = ML[:, (lev % 2) * 4 * C:(lev % 2 + 1) * 4 * C]
                    b.wait("pe", t_l, t_x, t_t, t_tb)
                    for q in range(4):
                        ins = mm(bank(L0_, q * C, C), m[:, q * C:q * C + C], XI[:, q * C:q * C + C], True, True)
                    t_p = b.pe(ins)
                    t_c = A(T1[:, :], bank(L0_), ACT.Copy, after=[t_p], chain=False)
                    if lev < 6:
                        t_l = G("tensor_tensor", tiles(ML[:, ((lev + 1) % 2) * 4 * C:((lev + 1) % 2 + 1) * 4 * C], C),
                                gb4[:, :, 0, :], rows(cc(f"lev{lev + 1}"), 4), ALU.mult, after=[t_p], chain=False)
                    yield
                    b.wait("pe", t_c)
                    for q in range(4 if lev < 6 else 0):
                        ins = mm(bank(L1_, q * C, C), XT[:, q * C:q * C + C], T1[:, q * C:q * C + C], True, True)
                    t_p1 = b.pe(ins) if lev < 6 else None
                    for q in range(4):
                        ins = mm(bank(L2_, q * C, C), T1[:, q * C:q * C + C], XT[:, q * C:q * C + C], True, True)
                    t_p2 = b.pe(ins)
                    if lev < 6:
                        t_x = V("tensor_tensor", XI[:, :], XI[:, :], bank(L1_), ALU.add, after=[t_p1], chain=False)
                    t_t = V("tensor_tensor", XT[:, :], XT[:, :], bank(L2_), ALU.add, after=[t_p2], chain=False)
                    yield
                t_s = t_y = None
                for c in range(NC):
                    v_c = TR[:, c * P:c * P + P]
                    by = (L1_, L2_)[c]
                    b.wait("pe", t_t, t_s, t_gkm)
                    if c:
                        mm(bank(L0_, 0, P), AR[:, 256:256 + C], ST, True, False)
                    for e in range(2):
                        ins = mm(bank(L0_, e * 64, 64), gk4[:, 2 * e + c, 0, :], v_c[:, e * 64:e * 64 + 64], c == 0, e == 1 or c == 0)
                    t = A(R0, bank(L0_, 0, P), ACT.Copy, after=[b.pe(ins)], chain=False)
                    for e in range(2):
                        mm(bank(by, e * P, P), v_c, gk4[:, 2 * e + c, 1, :], e == 0, False)
                        if c:
                            mm(bank(by, e * P, P), ST, AR[:, 256 + C:256 + 2 * C], False, False)
                    if c == 0:
                        mm(bank(L2_, 0, P), TR[:, 256:384], v_c, True, False)
                    yield
                    b.wait("pe", t)
                    for e in range(2):
                        ins = mm(bank(L0_, 128 + e * 64, 64), XT[:, (2 * e + c) * C:(2 * e + c) * C + C],
                                 R0[:, e * 64:e * 64 + 64], True, True)
                    t = A(SA, bank(L0_, 128, P), ACT.Copy, after=[b.pe(ins)], chain=False)
                    yield
                    b.wait("pe", t)
                    if c == 0:
                        ins = mm(bank(L2_, 0, P), TR[:, 384:512], SA, False, True)
                        t_s = V("scalar_tensor_tensor", ST, bank(L2_, 0, P), fac[:, bass.ds(i * 2 + w.p, 1)], cc("head_sum"),
                                ALU.mult, ALU.mult, after=[b.pe(ins)], chain=False)
                    for e in range(2):
                        ins = mm(bank(by, e * P, P), SA, gb4[:, 2 * e + c, 1, :], False, e == 1)
                    t_y = b.pe(ins)
                    for e in range(2):
                        p_ = slice(64 * e, 64 * e + 64)
                        V("tensor_scalar", CS[p_, bass.ds(i * (2 * T) + (w.p * T + c * C), C)], psum[p_, by, e * P:e * P + P], 1.0, None,
                          ALU.mult, after=[t_y], chain=False)
                    yield

            def side_steps(i):
                for u in range(SIDE):
                    b.wait("sp", slot_free())
                    full = fetch(M_ADA, i * SIDE + u)
                    for part in range(2):
                        b.wait("act", full, piece_free())
                        b.wait("dve", round_piece(M_ADA, part))
                        rest_of_piece(M_ADA, part)
                    yield
                    b.wait("pe", b.slab_out.here())
                    for part in range(2):
                        b.wait("pe", piece_ready())
                        done = multiply_conditions(part, 7)
                    ev_ada(i * SIDE + u, psum[0:4, 7, 0:256], done)
                    yield

            per = {b.c["pe"]: 2 * 27 + SIDE, b.c["act"]: 2 * 15 + SIDE, b.c["dve"]: 2 * 28, b.c["pool"]: 12, b.slab_out: SIDE,
                   b.piece_hi: 2 * SIDE, b.piece_lo: 2 * SIDE, b.piece_done: 2 * SIDE}
            per.update({c: 16 * SIDE // RING for c in b.slot_full})
            with b.loop(DT // 2, per) as i:
                streams = [side_steps(i), pair_steps(i, pairs[0]), pair_steps(i, pairs[1])]
                next(streams[1])
                while streams:
                    for st in list(streams):
                        if next(st, 1) == 1:
                            streams.remove(st)
            tap("ywkv", CS[:, :])
            Y = CS[:, :]
            b.join()

            def head_stat(src, matrix):
                t, _ = mean_over(src, T, matrix, DT, 1, 0)
                return t, psum[:, 0:4, :].rearrange("p b n -> p (b n)")
            t, m_ = head_stat(Y, "head_mean")
            t = V("tensor_tensor", Y, Y, m_, ALU.subtract, after=[t])
            t = A(SG[:, :], Y, ACT.Square, after=[t])
            b.wait("pe", t)
            t, m_ = head_stat(SG, "head_mean")
            rsqrt(BV[:, :], m_, LNX_EPS, SG[:, :], after=[t])
            V("tensor_tensor", Y, Y, BV[:, :], ALU.mult)
            V("tensor_tensor", tiles(Y, T), tiles(Y, T), cols(vv("lnx_g"), T), ALU.mult)
            V("tensor_tensor", tiles(Y, T), tiles(Y, T), cols(vv("lnx_b"), T), ALU.add)
            V("tensor_tensor", KK[:, :], Rr, Kr, ALU.mult)
            t = V("tensor_tensor", tiles(KK[:, :], T), tiles(KK[:, :], T), cols(vv("r_k"), T), ALU.mult)
            b.wait("pe", t)
            t, m_ = head_stat(KK, "head_sum")
            V("tensor_tensor", KK[:, :], Vr, m_, ALU.mult, after=[t])
            V("tensor_tensor", Y, Y, KK[:, :], ALU.add)
            b.join()
            for k in range(DT):
                ins = mm(bank(k // 2, (k % 2) * T, T), g2[:, k * P:k * P + P], gl, True, True)
            V("tensor_tensor", Y, Y, psum[:, 0:4, :].rearrange("p b n -> p (b n)"), ALU.mult, after=[b.pe(ins)])
            tap("yrwkv", Y)
            t = V("tensor_copy", rs_[:, 0:N8], Y)
            b.join()
        with ExitStack() as s:
            ms = Split(16 * T, s, "mixed")
            ms.set(mix[:, :])
            ms.set(rs_[:, 0:DT * T], DT * T)
            residual_linear(M_MIX0, feature(ms, T), M_KV[0])

    Kall = sb(DT * T, FB, "mem_k")
    Vall = sb(2 * D, FB, "mem_v")

    def ev_kv(j, ap, tok):
        A(at(Kall, j, T), ap[:, 0:T], ACT.Copy, after=[tok], chain=False)
        d = tiles(Vall[:, :], D)[:, :, bass.ds(j * P, P)]
        leave("act", nc.scalar.activation, d, tiles(ap[:, T:2 * T], P), ACT.Copy)

    def after_mix(layer):
        layer_norm(X[:, :], X[:, :], T, vv("mix_g", 8 * layer, 8), vv("mix_b", 8 * layer, 8), EPS5, None)
        tap(f"mix{layer}", X[:, :])
        with ExitStack() as s:
            Q, O, xs_ = sb(DT * T, s, "q"), Split(DT * T, s, "o"), Split(DT * T, s)
            with ExitStack() as s2:
                raw, Mx = sb(DT * T, s2), Split(DT * T, s2, "mem")
                b.join()
                Mx.set(raw[:, :], after=[load(raw[:, :], dram["mem"], f"mem{layer}")])
                b.join()
                linear(M_KV[layer], feature(Mx, T), T, ev_kv, M_XQ[layer], product=multiply_kv, mid={"act": 1})
                b.join()
            xs_.set(X[:, :])
            b.join()
            linear(M_XQ[layer], feature(xs_, T), T, copy_out(Q), M_XO[layer])
            b.join()
            S = sb(8 * T, s, "probs")
            PT = sb(8 * T, s, "probs_t")
            st = sb(16, s, "stats")
            for h in range(4):
                for qt in range(2):
                    for dd in range(2):
                        k = 2 * h + dd
                        ins = mm(bank(h, qt * T, T), Q[:, k * T + qt * P:k * T + qt * P + P],
                                 Kall[:, k * T:(k + 1) * T], dd == 0, dd == 1)
            t = b.pe(ins)
            t = A(S[:, :], psum[:, 0:4, :].rearrange("p b n -> p (b n)"), ACT.Copy, after=[t])
            t = softmax_rows(tiles(S[:, :], T), 8, T, 256 ** -0.5, st[:, 0:8], st[:, 8:16], [t])
            b.wait("pe", t)
            for h in range(4):
                for qt in range(2):
                    for kt in range(2):
                        ins = nc.tensor.transpose(bank(4 + h, kt * T + qt * P, P),
                                                  S[:, (2 * h + qt) * T + kt * P:(2 * h + qt) * T + kt * P + P], cc("ident"))
            t = A(PT[:, :], psum[:, 4:8, :].rearrange("p b n -> p (b n)"), ACT.Copy, after=[b.pe(ins)])
            b.wait("pe", t)
            for k in range(DT):
                for kt in range(2):
                    v = Vall[:, kt * D + k * P:kt * D + k * P + P]
                    ins = mm(bank(k // 2, (k % 2) * T, T), v, PT[:, (2 * (k // 2) + kt) * T:(2 * (k // 2) + kt + 1) * T],
                             kt == 0, kt == 1)
            O.set(psum[:, 0:4, :].rearrange("p b n -> p (b n)"), after=[b.pe(ins)])
            residual_linear(M_XO[layer], feature(O, T), M_W13[layer])
        layer_norm(X[:, :], X[:, :], T, vv("xa_g", 8 * layer, 8), vv("xa_b", 8 * layer, 8), EPS5, None)
        tap(f"xa{layer}", X[:, :])
        with ExitStack() as s:
            xs_ = Split(DT * T, s)
            xs_.set(X[:, :])
            b.join()
            ffn([M_W13[layer]], xs_, T, [M_W2[layer]],
                lambda w2, h, then: residual_linear(w2, feature(h, T), then, halves=2), (M_Q, M_C1)[layer])
        layer_norm(X[:, :], X[:, :], T, vv("ffn_g", 8 * layer, 8), vv("ffn_b", 8 * layer, 8), EPS5, None)
        tap(f"ffn{layer}", X[:, :])

    after_mix(0)

    with ExitStack() as s:
        Q, K, O = (sb(DT * T, s, n) for n in ("q", "k", "o"))
        xs_ = Split(DT * T, s)
        xs_.set(X[:, :])
        Vt = sb(2 * D, s, "v_tok")
        am = sb(2 * T, s, "causal")
        b.join()
        tm = load(am[:, :], dram["causal"], "causal")
        linear(M_Q, feature(xs_, T), T, copy_out(Q), M_K)
        linear(M_K, feature(xs_, T), T, copy_out(K), M_V)
        linear(M_V, feature(xs_, T), T, copy_tokens(Vt[:, :], 2, D), M_AOUT, product=multiply_tokens)
        b.join()
        Qs, Ks, Vs = sb(2 * T, s, "q_heads"), sb(2 * T, s, "k_heads"), sb(2 * 2 * P, s, "v_heads")
        S, PT = sb(8 * T, s, "probs"), sb(8 * T, s, "probs_t")
        st = sb(16, s, "stats")
        b.wait("dve", tm)
        S3 = S[:, :].rearrange("p (h q k) -> p h q k", h=4, q=2)
        with b.loop(4, {b.c["pe"]: 3, b.c["act"]: 12, b.c["dve"]: 10}) as i:
            t1 = A(Qs[:, :], at(Q, i, 2 * T), ACT.Copy, chain=False, after=[b.before("pe")])
            t2 = A(tiles(Vs[:, :], 256), tiles(Vt[:, :], D)[:, :, bass.ds(i * 256, 256)], ACT.Copy, chain=False)
            t3 = V("tensor_copy", Ks[:, :], at(K, i, 2 * T), after=[b.before("pe")], chain=False)
            b.wait("pe", t1, t2, t3, b.before("dve"))
            for h in range(4):
                p_ = slice(64 * (h % 2), 64 * (h % 2) + 64)
                for qt in range(2):
                    ins = mm(bank(h, qt * T, T), Qs[p_, (h // 2) * T + qt * P:(h // 2) * T + qt * P + P],
                             Ks[p_, (h // 2) * T:(h // 2) * T + T], True, True)
            t = b.pe(ins)
            for h in range(4):
                t = V("tensor_tensor", S[:, h * 2 * T:(h + 1) * 2 * T], bank(h), am[:, :], ALU.add, after=[t, t2], chain=False)
            t = softmax_rows(tiles(S[:, :], T), 8, T, HD ** -0.5, st[:, 0:8], st[:, 8:16], [t])
            b.wait("pe", t)
            for h in range(4):
                for qt in range(2):
                    for kt in range(2):
                        ins = nc.tensor.transpose(bank(4 + h, kt * T + qt * P, P),
                                                  S[:, (2 * h + qt) * T + kt * P:(2 * h + qt) * T + kt * P + P], cc("ident"))
            t = A(PT[:, :], psum[:, 4:8, :].rearrange("p b n -> p (b n)"), ACT.Copy, after=[b.pe(ins)], chain=False)
            b.wait("pe", t)
            for h in range(4):
                for kt in range(2):
                    ins = mm(bank(h, 0, T), Vs[:, kt * 256 + (h // 2) * P:kt * 256 + (h // 2) * P + P],
                             PT[:, (2 * h + kt) * T:(2 * h + kt + 1) * T], kt == 0, kt == 1)
            t = b.pe(ins)
            Oi = tiles(at(O, i, 2 * T), T)
            for hh in range(2):
                p_ = slice(64 * hh, 64 * hh + 64)
                src = psum[p_, 0:4, 0:T].rearrange("p (a e) n -> p a e n", e=2)[:, :, hh, :]
                if hh == 0:
                    t_o = V("tensor_copy", Oi[p_, :, :], src, after=[t], chain=False)
                else:
                    A(Oi[p_, :, :], src, ACT.Copy, after=[t, t_o], chain=False)
        b.join()
        xs_.set(O[:, :])
        residual_linear(M_AOUT, feature(xs_, T), M_KV[1])
    after_mix(1)

    FB.close()
    R = sb(DT * 2 * T, name="streams")
    r4 = R[:, :].rearrange("p (t s n) -> p t s n", s=2, n=T)
    b.join()
    t = load(r4[:, :, 0, :], dram["ctx"].rearrange("p (t n) -> p t n", n=T), "ctx")
    V("tensor_copy", r4[:, :, 1, :], tiles(X[:, :], T))
    for e in ("act", "dve"):
        b.wait(e, t)
    b.join()

    def mod(layer, part, lo=0, n=16):
        o = layer * 96 + part * 16 + lo
        return mods[:, o:o + n]

    def modulate(src, dst, ns, layer, gain, part, work=None):
        n = ns * T
        with ExitStack() as s:
            sq, rs, gm = *(work or (sb(DT * n, s), sb(2 * n, s))), sb(16, s)
            b.join()
            t = A(sq[:, :], src, ACT.Square)
            b.wait("pe", t)
            t, (ms,) = mean_over(sq, n, "ones_model", DT, DT, 4)
            rsqrt(rs[:, n:2 * n], ms, EPS6, rs[:, 0:n], after=[t])
            V("tensor_scalar", gm[:, :], mod(layer, part + 1), 1.0, None, ALU.add)
            V("tensor_tensor", tiles(gm[:, :], 2), tiles(gm[:, :], 2), cols(vv(gain, 8 * layer, 8), 2), ALU.mult)
            V("tensor_tensor", tiles(sq[:, :], n), tiles(src, n), rows(rs[:, n:2 * n], DT), ALU.mult)
            v = tiles(sq[:, :], T)
            if ns == 2:
                g, h = gm[:, :], mod(layer, part)
            else:
                g, h = tiles(gm[:, :], 2)[:, :, 1], tiles(mod(layer, part), 2)[:, :, 1]
            V("tensor_tensor", v, v, cols(g, T), ALU.mult)
            t = V("tensor_tensor", v, v, cols(h, T), ALU.add)
            dst.set(sq[:, :], after=[t])
            b.join()

    def gated_linear(m, x, then, layer, part):
        b.join()
        width, mo = m.mo * 2 * T, m.mo
        with ExitStack() as s:
            tmp = sb(4 * width, s)

            def evac(j, ap, tok):
                tm = tmp[:, 0:width]
                gates = mods[:, bass.ds(layer * 96 + part * 16 + j * (2 * mo), 2 * mo)]
                t = V("tensor_tensor", tiles(tm, T), tiles(ap, T), cols(gates, T), ALU.mult,
                      after=[tok, b.slab_out.here()], chain=False)
                leave("dve", nc.vector.tensor_tensor, at(R, j, width), at(R, j, width), tm, ALU.add, after=[t])
            linear(m, x, 2 * T, evac, then, mid={"dve": 1})
            b.join()


    with ExitStack() as s:
        W2 = 2 * T
        PW = T + 2 * PAD
        hm = Split(DT * W2, s, "modulated")
        YP = sb(DT * 2 * PW, s, "glu_padded")
        sg = sb(4 * W2, s, "sig")
        acc = sb(DT * W2, s, "conv")
        yp3 = tiles(YP[:, :], PW)
        V("memset", YP[:, :], 0.0)
        modulate(R[:, :], hm, 2, 0, "norm_mix", 0)
        ob = VOFF["conv_b1"][0]

        def ev_glu(j, ap, tok):
            ph = (b.piece_done.n // 2 - 1) % 4
            gt = sg[:, ph * W2:ph * W2 + W2]
            n = b.slab_out.n
            t = A(gt, ap[:, W2:2 * W2], ACT.Sigmoid, bias=vec[:, bass.ds(j + (ob + 8), 1)], chain=False,
                  after=[tok, Tok(b.slab_out, n - 3, b.slab_out.loop)])
            leave("dve", nc.vector.scalar_tensor_tensor, yp3[:, bass.ds(j * 2, 2), PAD:PAD + T],
                  tiles(ap[:, 0:W2], T), vec[:, bass.ds(j + ob, 1)], tiles(gt, T), ALU.add, ALU.mult, after=[t])
        linear(M_C1, feature(hm, W2), W2, ev_glu, M_C2, mid={"act": 1})
        b.join()
        od = VOFF["conv_dw"][0]
        with b.loop(DT, {b.c["dve"]: CONV_W}) as i:
            a_i = tiles(at(acc, i, W2), T)
            for k in range(CONV_W):
                src = yp3[:, bass.ds(i * 2, 2), k:k + T]
                wk = vec[:, bass.ds(i + (od + 8 * k), 1)]
                if k == 0:
                    V("tensor_scalar", a_i, src, wk, vec[:, bass.ds(i + VOFF["conv_dw_b"][0], 1)], ALU.mult, ALU.add)
                else:
                    V("scalar_tensor_tensor", a_i, src, wk, a_i, ALU.mult, ALU.add)
        b.join()
        tap("dwconv", acc[:, :])
        layer_norm(acc[:, :], acc[:, :], W2, vv("conv_norm"), None, EPS6, None)
        t = A(acc[:, :], acc[:, :], ACT.Silu)
        hm.set(acc[:, :], after=[t])
        gated_linear(M_C2, feature(hm, W2), M_GU0[0], 0, 2)
    tap("convout", R[:, :])
    with ExitStack() as s:
        hm = Split(DT * 2 * T, s, "modulated")
        modulate(R[:, :], hm, 2, 0, "norm_ffn", 3)
        ffn(M_GU0, hm, 2 * T, M_DOWN0,
            lambda w2, h, then: gated_linear(w2, feature(h, 2 * T), then, 0, 5), M_RQ)
    tap("l0out", R[:, :])

    def gated_x(m, x, then, layer, part, halves=1):
        b.join()
        def evac(j, ap, tok):
            gate = mods[:, bass.ds(j * 2 + (layer * 96 + part * 16 + 1), 1)]
            leave("dve", nc.vector.scalar_tensor_tensor, at(X, j, T), ap, gate, at(X, j, T), ALU.mult, ALU.add, after=[tok])
        linear(m, x, T, evac, then, halves=halves)
        b.join()

    with ExitStack() as s:
        V("tensor_copy", tiles(X[:, :], T), r4[:, :, 1, :])
        QX, KX = sb(DT * T, s, "q"), sb(DT * 2 * T, s, "k")
        Vt = sb(4 * 2048, s, "v_tok")
        Gt, O = sb(16 * T, s, "gate"), sb(16 * T, s, "o")
        with ExitStack() as s2:
            hm = Split(DT * 2 * T, s2, "modulated")
            modulate(R[:, :], hm, 2, 1, "norm_mix", 0, work=(O, QX))
            xs = feature(hm, 2 * T, T, T)

            def ev_g(j, ap, tok):
                leave("act", nc.scalar.activation, at(Gt, j, 512), ap, ACT.Silu, after=[tok])
            linear(M_RQ, xs, T, copy_out(QX), M_RK)
            linear(M_RK, feature(hm, 2 * T), 2 * T, copy_out(KX, 1024), M_RV)
            linear(M_RV, feature(hm, 2 * T), 2 * T, copy_tokens(Vt[:, :], 4, 2048), M_RG, product=multiply_tokens)
            linear(M_RG, xs, T, ev_g, M_ROUT)
            b.join()
        with ExitStack() as s2:
            dist, rope = sb(12 * T, s2, "dist"), sb(4 * T, s2, "rope")
            t = [load(dist[:, :], dram["dist"], "dist"), load(rope[:, :], dram["rope"], "rope")]
            b.wait("dve", t)
            b.wait("act", t)
            tmp = O[:, 0:DT * T]
            tab = rope[:, :].rearrange("p (w m n) -> p w m n", w=2, m=2)
            kx4 = KX[:, :].rearrange("p (h m s n) -> p h m s n", m=2, s=2, n=T)
            for dst, src, width in ((QX[:, :].rearrange("p (h m n) -> p h m n", m=2, n=T), QX, T),
                                    (kx4[:, :, :, 1, :], KX, 2 * T)):
                for k in range(DT):
                    ins = mm(bank(k // 2, (k % 2) * T, T), cc("swap"), src[:, k * width + width - T:(k + 1) * width], True, True)
                t = b.pe(ins)
                tp = tmp.rearrange("p (h m n) -> p h m n", m=2, n=T)
                tb = lambda w: tab[:, w:w + 1, :, :].broadcast_to([P, 4, 2, T])
                V("tensor_tensor", tp, psum[:, 0:4, :].rearrange("p b (m n) -> p b m n", m=2), tb(1), ALU.mult, after=[t])
                V("tensor_tensor", dst, dst, tb(0), ALU.mult)
                V("tensor_tensor", dst, dst, tp, ALU.add)
                b.join()
            dw = sb(5 * 8, s2)
            w_ = [dw[:, i * 8:i * 8 + 8] for i in range(5)]
            log1p_exp_neg_abs(vv("decay"), w_[0], w_[1], w_[2])
            V("tensor_scalar", w_[3], vv("decay"), 0.0, None, ALU.min)
            lg = w_[3]
            t_lg = V("tensor_tensor", lg, lg, w_[2], ALU.subtract)
            WF, WB, SW = sb(4 * T, s2, "w_fwd"), sb(4 * T, s2, "w_bwd"), sb(4 * T, s2, "weights")
            for h in range(4):
                t = A(WF[:, :], dist[:, 0:4 * T], ACT.Exp, scale=lg[:, h:h + 1], after=[b.c["dve"].here()])
                t2 = A(WB[:, :], dist[:, 4 * T:8 * T], ACT.Exp, scale=lg[:, 4 + h:5 + h])
                for st_ in range(4):
                    for dd in range(2):
                        k = 2 * h + dd
                        ins = mm(bank(st_ // 2, (st_ % 2) * T, T), KX[:, k * 512 + st_ * P:k * 512 + st_ * P + P],
                                 QX[:, k * T:k * T + T], dd == 0, dd == 1)
                tq = b.pe(ins)
                V("tensor_tensor", WF[:, 2 * T:], WF[:, 2 * T:], dist[:, 8 * T:10 * T], ALU.mult, after=[t])
                V("tensor_tensor", WB[:, 2 * T:], WB[:, 2 * T:], dist[:, 10 * T:12 * T], ALU.mult, after=[t2])
                V("tensor_tensor", WF[:, :], WF[:, :], WB[:, :], ALU.add)
                t = V("scalar_tensor_tensor", SW[:, :], psum[:, 0:2, :].rearrange("p b n -> p (b n)"), 256 ** -0.5, WF[:, :],
                      ALU.mult, ALU.mult, after=[tq])
                b.wait("pe", t)
                for m in range(4):
                    for st_ in range(4):
                        ins = mm(bank(2 + m // 2, (m % 2) * T, T), Vt[:, st_ * 2048 + h * 512 + m * P:st_ * 2048 + h * 512 + m * P + P],
                                 SW[:, st_ * T:st_ * T + T], st_ == 0, st_ == 3)
                A(O[:, h * 4 * T:(h + 1) * 4 * T], psum[:, 2:4, :].rearrange("p b n -> p (b n)"), ACT.Copy, after=[b.pe(ins)])
                b.join()
        tap("reto", O[:, :])
        with ExitStack() as s2:
            sq, rs = sb(16 * T, s2), sb(8 * T, s2)
            t = A(sq[:, :], O[:, :], ACT.Square)
            b.wait("pe", t)
            t, _ = mean_over(sq, T, "ones_half", 16, 4, 4)
            rsqrt(rs[:, 4 * T:], psum[:, 4:6, :].rearrange("p b n -> p (b n)"), EPS6, rs[:, 0:4 * T], after=[t])
            for h in range(4):
                v = tiles(O[:, h * 4 * T:(h + 1) * 4 * T], T)
                V("tensor_tensor", v, v, rows(rs[:, (4 + h) * T:(5 + h) * T], 4), ALU.mult)
            V("tensor_tensor", O[:, :], O[:, :], Gt[:, :], ALU.mult)
            b.join()
        os_ = Split(16 * T, s, "o")
        os_.set(O[:, :])
        gated_x(M_ROUT, feature(os_, T), M_GU1, 1, 2)
    tap("mods", mods[:, :])
    tap("retout", X[:, :])
    with ExitStack() as s:
        hm = Split(DT * T, s, "modulated")
        modulate(X[:, :], hm, 1, 1, "norm_ffn", 3)
        ffn([M_GU1], hm, T, [M_DOWN1], lambda w2, h, then: gated_x(w2, feature(h, T), then, 1, 5, halves=2), None)
    b.wait("sp", *b.all())
    done = load(out, X[:, :], "out")
    b.wait("sp", done)


def slabs(w, kt, groups, by_k=False):
    t = w.reshape(-1, P, w.shape[1] // P, P)
    out = []
    for g in groups:
        for lo in range(0, t.shape[0], kt):
            order = (1, 0, 2, 3) if by_k else (1, 2, 0, 3)
            out.append(t[lo:lo + kt][:, :, list(g), :].transpose(order).reshape(P, -1))
    return np.ascontiguousarray(np.stack(out))


def arrange(inp):
    def feat(x):
        return np.ascontiguousarray(x.T.reshape(DT, P, -1).transpose(1, 0, 2).reshape(P, -1))

    def col(v):
        return np.asarray(v).reshape(-1, P).T
    two = lambda n, o=0: [(o + 2 * i, o + 2 * i + 1) for i in range(n)]
    one = lambda n: [(i,) for i in range(n)]
    pair = lambda n: [(i, n + i) for i in range(n)]
    d = {"x": feat(inp["x"][0]), "mem": feat(inp["mem"][0]), "ctx": feat(inp["ctx_2"][0])}
    w = inp["even_w_in"][0]
    main = np.concatenate([w[:, :2560], w[:, 2576:]], axis=1)
    d["w_in"] = slabs(main, 8, two(23))
    d["w_dt"] = np.ascontiguousarray(w[:, 2560:2576].reshape(DT, P, 16).transpose(1, 0, 2).reshape(P, -1))
    d["w2a2"], d["g2"] = np.concatenate([inp["rwkv_w2"][0], inp["rwkv_a2"][0]], axis=0), inp["rwkv_g2"][0]
    d["w_mix0"] = slabs(inp["even_w_out"][0], 16, one(8))
    kv = inp["xa_wkv"]
    for l in range(2):
        d[f"w_kv{l}"] = slabs(kv[l], 8, pair(8))
    d["w_ada"] = np.concatenate([slabs(inp["ada_w_2"][l], 8, two(24), True) for l in range(2)])
    for l in range(2):
        d[f"w_xq{l}"] = slabs(inp["xa_wq"][l], 8, two(4))
        d[f"w_xo{l}"] = slabs(inp["xa_wo"][l], 8, two(4))
        d[f"w13_{l}"] = slabs(inp["ffn_w13"][l], 8, pair(FFN_T))
        d[f"w2_{l}"] = slabs(inp["ffn_w2"][l], 11, one(8))
        d[f"gu_{l}"] = slabs(inp["ffn_w_gu_2"][l], 8, pair(FFN_T))
        down = inp["ffn_w_down_2"][l]
        d[f"down_{l}"] = slabs(down, 11, one(8)) if l else \
            np.concatenate([slabs(down[:11 * P], 11, one(8)), slabs(down[11 * P:], 11, one(8))])
    qkv = inp["odd_w_qkv"][0]
    d["w_qkv"] = np.concatenate([slabs(qkv[:, :2 * D], 8, two(8)), slabs(qkv[:, 2 * D:], 8, two(4), True)])
    d["w_aout"] = slabs(inp["odd_w_out"][0], 8, two(4))
    d["w_c1"] = slabs(inp["conv_w1_2"][0], 8, pair(8))
    d["w_c2"] = slabs(inp["conv_w2_2"][0], 8, two(4))
    ret = inp["ret_w_in_2"][0]
    d["w_ret"] = np.concatenate([slabs(ret[:, :2 * D], 8, two(8)), slabs(ret[:, 2 * D:4 * D], 8, two(8), True),
                                 slabs(ret[:, 4 * D:], 8, two(8))])
    d["w_rout"] = slabs(inp["ret_w_out_2"][0], 16, one(8))
    heads = np.zeros((P, 2), np.float32)
    heads[:NH, 0], heads[:NH, 1] = inp["ssd_dt_bias"][0], inp["ssd_a_log"][0]
    cond = np.stack([col(inp["c_ctx_2"]), col(inp["c_2"][0])], axis=2).reshape(P, -1)
    decay = np.broadcast_to(np.concatenate([inp["ret_decay_f_2"][0], inp["ret_decay_b_2"][0]]), (P, 8))
    v = {
        "conv_w": np.concatenate([col(inp["ssd_conv_w"][0][k]) for k in range(4)], axis=1),
        "conv_b": col(inp["ssd_conv_b"][0]), "ssd_d": col(np.repeat(inp["ssd_d"][0], HD)),
        "ssd_g": col(inp["ssd_norm_g"][0]), "mu": col(inp["rwkv_mu"][0]), "w0": col(inp["rwkv_w0"][0]),
        "a0": col(inp["rwkv_a0"][0]), "k_k": col(inp["rwkv_k_k"][0]), "k_a": col(inp["rwkv_k_a"][0]),
        "r_k": col(inp["rwkv_r_k"][0].reshape(-1)), "lnx_g": col(inp["rwkv_lnx_g"][0]),
        "lnx_b": col(inp["rwkv_lnx_b"][0]), "mix_g": col(inp["ln_mix_g"]), "mix_b": col(inp["ln_mix_b"]),
        "xa_g": col(inp["ln_xa_g"]), "xa_b": col(inp["ln_xa_b"]), "ffn_g": col(inp["ln_ffn_g"]),
        "ffn_b": col(inp["ln_ffn_b"]), "cond": cond, "ada_b": col(inp["ada_b_2"]),
        "norm_mix": col(inp["norm_mix_2"]), "norm_ffn": col(inp["norm_ffn_2"]), "conv_b1": col(inp["conv_b1_2"]),
        "conv_dw": np.concatenate([col(inp["conv_dw_2"][0][k]) for k in range(CONV_W)], axis=1),
        "conv_dw_b": col(inp["conv_dw_b_2"]), "conv_norm": col(inp["conv_norm_2"]), "heads": heads, "decay": decay,
    }
    d["vectors"] = np.concatenate([v[n] for n, _ in VECTORS], axis=1)
    assert d["vectors"].shape[1] == NVEC
    d["consts"] = shape_constants()
    d["causal"] = attention_masks()
    d["dist"], d["rope"] = retention_constants()
    return {k: np.ascontiguousarray(a, dtype=np.float32) if a.dtype == np.float32 else a for k, a in d.items()}


def build(nc, arrays, tap_shapes=None):
    dram = {n: nc.dram_tensor(f"in_{n}", a.shape, F32, kind="ExternalInput").ap() for n, a in arrays.items()}
    out = nc.dram_tensor("out", (P, DT * T), F32, kind="ExternalOutput").ap()
    taps = {n: nc.dram_tensor(f"tap_{n}", s, F32, kind="ExternalOutput").ap() for n, s in (tap_shapes or {}).items()}
    program(nc, dram, out, taps)


def kernel(**inputs):
    import concourse.bacc as _bacc
    from concourse.bass_utils import run_bass_kernel_spmd as _run

    arrays = arrange({k: np.asarray(v) for k, v in inputs.items()})
    nc = _bacc.Bacc("TRN2", target_bir_lowering=False, num_devices=1)
    build(nc, arrays)
    r = _run(nc, [{f"in_{n}": a for n, a in arrays.items()}], core_ids=[0])
    y = r.results[0]["out"]
    return y.reshape(P, DT, T).transpose(1, 0, 2).reshape(D, T).T.reshape(1, T, D)
```

```python
import math
from contextlib import ExitStack, contextmanager

import numpy as np

import concourse.bass as bass
from concourse import mybir

F32 = mybir.dt.float32
F32R = mybir.dt.float32r
ACT = mybir.ActivationFunctionType
ALU = mybir.AluOpType
AX = mybir.AxisListType

P = 128
D = 1024
DT = D // P
T = 256
C = 128
NC = T // C
HD = 64
NH = D // HD
XBC_T = 12
RW_T = 26
FFN_T = 22
SLOT = 16 * P
RING = 4
PIECE = 8 * P
PIECES = 2
ALPHA = 4.0 ** 0.25
EPS5, EPS6, LNX_EPS = 1e-5, 1e-6, 64e-5
KAPPA = math.exp(-0.5)
CONV_W = 31
PAD = CONV_W // 2
NEG = -1e30

VECTORS = [
    ("conv_w", 4 * XBC_T), ("conv_b", XBC_T), ("ssd_d", 8), ("ssd_g", 8), ("mu", RW_T), ("w0", 8),
    ("a0", 8), ("k_k", 8), ("k_a", 8), ("r_k", 8), ("lnx_g", 8), ("lnx_b", 8),
    ("mix_g", 16), ("mix_b", 16), ("xa_g", 16), ("xa_b", 16), ("ffn_g", 16), ("ffn_b", 16),
    ("cond", 16), ("ada_b", 96), ("norm_mix", 16), ("norm_ffn", 16), ("conv_b1", 16),
    ("conv_dw", CONV_W * 8), ("conv_dw_b", 8), ("conv_norm", 8), ("heads", 2), ("decay", 8),
]
VOFF, _o = {}, 0
for _n, _c in VECTORS:
    VOFF[_n] = (_o, _c)
    _o += _c
NVEC = _o
CONSTS = ["ident", "ones", "ones_model", "ones_half", "head_sum", "head_mean", "upper_strict", "upper",
          "low0"] + [f"lev{k}" for k in range(7)] + ["swap", "cond_sum"]
COFF = {n: i * P for i, n in enumerate(CONSTS)}


def shape_constants():
    s, t = np.arange(P)[:, None], np.arange(P)[None, :]
    out = {"ident": s == t, "ones": np.ones((P, P)), "ones_model": np.full((P, P), 1 / D),
           "ones_half": np.full((P, P), 1 / 512), "head_sum": s // HD == t // HD,
           "head_mean": (s // HD == t // HD) / HD, "upper_strict": s < t, "upper": s <= t}
    for k in range(7):
        b = 1 << k
        lev = (s // (2 * b) == t // (2 * b)) & (s % (2 * b) < b) & (t % (2 * b) >= b)
        out[f"lev{k}"] = lev
        if k == 0:
            out["low0"] = lev.T
    out["cond_sum"] = (s % 2 == t) & (s < 4)
    out["swap"] = np.where(s == t + 64, -1.0, 0.0) + np.where(t == s + 64, 1.0, 0.0)
    return np.concatenate([out[n].astype(np.float32) for n in CONSTS], axis=1)


def attention_masks():
    q = np.arange(P)[:, None, None] + P * np.arange(2)[None, :, None]
    k = np.arange(T)[None, None, :]
    return np.where(k <= q, 0.0, NEG).astype(np.float32).reshape(P, 2 * T)


def retention_constants():
    m, t = np.arange(T)[:, None], np.arange(T)[None, :]
    fwd = np.concatenate([t + T - m, np.abs(t - m)])
    bwd = np.concatenate([T - t + m, np.abs(t - m)])
    seen_f, seen_b = (m <= t), (m >= t)

    def tiles(a):
        return a.reshape(-1, P, T).transpose(1, 0, 2).reshape(P, -1)
    dist = np.concatenate([tiles(fwd), tiles(bwd), tiles(seen_f), tiles(seen_b)], axis=1)
    inv = (np.float32(10000.0) ** (-np.arange(64, dtype=np.float32) / np.float32(64))).astype(np.float32)
    tok = np.arange(T)
    tabs = []
    for pos in (tok // 64, tok % 64):
        ang = (pos[None, :].astype(np.float32) * inv[:, None]).astype(np.float32)
        ang = np.concatenate([ang, ang], axis=0)
        tabs += [np.cos(ang), np.sin(ang)]
    order = [tabs[0], tabs[2], tabs[1], tabs[3]]
    return dist.astype(np.float32), np.concatenate(order, axis=1).astype(np.float32)


class Tok:

    def __init__(self, clock, n, loop):
        self.clock, self.n, self.loop = clock, n, loop


class Count:

    def __init__(self, sem, inc=1):
        self.sem, self.inc, self.n, self.loop = sem, inc, 0, None

    def mark(self, ins):
        ins.then_inc(self.sem, self.inc)
        self.n += self.inc
        return Tok(self, self.n, self.loop)

    def here(self):
        return Tok(self, self.n, self.loop)

    def value(self, n):
        return Tok(self, n, self.loop)


class Matrix:

    def __init__(self, name, slabs, kt=8, mo=2, row0=0):
        self.name, self.slabs, self.kt, self.mo, self.row0 = name, slabs, kt, mo, row0
        self.size = kt * mo * P
        self.half = (kt * mo + 1) // 2

    def words(self, part):
        return (0, self.half * P) if part == 0 else (self.half * P, self.size)


class Loop:
    def __init__(self, index, count, per):
        self.index, self.count, self.per, self.open = index, count, per, True


SIDE = 12
M_IN_Z, M_IN_XBC, M_IN_RW = Matrix("w_in", 4), Matrix("w_in", 6, row0=4), Matrix("w_in", 13, row0=10)
M_ADA = Matrix("w_ada", 48)
M_MIX0 = Matrix("w_mix0", 8, 16, 1)
M_KV, M_XQ, M_XO = ([Matrix(f"{w}{l}", n) for l in range(2)] for w, n in (("w_kv", 8), ("w_xq", 4), ("w_xo", 4)))
M_W13 = [Matrix(f"w13_{l}", 22) for l in range(2)]
M_W2 = [Matrix(f"w2_{l}", 16, 11, 1) for l in range(2)]
M_Q, M_K, M_V = (Matrix("w_qkv", 4, row0=4 * i) for i in range(3))
M_AOUT = Matrix("w_aout", 4)
M_C1, M_C2 = Matrix("w_c1", 8), Matrix("w_c2", 4)
M_GU0 = [Matrix("gu_0", 11, row0=11 * i) for i in range(2)]
M_DOWN0 = [Matrix("down_0", 8, 11, 1, row0=8 * i) for i in range(2)]
M_RQ, M_RK, M_RV, M_RG = (Matrix("w_ret", n, row0=r) for n, r in ((4, 0), (4, 4), (8, 8), (8, 16)))
M_ROUT = Matrix("w_rout", 8, 16, 1)
M_GU1, M_DOWN1 = Matrix("gu_1", 22), Matrix("down_1", 16, 11, 1)


class Build:

    def __init__(self, nc, ctx):
        self.nc, self.ctx = nc, ctx
        self.eng = {"pe": nc.tensor, "act": nc.scalar, "dve": nc.vector, "pool": nc.gpsimd, "sp": nc.sync}
        self.c = {e: Count(self.sem("done_" + e)) for e in ("pe", "act", "dve", "pool")}
        self.loads = Count(self.sem("small_loads"), 16)
        self.slot_full = [Count(self.sem(f"slot_full{i}"), 16) for i in range(RING)]
        self.piece_hi = Count(self.sem("piece_hi"))
        self.piece_lo = Count(self.sem("piece_lo"))
        self.piece_done = Count(self.sem("piece_done"))
        self.slab_out = Count(self.sem("slab_out"))
        self.counts = list(self.c.values()) + [self.loads, self.slab_out, self.piece_hi, self.piece_lo,
                                               self.piece_done] + self.slot_full
        self.seen = {}

    def sem(self, name):
        return self.ctx.enter_context(self.nc.semaphore(name))

    def wait(self, e, *toks):
        for t in toks:
            if t is None:
                continue
            if isinstance(t, (list, tuple)):
                self.wait(e, *t)
                continue
            key = (e, t.clock)
            lp = t.loop
            if lp is not None and not lp.open:
                t, lp = Tok(t.clock, t.n + (lp.count - 1) * lp.per.get(t.clock, 0), None), None
            if lp is None:
                if t.n <= 0 or self.seen.get((key, None), 0) >= t.n:
                    continue
                self.seen[(key, None)] = t.n
                self.eng[e].wait_ge(t.clock.sem, t.n)
            else:
                if self.seen.get((key, lp), -1 << 30) >= t.n:
                    continue
                self.seen[(key, lp)] = t.n
                per = lp.per.get(t.clock, 0)
                assert t.n >= 1, "a wait that may be negative"
                self.eng[e].wait_ge(t.clock.sem, lp.index * per + t.n if per else t.n)

    def run(self, e, fn, *a, after=(), chain=True, **kw):
        self.wait(e, *(after if isinstance(after, (list, tuple)) else (after,)))
        if chain:
            self.wait(e, self.c[e].here())
        return self.c[e].mark(fn(*a, **kw))

    def V(self, op, *a, **kw):
        return self.run("dve", OPS[op](self.nc.vector), *a, **kw)

    def G(self, op, *a, **kw):
        return self.run("pool", OPS[op](self.nc.gpsimd), *a, **kw)

    def A(self, out, in_, func, **kw):
        return self.run("act", self.nc.scalar.activation, out, in_, func, **kw)

    def mm(self, out, lhsT, rhs, start, stop):
        return self.nc.tensor.matmul(out, lhsT, rhs, start=start, stop=stop)

    def pe(self, ins):
        return self.c["pe"].mark(ins)

    def fetched(self):
        return sum(c.n for c in self.slot_full) // 16

    def before(self, e):
        c = self.c[e]
        return Tok(c, self.start[c], c.loop)

    def all(self):
        return [c.here() for c in self.c.values()] + [self.slab_out.here(), self.loads.here(), self.piece_done.here()]

    def join(self, *engines):
        for e in engines or ("pe", "act", "dve", "pool"):
            self.wait(e, *self.all())

    @contextmanager
    def loop(self, count, per):
        start = {c: c.n for c in self.counts}
        with self.nc.Fori(0, count) as i:
            lp = Loop(i, count, per)
            for c in self.counts:
                c.loop = lp
            self.start = start
            yield i
        lp.open = False
        bad = {c.sem.name: (c.n - start[c], per.get(c, 0)) for c in self.counts if c.n - start[c] != per.get(c, 0)}
        assert not bad, bad
        for c in self.counts:
            c.n = start[c] + count * per.get(c, 0)
            c.loop = None


OPS = {
    "tensor_tensor": lambda e: e.tensor_tensor, "tensor_scalar": lambda e: e.tensor_scalar,
    "scalar_tensor_tensor": lambda e: e.scalar_tensor_tensor, "tensor_copy": lambda e: e.tensor_copy,
    "tensor_reduce": lambda e: e.tensor_reduce, "memset": lambda e: e.memset,
    "reciprocal": lambda e: e.reciprocal, "scan": lambda e: e.tensor_tensor_scan,
}


def cols(ap, n):
    return ap.rearrange("p (t o) -> p t o", o=1).broadcast_to([ap.shape[0], ap.shape[1], n])


def rows(ap, t):
    return ap.rearrange("p (o n) -> p o n", o=1).broadcast_to([ap.shape[0], t, ap.shape[1]])


def tiles(ap, n):
    return ap.rearrange("p (t n) -> p t n", n=n)


def program(nc, dram, out, taps=None):
    with ExitStack() as ctx:
        _program(Build(nc, ctx), dram, out, taps or {})


def _program(b, dram, out, taps):
    nc = b.nc
    keep = b.ctx
    names = [0]
    V, G, A, mm = b.V, b.G, b.A, b.mm

    def sb(cols_, stack=keep, name="t", dt=F32):
        names[0] += 1
        return stack.enter_context(nc.sbuf_tensor(f"{name}_{names[0]}", [P, cols_], dt))

    class Split:

        def __init__(self, words, stack, name="x"):
            self.hi, self.lo = sb(words, stack, name + "_hi", F32R), sb(words, stack, name + "_lo", F32R)

        def __getitem__(self, sl):
            return self.hi[:, sl], self.lo[:, sl]

        def set(self, src, lo=0, after=()):
            w = src.shape[-1]
            t = A(self.hi[:, lo:lo + w], src, ACT.Copy, after=after, chain=False)
            return V("tensor_tensor", self.lo[:, lo:lo + w], src, self.hi[:, lo:lo + w].bitcast(F32),
                     ALU.subtract, after=[t], chain=False)


    vec = sb(NVEC, name="vectors")
    con = sb(P * len(CONSTS), name="constants")
    X = sb(DT * T, name="x")
    ring = [sb(SLOT, name=f"ring{i}") for i in range(RING)]
    pieces = [Split(PIECE, keep, f"piece{i}") for i in range(PIECES)]
    mods = sb(2 * 48 * 2, name="mods")
    psum = keep.enter_context(nc.psum_tensor("psum", [P, 8, 512], F32))

    def vv(name, lo=0, n=None):
        o, c = VOFF[name]
        return vec[:, o + lo:o + (c if n is None else lo + n)]

    def cc(name):
        return con[:, COFF[name]:COFF[name] + P]

    def load(dst, src, name=None):
        count = b.loads
        if name:
            count = Count(b.sem("load_" + name), 16)
            b.counts.append(count)
        return count.mark((nc.scalar if name else nc.sync).dma_start(dst, src))

    def tap(name, ap):
        if name in taps:
            b.wait("sp", *b.all())
            b.wait("sp", load(taps[name], ap))
            b.join()

    load(X[:, :], dram["x"])
    load(vec[:, :], dram["vectors"])

    def fetch(m, j):
        slot = b.fetched() % RING
        src = dram[m.name][m.row0 + j, :, :] if isinstance(j, int) else \
            dram[m.name][bass.ds(j + m.row0, 1), :, :].rearrange("s p n -> p (s n)")
        return b.slot_full[slot].mark(nc.sync.dma_start(ring[slot][:, 0:m.size], src))

    def round_piece(m, part):
        lo, hi = m.words(part)
        h = pieces[b.piece_hi.n % PIECES]
        return b.piece_hi.mark(nc.scalar.activation(h.hi[:, 0:hi - lo], ring[(b.fetched() - 1) % RING][:, lo:hi], ACT.Copy))

    def rest_of_piece(m, part):
        lo, hi = m.words(part)
        h = pieces[b.piece_lo.n % PIECES]
        return b.piece_lo.mark(nc.vector.tensor_tensor(
            h.lo[:, 0:hi - lo], ring[(b.fetched() - 1) % RING][:, lo:hi], h.hi[:, 0:hi - lo].bitcast(F32), ALU.subtract))

    def mm3(out, a, c, start, stop):
        for q, (l, r) in enumerate(((a[0], c[0]), (a[0], c[1]), (a[1], c[0]))):
            ins = mm(out, l, r, start and q == 0, stop and q == 2)
        return ins

    def multiply(m, x, n, part, first_bank, k0=0, start=True, stop=True):
        h = pieces[b.piece_done.n % PIECES]
        for t in range(m.half) if part == 0 else range(m.half, m.kt * m.mo):
            mt, k = t // m.kt, t % m.kt
            at_ = mt * n
            out_ = psum[:, first_bank + at_ // 512, at_ % 512:at_ % 512 + n]
            w = h[slice((t - m.half * part) * P, (t - m.half * part + 1) * P)]
            ins = mm3(out_, w, x(k + k0), start and k == 0, stop and k == m.kt - 1)
        return b.piece_done.mark(ins)

    def multiply_tokens(m, x, n, part, first_bank, **kw):
        h = pieces[b.piece_done.n % PIECES]
        for tt in range(n // P):
            out_ = psum[:, first_bank + tt // 2, (tt % 2) * 256:(tt % 2) * 256 + 256]
            for k in range(4):
                xk = tuple(a[:, tt * P:tt * P + P] for a in x(4 * part + k))
                ins = mm3(out_, xk, h[slice(k * 256, k * 256 + 256)], part == 0 and k == 0 and tt % 2 == 0,
                          part == 1 and k == 3 and tt % 2 == 1)
        return b.piece_done.mark(ins)

    def multiply_kv(m, x, n, part, first_bank, **kw):
        if part == 0:
            return multiply(m, x, n, 0, first_bank, stop=False)
        h = pieces[b.piece_done.n % PIECES]
        for tt in range(T // P):
            for k in range(DT):
                xk = tuple(a[:, tt * P:tt * P + P] for a in x(k))
                ins = mm3(psum[:, first_bank, T + tt * P:T + tt * P + P], xk, h[slice(k * P, k * P + P)],
                          False, tt == T // P - 1 and k == DT - 1)
        return b.piece_done.mark(ins)

    def multiply_conditions(part, bk):
        h = pieces[b.piece_done.n % PIECES]
        for k in range(4):
            c4 = cond4[:, 4 * (4 * part + k):4 * (4 * part + k) + 4]
            for q, w in enumerate((h.hi, h.lo)):
                ins = mm(psum[0:4, bk, 0:256], c4, w[:, k * 256:k * 256 + 256],
                         part == 0 and k == 0 and q == 0, part == 1 and k == 3 and q == 1)
        return b.piece_done.mark(ins)

    def slot_free():
        return b.piece_lo.value(2 * (b.fetched() - RING + 1))

    def piece_free():
        return b.piece_done.value(b.piece_hi.n - PIECES + 1)

    def piece_ready():
        return b.piece_lo.value(b.piece_done.n + 1)

    def leave(e, fn, *a, after=(), chain=False, **kw):
        b.wait(e, *(after if isinstance(after, (list, tuple)) else (after,)))
        if chain:
            b.wait(e, b.c[e].here())
        ins = fn(*a, **kw)
        ins.then_inc(b.slab_out.sem, b.slabs_a_result)
        b.slab_out.n += b.slabs_a_result
        return b.slab_out.here()

    b.slabs_a_result = 1
    b.prepared = None

    def prepare_first(m):
        b.wait("sp", slot_free())
        full = fetch(m, 0)
        for part in range(2):
            b.wait("act", full, piece_free())
            b.wait("dve", round_piece(m, part))
            rest_of_piece(m, part)
        b.prepared = m

    def linear(m, x, n, evac, then=None, product=multiply, halves=1, mid=None):
        nb = max(1, (m.mo * n + 511) // 512)
        depth = (4 if halves == 1 else 2) // nb
        base = b.slab_out.n
        b.wait("pe", b.slab_out.here())
        b.slabs_a_result = halves
        if b.prepared is None:
            prepare_first(m)
        assert b.prepared is m, (b.prepared.name, m.name)

        def turn(j, jo, u, nxt, k):
            bk = (b.slab_out.n - base) // halves % depth * nb
            kpart = u % halves
            for part in range(2):
                b.wait("pe", piece_ready())
                if part == 0 and kpart == 0:
                    b.wait("pe", b.slab_out.value(b.slab_out.n - (depth - 1) * halves))
                done = product(m, x, n, part, bk, k0=kpart * m.kt, start=kpart == 0, stop=kpart == halves - 1)
                if nxt is None:
                    continue
                if part == 0:
                    b.wait("sp", slot_free())
                    full = fetch(nxt, k)
                b.wait("act", full, piece_free())
                b.wait("dve", round_piece(nxt, part))
                rest_of_piece(nxt, part)
            if kpart == halves - 1:
                res = psum[:, bk, 0:m.mo * n] if nb == 1 else psum[:, bk:bk + nb, :].rearrange("p b n -> p (b n)")
                evac(jo, res, done)

        turns = (m.slabs - 1) // RING
        j0 = 0
        if turns > 1:
            per = {b.piece_hi: 2 * RING, b.piece_lo: 2 * RING, b.piece_done: 2 * RING, b.slab_out: RING}
            per.update({c: 16 for c in b.slot_full})
            for e, k in (mid or {}).items():
                per[b.c[e]] = k * RING // halves
            with b.loop(turns, per) as i:
                for u in range(RING):
                    j = i * RING + u
                    turn(j, j if halves == 1 else i * (RING // halves) + u // halves, u, m, i * RING + (u + 1))
            j0 = turns * RING
        for j in range(j0, m.slabs):
            turn(j, j // halves, j, *((m, j + 1) if j + 1 < m.slabs else (then, 0)))
        b.prepared = then
        b.slabs_a_result = 1
        return b.slab_out.here()

    def at(ap, j, width):
        return ap[:, bass.ds(j * width, width)]

    def bank(i, lo=0, n=512):
        return psum[:, i, lo:lo + n]

    def mean_over(src, n, matrix, nt, group, b0=4):
        outs = []
        for gidx in range(nt // group):
            off = gidx * n
            o = psum[:, b0 + off // 512, off % 512:off % 512 + n]
            for k in range(group):
                t = gidx * group + k
                ins = mm(o, cc(matrix), src[:, t * n:t * n + n], k == 0, k == group - 1)
            outs.append(o)
        return b.pe(ins), outs

    def rsqrt(dst, src, eps, tmp, after=()):
        V("tensor_scalar", tmp, src, eps, None, ALU.add, after=after)
        t = A(tmp, tmp, ACT.Sqrt, after=[b.c["dve"].here()])
        return V("reciprocal", dst, tmp, after=[t])

    eps_cols = sb(5, name="eps")
    V("memset", eps_cols[:, 0:1], EPS5)
    V("memset", eps_cols[:, 1:2], EPS6)
    V("memset", eps_cols[:, 2:3], 1.0)
    V("memset", eps_cols[:, 4:5], LNX_EPS)
    EPS_COL = {EPS5: eps_cols[:, 0:1], EPS6: eps_cols[:, 1:2]}

    def warm(func):
        A(eps_cols[:, 3:4], eps_cols[:, 2:3], func, chain=True)

    def norm(src, dst, n, eps, gain, shift, split=None, centre=False, func=ACT.Identity, work=None, meanwhile=None):
        with ExitStack() as s:
            sq, rs = work or (sb(DT * n, s, "squares"), sb(2 * n, s, "rstd"))
            dst = sq if dst is None else dst
            W, kt = 2 * T, 2 * T // n
            chunks = [slice(c * W, c * W + W) for c in range(DT * n // W)]
            b.join()
            A(eps_cols[:, 3:4], eps_cols[:, 2:3], ACT.Sqrt)
            t_mean = None
            if centre:
                t_mean, (mean,) = mean_over(src, n, "ones_model", DT, DT, 4)
            if meanwhile:
                meanwhile()
            for c, w in enumerate(chunks):
                if centre:
                    t_mean = V("tensor_tensor", tiles(src[:, w], n), tiles(src[:, w], n), rows(mean, kt), ALU.subtract,
                               after=[t_mean], chain=False)
                t = A(sq[:, w], src[:, w], ACT.Square, after=[t_mean], chain=False)
                b.wait("pe", t)
                for k in range(kt):
                    ins = mm(bank(5, 0, n), cc("ones_model"), sq[:, w.start + k * n:w.start + k * n + n],
                             c == 0 and k == 0, w.stop == DT * n and k == kt - 1)
            t = A(rs[:, 0:n], bank(5, 0, n), ACT.Sqrt, bias=EPS_COL[eps], after=[b.pe(ins)], chain=False)
            t_r = V("reciprocal", rs[:, n:2 * n], rs[:, 0:n], after=[t], chain=False)
            rest, ready = None, []
            for c, w in enumerate(chunks):
                b0, b1 = (slice(w.start + q * T, w.start + q * T + T) for q in range(2))
                t = V("tensor_tensor", tiles(sq[:, w], n), tiles(src[:, w], n), rows(rs[:, n:2 * n], kt), ALU.mult,
                      after=[t_r], chain=False)
                t_a = A(dst[:, b0], sq[:, b0], func, scale=gain(2 * c), bias=shift(2 * c), after=[t], chain=False)
                if func == ACT.Identity:
                    t_v = V("tensor_scalar", dst[:, b1], sq[:, b1], gain(2 * c + 1), shift(2 * c + 1), ALU.mult, ALU.add,
                            after=[t], chain=False)
                else:
                    t_v = t_a = A(dst[:, b1], sq[:, b1], func, scale=gain(2 * c + 1), bias=shift(2 * c + 1), chain=False)
                if split:
                    t = A(split.hi[:, w], dst[:, w], ACT.Copy, after=[t_v, t_a], chain=False)
                    if rest:
                        ready.append(V("tensor_tensor", *rest[0], ALU.subtract, after=rest[1], chain=False))
                    rest = (split.lo[:, w], dst[:, w], split.hi[:, w].bitcast(F32)), [t]
            if rest:
                ready.append(V("tensor_tensor", *rest[0], ALU.subtract, after=rest[1], chain=False))
            if not rest:
                b.join()
            return ready

    def layer_norm(gain, shift, layer, split=None, meanwhile=None):
        return norm(X, X, T, EPS5, lambda k: vv(gain, 8 * layer + k, 1), lambda k: vv(shift, 8 * layer + k, 1), split, centre=True, meanwhile=meanwhile)

    def residual_linear(m, x, then, halves=1):
        b.join()
        width = m.mo * T

        def evac(j, ap, tok):
            xs = at(X, j, width)
            leave("dve", nc.vector.scalar_tensor_tensor, xs, xs, ALPHA, ap, ALU.mult, ALU.add, after=[tok])
        linear(m, x, T, evac, then, halves=halves)
        b.join()

    def copy_out(dst, width=512, e="act"):
        def evac(j, ap, tok):
            if e == "act":
                leave("act", nc.scalar.activation, at(dst, j, width), ap, ACT.Copy, after=[tok])
            else:
                leave("dve", nc.vector.tensor_copy, at(dst, j, width), ap, after=[tok])
        return evac

    def copy_tokens(dst, nt, total):
        def evac(j, ap, tok):
            d = dst.rearrange("p (t c) -> p t c", c=total)[:, :, bass.ds(j * 256, 256)]
            leave("act", nc.scalar.activation, d, ap.rearrange("p (t c) -> p t c", c=256), ACT.Copy, after=[tok])
        return evac

    def feature(x, n, lo=0, width=None, ready=None):
        def operand(k):
            if ready:
                b.wait("pe", ready[k * len(ready) // DT])
            return x[slice(k * n + lo, k * n + lo + (width or n))]
        return operand

    def softmax_exp(S, n_rows, scale, mx, sm, after):
        V("tensor_reduce", mx, S, AX.X, ALU.max, after=after)
        t = V("tensor_scalar", mx, mx, -scale, None, ALU.mult)
        for r in range(n_rows):
            t2 = A(S[:, r, :], S[:, r, :], ACT.Exp, bias=mx[:, r:r + 1], scale=scale,
                   accum_out=sm[:, r:r + 1], after=[t], chain=False)
        return t2

    def softmax_divide(S, width, sm, after):
        V("reciprocal", sm, sm, after=after)
        return V("tensor_tensor", S, S, cols(sm, width), ALU.mult)

    def transpose_probs(S, PT, heads, after):
        b.wait("pe", after)
        for h in heads:
            for qt in range(2):
                for kt in range(2):
                    ins = nc.tensor.transpose(bank(4 + h, kt * T + qt * P, P),
                                              S[:, (2 * h + qt) * T + kt * P:(2 * h + qt) * T + kt * P + P], cc("ident"))
        lo, hi = heads[0], heads[-1] + 1
        return A(PT[:, lo * 2 * T:hi * 2 * T], psum[:, 4 + lo:4 + hi, :].rearrange("p b n -> p (b n)"), ACT.Copy,
                 after=[b.pe(ins)], chain=False)

    def ffn(w13s, xin, n, w2s, down, then, ready=None):
        for w13, w2, nxt in zip(w13s, w2s, [*w13s[1:], then]):
            tn = w13.slabs
            with ExitStack() as s:
                h = Split(tn * n, s, "hidden")
                gate, prod = sb(2 * n, s, "gate"), sb(2 * n, s, "prod")

                def evac(j, ap, tok):
                    ph = b.piece_done.n // 2 % 2
                    gt, pr = gate[:, ph * n:ph * n + n], prod[:, ph * n:ph * n + n]
                    t = A(gt, ap[:, 0:n], ACT.Silu, chain=False,
                          after=[tok, Tok(b.slab_out, b.slab_out.n - 1, b.slab_out.loop)])
                    t = leave("dve", nc.vector.tensor_tensor, pr, gt, ap[:, n:2 * n], ALU.mult, after=[t])
                    t = A(at(h.hi, j, n), pr, ACT.Copy, after=[t], chain=False)
                    V("tensor_tensor", at(h.lo, j, n), pr, at(h.hi, j, n).bitcast(F32), ALU.subtract,
                      after=[t], chain=False)
                warm(ACT.Silu)
                linear(w13, feature(xin, n, ready=ready), n, evac, w2, mid={"act": 2, "dve": 1})
                b.join()
                down(w2, h, nxt)

    cond4 = sb(DT * 4, name="cond_rows", dt=F32R)
    ada_rows = sb(2 * 256, name="ada_rows")
    sel = con[0:4, COFF["cond_sum"]:COFF["cond_sum"] + 2]

    def ev_ada(j, ap, tok):
        bk = 7
        ph = b.piece_done.n // 2 % 2
        row = ada_rows[0:4, ph * 256:ph * 256 + 256]
        t = A(row, ap[0:4, :], ACT.Copy, after=[tok], chain=False)
        b.wait("pe", t)
        for m in range(2):
            ins = mm(bank(bk, 256 + 2 * m, 2), row[:, m * P:m * P + P], sel, True, True)
        bias = cols(vv("ada_b")[:, bass.ds(j * 2, 2)], 2)
        leave("dve", nc.vector.tensor_tensor, tiles(at(mods, j, 4), 2), tiles(bank(bk, 256, 4), 2), bias,
              ALU.add, after=[b.pe(ins)])

    FB = ExitStack()
    with ExitStack() as L0:
        mix = sb(DT * T, L0, "ssd_out")
        scond = sb(16, L0, "silu_cond")
        wdt = sb(DT * 16, L0, "w_dt")
        g2 = sb(D, L0, "g2")
        w2a2 = sb(D, L0, "w2a2")
        later = [load(wdt[:, :], dram["w_dt"], "w_dt"), load(con[:, :], dram["consts"], "consts"),
                 load(g2[:, :], dram["g2"], "g2"), load(w2a2[:, :], dram["w2a2"], "w2a2")]
        rs_ = sb(RW_T * T, L0, "shifted")
        with ExitStack() as S1:
            Z = sb(DT * T, S1, "z")
            XBC = sb(XBC_T * (T + 3), S1, "xbc")
            XC = sb(XBC_T * T, S1, "xc")
            RW = S1.enter_context(ExitStack())
            xs_ = Split(DT * T, RW)
            rw_all = sb(RW_T * (T + 1) + 1, RW, "rw")
            rw = rw_all[:, 0:RW_T * (T + 1)]
            b.join()
            zero = V("memset", tiles(XBC[:, :], T + 3)[:, :, 0:3], 0.0)
            zero = V("memset", tiles(rw[:, :], T + 1)[:, :, 0:1], 0.0)
            t = A(scond[:, :], vv("cond"), ACT.Silu)
            c4 = tiles(cond4[:, :], 4)
            t = A(c4[:, :, 0:2], tiles(scond[:, :], 2), ACT.Copy, after=[t])
            V("tensor_tensor", c4[:, :, 2:4], tiles(scond[:, :], 2), c4[:, :, 0:2].bitcast(F32), ALU.subtract, after=[t])
            xs_.set(X[:, :])
            b.join()

            def ev_z(j, ap, tok):
                leave("act", nc.scalar.activation, at(Z, j, 512), ap, ACT.Silu, after=[tok])

            def padded(dst, pad):
                def evac(j, ap, tok):
                    d = tiles(dst[:, :], T + pad)[:, bass.ds(j * 2, 2), pad:T + pad]
                    leave("act", nc.scalar.activation, d, tiles(ap, T), ACT.Copy, after=[tok])
                return evac
            b.wait("act", zero)
            linear(M_IN_Z, feature(xs_, T), T, ev_z, then=M_IN_XBC)
            b.wait("pe", later[0])
            for k in range(DT):
                ins = mm(psum[0:16, 4, 0:T], wdt[:, k * 16:k * 16 + 16], X[:, k * T:k * T + T], k == 0, k == DT - 1)
            t_dt = b.pe(ins)
            linear(M_IN_XBC, feature(xs_, T), T, padded(XBC, 3), then=M_IN_RW)
            xc3, xb3 = tiles(XC[:, :], T), tiles(XBC[:, :], T + 3)
            cur, prv = tiles(rw[:, :], T + 1)[:, :, 1:T + 1], tiles(rw[:, :], T + 1)[:, :, 0:T]
            R3 = tiles(rs_[:, :], T)
            copy_rw = padded(rw, 1)
            oc, omu = VOFF["conv_w"][0], VOFF["mu"][0]

            def ev_rw(j, ap, tok):
                copy_rw(j, ap, tok)
                two = bass.ds(j * 2, 2)
                G("tensor_tensor", R3[:, two, :], prv[:, two, :], cur[:, two, :], ALU.subtract, after=[b.slab_out.here()], chain=False)
                G("tensor_tensor", R3[:, two, :], R3[:, two, :], cols(vec[:, bass.ds(j * 2 + omu, 2)], T), ALU.mult)
                now = tiles(rw_all[:, bass.ds(j * (2 * (T + 1)) + 1, 2 * (T + 1))], T + 1)[:, :, 0:T]
                G("tensor_tensor", R3[:, two, :], R3[:, two, :], now, ALU.add)
                if isinstance(j, int) and j >= XBC_T:
                    return
                o = xc3[:, bass.ds(j, 1), :]
                for w in range(4):
                    src, wk = xb3[:, bass.ds(j, 1), w:w + T], vec[:, bass.ds(j + (oc + w * XBC_T), 1)]
                    if w == 0:
                        V("tensor_scalar", o, src, wk, vec[:, bass.ds(j + VOFF["conv_b"][0], 1)], ALU.mult, ALU.add, chain=False)
                    else:
                        V("scalar_tensor_tensor", o, src, wk, o, ALU.mult, ALU.add)
            b.wait("dve", b.slab_out.here())
            b.wait("pool", zero)
            linear(M_IN_RW, feature(xs_, T), T, ev_rw, mid={"pool": 3, "dve": 4})
            t = b.c["dve"].here()
            A(XC[:, :], XC[:, :], ACT.Silu, after=[t])
            for e in ("pe", "act", "dve", "pool"):
                b.wait(e, later)
            b.join()
            RW.close()
            tap("z", Z[:, :]), tap("rs", rs_[:, :])

            XD_ = sb(2 * D, S1, "x_dt")
            tmp = sb(XBC_T * T, S1, "tmp")
            sm = sb(5 * T, S1, "dt_work")
            d16 = [sm[0:16, i * T:i * T + T] for i in range(5)]
            heads = vec[0:16, VOFF["heads"][0]:VOFF["heads"][0] + 2]
            V("tensor_scalar", d16[0], psum[0:16, 4, 0:T], heads[:, 0:1], None, ALU.add, after=[t_dt])

            def log1p_exp_neg_abs(x, w1, w2, w3):
                V("tensor_scalar", w1, x, -1.0, None, ALU.mult)
                V("tensor_tensor", w1, w1, x, ALU.min)
                t = A(w1, w1, ACT.Exp, after=[b.c["dve"].here()])
                t = V("tensor_scalar", w2, w1, 1.0, None, ALU.add, after=[t])
                t = A(w3, w2, ACT.Ln, after=[t])
                V("tensor_scalar", w2, w2, -1.0, 1e-30, ALU.add, ALU.max, after=[t])
                V("reciprocal", w2, w2)
                V("tensor_tensor", w2, w2, w1, ALU.mult)
                return V("tensor_tensor", w3, w3, w2, ALU.mult, after=[t])
            log1p_exp_neg_abs(d16[0], d16[1], d16[2], d16[3])
            V("tensor_scalar", d16[0], d16[0], 0.0, None, ALU.max)
            t = V("tensor_tensor", d16[0], d16[0], d16[3], ALU.add)
            an = sb(1, S1, "a_neg")
            t = A(an[0:16, :], heads[:, 1:2], ACT.Exp)
            V("tensor_scalar", d16[1], d16[0], an[0:16, 0:1], -1.0, ALU.mult, ALU.mult, after=[t])
            V("memset", d16[2], 1.0)
            for c in range(NC):
                s_ = slice(c * C, c * C + C)
                V("scan", d16[4][:, s_], d16[2][:, s_], d16[1][:, s_], 0.0, ALU.mult, ALU.add)
            tap("dt", sm[0:16, 0:T]), tap("acum", sm[0:16, 4 * T:5 * T]), tap("xc", XC[:, :])
            YD = mix[:, :]
            V("tensor_tensor", tiles(YD, T), tiles(XC[:, 0:DT * T], T), cols(vv("ssd_d"), T), ALU.mult)
            b.join()
            AE, EA = tmp[:, 0:16 * C], XBC[:, 0:16 * C]
            SEG = sb(16 * C, S1, "seg")
            XDT, XDD = XD_[:, 0:D], tmp[:, 16 * C:16 * C + D]
            CBm, Bt, S0 = sb(2 * C, S1, "cb"), sb(2 * C, S1, "b_tok"), XD_[:, D:2 * D]
            dT, dec = sb(2 * NH, S1, "dt_tok"), sb(NH, S1, "decay")
            one16 = con[0:16, COFF["ones"]:COFF["ones"] + P]
            id16 = con[0:16, COFF["ident"]:COFF["ident"] + 16]
            for c in range(NC):
                s_ = slice(c * C, c * C + C)
                V("tensor_tensor", tiles(AE[0:16, :], C), rows(d16[4][:, s_], NH), cols(id16, C), ALU.mult)
                b.join()
                for q in range(4):
                    mm(bank(q), one16, AE[0:16, q * 512:q * 512 + 512], True, True)
                nc.tensor.transpose(psum[:, 4, 0:16], d16[0][:, s_], id16)
                nc.tensor.transpose(psum[:, 4, 16:32], d16[4][:, s_], id16)
                for g in range(2):
                    mm(bank(5, g * C, C), XC[:, (8 + g) * T + c * C:(8 + g) * T + c * C + C],
                       XC[:, (10 + g) * T + c * C:(10 + g) * T + c * C + C], True, True)
                for k in range(DT):
                    ins = nc.tensor.transpose(psum[:, 6 + k // 4, (k % 4) * P:(k % 4) * P + P],
                                              XC[:, k * T + c * C:k * T + c * C + C], cc("ident"))
                t = b.pe(ins)
                V("tensor_copy", dT[:, :], psum[:, 4, 0:32], after=[t])
                V("tensor_tensor", tiles(CBm[:, :], C), tiles(bank(5, 0, 2 * C), C), rows(cc("upper"), 2), ALU.mult)
                V("tensor_tensor", tiles(XDT[:, :], HD), psum[:, 6:8, :].rearrange("p b (h d) -> p (b h) d", d=HD),
                  cols(dT[:, 0:16], HD), ALU.mult)
                abc = psum[:, 0:4, :].rearrange("p b (h l) -> p (b h) l", l=C)
                V("tensor_tensor", tiles(SEG[:, :], C), abc, cols(dT[:, 16:32], C), ALU.subtract)
                t = V("tensor_scalar", SEG[:, :], SEG[:, :], 0.0, None, ALU.min)
                if c == 0:
                    V("tensor_tensor", dec[:, :], abc[:, :, C - 1], dT[:, 16:32], ALU.subtract)
                    td = V("tensor_scalar", dec[:, :], dec[:, :], 0.0, None, ALU.min)
                    A(dec[:, :], dec[:, :], ACT.Exp, after=[td])
                else:
                    A(EA[:, :], psum[:, 0:4, :].rearrange("p b n -> p (b n)"), ACT.Exp, after=[t])
                t = A(SEG[:, :], SEG[:, :], ACT.Exp, after=[t])
                for g in range(2):
                    w = slice(g * 8 * C, (g + 1) * 8 * C)
                    V("tensor_tensor", tiles(SEG[:, w], C), tiles(SEG[:, w], C),
                      rows(CBm[:, g * C:g * C + C], 8), ALU.mult, after=[t])
                    if c == 1:
                        V("tensor_tensor", tiles(EA[:, w], C), tiles(EA[:, w], C),
                          rows(XC[:, (10 + g) * T + C:(10 + g) * T + 2 * C], 8), ALU.mult)
                if c == 0:
                    V("tensor_tensor", tiles(XDD[:, :], HD), tiles(XDT[:, :], HD), cols(dec[:, :], HD), ALU.mult)
                b.join()
                for pr in range(8):
                    o = bank(pr // 2, (pr % 2) * 256, 256)
                    ins = mm(o, XDT[:, pr * P:pr * P + P], SEG[:, pr * 256:pr * 256 + 256], True, c == 0)
                    if c:
                        ins = mm(o, S0[:, pr * P:pr * P + P], EA[:, pr * 256:pr * 256 + 256], False, True)
                ty = b.pe(ins)
                if c == 0:
                    for g in range(2):
                        ins = nc.tensor.transpose(bank(4, g * P, P), XC[:, (8 + g) * T:(8 + g) * T + C], cc("ident"))
                    t = A(Bt[:, :], bank(4, 0, 256), ACT.Copy, after=[b.pe(ins)])
                    b.wait("pe", t)
                    for g in range(2):
                        ins = mm(bank(5 + g), Bt[:, g * P:g * P + P], XDD[:, g * 512:g * 512 + 512], True, True)
                    A(S0[:, :], psum[:, 5:7, :].rearrange("p b n -> p (b n)"), ACT.Copy, after=[b.pe(ins)])
                for hh in range(2):
                    p_ = slice(64 * hh, 64 * hh + 64)
                    o = tiles(YD, T)[p_, :, s_]
                    y = psum[p_, 0:4, :].rearrange("p b (q e l) -> p (b q) e l", q=2, e=2)[:, :, hh, :]
                    V("tensor_tensor", o, o, y, ALU.add, after=[ty])
                b.join()
            V("tensor_tensor", YD, YD, Z[:, :], ALU.mult)
            tap("yz", YD)
            sq = tmp[:, 0:DT * T]
            t = A(sq, YD, ACT.Square, after=[b.c["dve"].here()])
            b.wait("pe", t)
            t, _ = mean_over(sq, T, "ones_half", DT, 4, 4)
            rsd = sb(4 * T, S1, "rstd")
            rsqrt(rsd[:, 2 * T:], bank(4), EPS5, rsd[:, 0:2 * T], after=[t])
            for g in range(2):
                v = tiles(YD[:, g * 4 * T:(g + 1) * 4 * T], T)
                V("tensor_tensor", v, v, rows(rsd[:, (2 + g) * T:(3 + g) * T], 4), ALU.mult)
            V("tensor_tensor", tiles(YD, T), tiles(YD, T), cols(vv("ssd_g"), T), ALU.mult)
            tap("yssd", YD)
            b.join()

        with ExitStack() as S2:
            N8 = DT * T
            Rr, Kr, Vr = rs_[:, 0:N8], rs_[:, N8:2 * N8], rs_[:, 2 * N8:3 * N8]
            lo, gl = rs_[:, 24 * T:25 * T], rs_[:, 25 * T:26 * T]
            SG, CS, KK, BV = (sb(N8, S2, n) for n in ("sig_w", "cum", "kk", "b_vec"))
            on = sb(C, S2, "ones_row")
            edge = sb(2 * DT * NC, S2, "mid")
            fac = sb(DT, S2, "carry")
            scratch = S2.enter_context(ExitStack())
            SQ, AK = sb(N8, scratch, "squares"), sb(N8, scratch, "a_scaled")
            t = A(lo[0:64, :], lo[0:64, :], ACT.Tanh)
            t_kk = V("tensor_tensor", tiles(KK[:, :], T), tiles(Kr, T), cols(vv("k_k"), T), ALU.mult)
            b.wait("pe", t)
            t_w, t_a = [], []
            for half in range(2):
                p_ = slice(64 * half, 64 * half + 64)
                for k in range(DT):
                    ins = mm(bank(half * 4 + k // 2, (k % 2) * T, T), w2a2[p_, k * P:k * P + P], lo[p_, :], True, True)
                (t_w, t_a)[half].append(b.pe(ins))
            for half, dst, bias in ((0, SG, "w0"), (1, BV, "a0")):
                for k in range(DT):
                    A(dst[:, k * T:k * T + T], bank(half * 4 + k // 2, (k % 2) * T, T), ACT.Sigmoid,
                      bias=vv(bias, k, 1), after=(t_w, t_a)[half], chain=False)
                if half == 0:
                    t_sg = b.c["act"].here()
                    t_sq = A(SQ[:, :], KK[:, :], ACT.Square, after=[t_kk], chain=False)
            t_bv = b.c["act"].here()
            A(gl, gl, ACT.Sigmoid, chain=False)
            G("tensor_scalar", AK[:, :], BV[:, :], -1.0, None, ALU.add, after=[t_bv])
            t_ak = G("tensor_tensor", tiles(AK[:, :], T), tiles(AK[:, :], T), cols(vv("k_a"), T), ALU.mult)
            b.wait("pe", t_sg, t_sq)
            t_n, _ = mean_over(SQ[:, :], T, "head_sum", DT, 1, 0)
            t = V("memset", on[:, :], 1.0)
            for q in range(DT * NC):
                V("scan", CS[:, q * C:q * C + C], on[:, :], SG[:, q * C:q * C + C], 0.0, ALU.mult, ALU.add,
                  chain=q == 0, after=[t, t_sg])
            q3 = tiles(CS[:, :], C)
            t = V("tensor_scalar", SQ[:, :], psum[:, 0:4, :].rearrange("p b n -> p (b n)"), 1e-24, None, ALU.max, after=[t_n])
            t = A(SQ[:, :], SQ[:, :], ACT.Ln, after=[t])
            t_inv = A(SQ[:, :], SQ[:, :], ACT.Exp, scale=-0.5)
            V("tensor_copy", edge[:, 0:16], q3[:, :, C // 2 - 1])
            V("tensor_tensor", q3, q3, cols(edge[:, 0:16], C), ALU.subtract)
            e3 = edge[:, :].rearrange("p (w t c) -> p w t c", w=2, c=2)
            t = V("tensor_tensor", e3[:, 1, :, 0], q3.rearrange("p (t c) n -> p t c n", c=2)[:, :, 0, C - 1],
                  e3[:, 0, :, 1], ALU.add)
            A(fac[:, :], e3[:, 1, :, 0], ACT.Exp, scale=-KAPPA, after=[t])
            V("tensor_tensor", KK[:, :], KK[:, :], SQ[:, :], ALU.mult, after=[t_inv])
            V("scalar_tensor_tensor", Kr, AK[:, :], 1.0, Kr, ALU.add, ALU.mult, after=[t_ak])
            V("tensor_tensor", BV[:, :], BV[:, :], KK[:, :], ALU.mult)
            b.join()
            scratch.close()
            tap("kk", KK[:, :]), tap("cs", CS[:, :]), tap("kr", Kr), tap("bv", BV[:, :])

            PB = S2.enter_context(ExitStack())
            class Pair:

                def __init__(self, p):
                    self.p = p
                    self.EX, self.DE = sb(T, PB, "exp"), sb(T, PB, "decay")
                    self.AR = sb(2 * 2 * C, PB, "a_r")
                    self.KB = sb(2 * T, PB, "k_b")
                    self.VP = sb(T, PB, "v_pair")
                    self.TR = sb(4 * P, PB, "by_token")
                    self.GB, self.GK = sb(4 * 2 * C, PB, "gram_b"), sb(4 * 2 * C, PB, "gram_k")
                    self.ML = sb(2 * 4 * C, PB, "level")
                    self.XI, self.XT, self.T1 = (sb(4 * C, PB, n) for n in ("inv", "inv_t", "prod"))
                    self.R0, self.SA, self.ST = (self.EX[:, 0:P], self.EX[:, P:2 * P], self.VP[:, 0:P])
                    self.banks = ((0, 5, 6), (4, 1, 2))[p]
                    self.bank_tr = (0, 3)[p]
            pairs = [Pair(0), Pair(1)]
            up2 = con[:, COFF["upper_strict"]:COFF["upper_strict"] + 2 * C]
            b.join()

            grams_out = [None]

            def pair_steps(i, w):
                EX, AR, KB, VP, TR, GB, GK, ML, XI, XT, T1, R0, SA, ST = (
                    w.EX, w.AR, w.KB, w.VP, w.TR, w.GB, w.GK, w.ML, w.XI, w.XT, w.T1, w.R0, w.SA, w.ST)
                L0_, L1_, L2_ = w.banks
                tile = lambda a: a[:, bass.ds(i * (2 * T) + w.p * T, T)]
                ar4 = AR[:, :].rearrange("p (c w n) -> p c w n", c=2, w=2)
                gb4, gk4 = (tiles(g[:, :], C).rearrange("p (q w) n -> p q w n", w=2) for g in (GB, GK))
                old = [b.before(e) for e in ("pe", "act", "dve", "pool")]
                DE = w.DE[:, :]
                cs_i, sg_i = tile(CS), tile(SG)
                t_d = V("tensor_tensor", DE, cs_i, sg_i, ALU.subtract, after=old, chain=False)
                t_e = A(EX[:, :], cs_i, ACT.Exp, scale=KAPPA, after=old, chain=False)
                t_e2 = A(DE, DE, ACT.Exp, scale=-KAPPA, after=[t_e, t_d], chain=False)
                t_r = A(cs_i, cs_i, ACT.Exp, scale=-KAPPA, chain=False)
                t_v = A(VP[:, :], tile(Vr), ACT.Copy, chain=False)
                V("tensor_tensor", KB[:, 0:T], tile(Kr), EX[:, :], ALU.mult, after=[t_e], chain=False)
                V("tensor_tensor", KB[:, T:2 * T], tile(BV), EX[:, :], ALU.mult, chain=False)
                V("tensor_tensor", ar4[:, :, 1, :], tiles(tile(Rr), C), tiles(cs_i, C), ALU.mult, after=[t_r], chain=False)
                t = V("scalar_tensor_tensor", ar4[:, :, 0, :], tiles(tile(KK), C), -1.0, tiles(DE, C),
                      ALU.mult, ALU.mult, after=[t_e2], chain=False)
                yield
                b.wait("pe", t, t_v, grams_out[0])
                for e in range(2):
                    p_ = slice(64 * e, 64 * e + 64)
                    for c in range(NC):
                        mm(bank(1 + e, c * 256, 256), KB[p_, T + c * C:T + c * C + C], AR[p_, c * 256:c * 256 + 256], True, True)
                        ins = mm(bank(3 + e, c * C, C), AR[p_, c * 256:c * 256 + C], KB[p_, T + c * C:T + c * C + C], True, True)
                t_gb = b.pe(ins)
                two = lambda lo: psum[:, lo:lo + 2, :].rearrange("p b (c n) -> p (b c) n", n=256)
                t_m = V("tensor_tensor", tiles(GB[:, :], 256), two(1), rows(up2, 4), ALU.mult, after=[t_gb], chain=False)
                x4, t4 = tiles(XI[:, :], C), tiles(XT[:, :], C)
                for e in range(2):
                    t_i1 = V("tensor_tensor", tiles(XI[:, e * 2 * C:(e + 1) * 2 * C], C), tiles(psum[:, 3 + e, 0:2 * C], C),
                             rows(cc("low0"), 2), ALU.mult, chain=False)
                t_l = G("tensor_tensor", tiles(ML[:, 4 * C:], C), gb4[:, :, 0, :], rows(cc("lev1"), 4), ALU.mult,
                        after=[t_m], chain=False)
                yield
                b.wait("pe", t_i1 if w.p else t_m)
                for q, src in enumerate((VP[:, 0:C], VP[:, C:T], KB[:, 0:C], KB[:, T:T + C])):
                    ins = nc.tensor.transpose(bank(w.bank_tr, q * P, P), src, cc("ident"))
                t_tr = b.pe(ins)
                for e in range(2):
                    p_ = slice(64 * e, 64 * e + 64)
                    for c in range(NC):
                        ins = mm(bank(1 + e, c * 256, 256), KB[p_, c * C:c * C + C], AR[p_, c * 256:c * 256 + 256], True, True)
                t_gk = b.pe(ins)
                V("tensor_tensor", t4, gb4[:, :, 0, :], rows(cc("lev0"), 4), ALU.mult, after=[t_m], chain=False)
                V("tensor_tensor", x4, x4, rows(cc("ident"), 4), ALU.add, chain=False, after=[t_i1])
                t_x = V("tensor_tensor", t4, t4, rows(cc("ident"), 4), ALU.add)
                t_tb = A(TR[:, :], bank(w.bank_tr), ACT.Copy, after=[t_tr], chain=False)
                t_t = t_gkm = V("tensor_tensor", tiles(GK[:, :], 256), two(1), rows(up2, 4), ALU.mult, after=[t_gk], chain=False)
                grams_out[0] = t_gkm
                yield
                for lev in range(1, 7):
                    m = ML[:, (lev % 2) * 4 * C:(lev % 2 + 1) * 4 * C]
                    b.wait("pe", t_l, t_x, t_t, t_tb)
                    for q in range(4):
                        ins = mm(bank(L0_, q * C, C), m[:, q * C:q * C + C], XI[:, q * C:q * C + C], True, True)
                    t_p = b.pe(ins)
                    t_c = A(T1[:, :], bank(L0_), ACT.Copy, after=[t_p], chain=False)
                    if lev < 6:
                        t_l = G("tensor_tensor", tiles(ML[:, ((lev + 1) % 2) * 4 * C:((lev + 1) % 2 + 1) * 4 * C], C),
                                gb4[:, :, 0, :], rows(cc(f"lev{lev + 1}"), 4), ALU.mult, after=[t_p], chain=False)
                    yield
                    b.wait("pe", t_c)
                    for q in range(4 if lev < 6 else 0):
                        ins = mm(bank(L1_, q * C, C), XT[:, q * C:q * C + C], T1[:, q * C:q * C + C], True, True)
                    t_p1 = b.pe(ins) if lev < 6 else None
                    for q in range(4):
                        ins = mm(bank(L2_, q * C, C), T1[:, q * C:q * C + C], XT[:, q * C:q * C + C], True, True)
                    t_p2 = b.pe(ins)
                    if lev < 6:
                        t_x = V("tensor_tensor", XI[:, :], XI[:, :], bank(L1_), ALU.add, after=[t_p1], chain=False)
                    t_t = V("tensor_tensor", XT[:, :], XT[:, :], bank(L2_), ALU.add, after=[t_p2], chain=False)
                    yield
                t_s = t_y = None
                for c in range(NC):
                    v_c = TR[:, c * P:c * P + P]
                    by = (L1_, L2_)[c]
                    b.wait("pe", t_t, t_s, t_gkm)
                    if c:
                        mm(bank(L0_, 0, P), AR[:, 256:256 + C], ST, True, False)
                    for e in range(2):
                        ins = mm(bank(L0_, e * 64, 64), gk4[:, 2 * e + c, 0, :], v_c[:, e * 64:e * 64 + 64], c == 0, e == 1 or c == 0)
                    t = A(R0, bank(L0_, 0, P), ACT.Copy, after=[b.pe(ins)], chain=False)
                    for e in range(2):
                        mm(bank(by, e * P, P), v_c, gk4[:, 2 * e + c, 1, :], e == 0, False)
                        if c:
                            mm(bank(by, e * P, P), ST, AR[:, 256 + C:256 + 2 * C], False, False)
                    if c == 0:
                        mm(bank(L2_, 0, P), TR[:, 256:384], v_c, True, False)
                    yield
                    b.wait("pe", t)
                    for e in range(2):
                        ins = mm(bank(L0_, 128 + e * 64, 64), XT[:, (2 * e + c) * C:(2 * e + c) * C + C],
                                 R0[:, e * 64:e * 64 + 64], True, True)
                    t = A(SA, bank(L0_, 128, P), ACT.Copy, after=[b.pe(ins)], chain=False)
                    yield
                    b.wait("pe", t)
                    if c == 0:
                        ins = mm(bank(L2_, 0, P), TR[:, 384:512], SA, False, True)
                        t_s = V("scalar_tensor_tensor", ST, bank(L2_, 0, P), fac[:, bass.ds(i * 2 + w.p, 1)], cc("head_sum"),
                                ALU.mult, ALU.mult, after=[b.pe(ins)], chain=False)
                    for e in range(2):
                        ins = mm(bank(by, e * P, P), SA, gb4[:, 2 * e + c, 1, :], False, e == 1)
                    t_y = b.pe(ins)
                    for e in range(2):
                        p_ = slice(64 * e, 64 * e + 64)
                        V("tensor_scalar", CS[p_, bass.ds(i * (2 * T) + (w.p * T + c * C), C)], psum[p_, by, e * P:e * P + P], 1.0, None,
                          ALU.mult, after=[t_y], chain=False)
                    yield

            def side_steps(i):
                for u in range(SIDE):
                    b.wait("sp", slot_free())
                    full = fetch(M_ADA, i * SIDE + u)
                    for part in range(2):
                        b.wait("act", full, piece_free())
                        b.wait("dve", round_piece(M_ADA, part))
                        rest_of_piece(M_ADA, part)
                    yield
                    b.wait("pe", b.slab_out.here())
                    for part in range(2):
                        b.wait("pe", piece_ready())
                        done = multiply_conditions(part, 7)
                    ev_ada(i * SIDE + u, psum[0:4, 7, 0:256], done)
                    yield

            per = {b.c["pe"]: 2 * 27 + SIDE, b.c["act"]: 2 * 15 + SIDE, b.c["dve"]: 2 * 28, b.c["pool"]: 12, b.slab_out: SIDE,
                   b.piece_hi: 2 * SIDE, b.piece_lo: 2 * SIDE, b.piece_done: 2 * SIDE}
            per.update({c: 16 * SIDE // RING for c in b.slot_full})
            with b.loop(DT // 2, per) as i:
                streams = [side_steps(i), pair_steps(i, pairs[0]), pair_steps(i, pairs[1])]
                next(streams[1])
                while streams:
                    for st in list(streams):
                        if next(st, 1) == 1:
                            streams.remove(st)
            tap("ywkv", CS[:, :])
            Y = CS[:, :]
            b.join()
            PB.close()
            ms = Split(16 * T, S2, "mixed")
            eight = psum[:, 0:4, :].rearrange("p b n -> p (b n)")
            t_m, _ = mean_over(Y, T, "head_mean", DT, 1, 0)
            V("tensor_tensor", KK[:, :], Rr, Kr, ALU.mult)
            t_rk = V("tensor_tensor", tiles(KK[:, :], T), tiles(KK[:, :], T), cols(vv("r_k"), T), ALU.mult)
            t = V("tensor_tensor", Y, Y, eight, ALU.subtract, after=[t_m])
            t_sq = A(SG[:, :], Y, ACT.Square, after=[t])
            b.wait("pe", t_rk)
            t_b, _ = mean_over(KK, T, "head_sum", DT, 1, 4)
            b.wait("pe", t_sq)
            t_v, _ = mean_over(SG, T, "head_mean", DT, 1, 0)
            t = A(BV[:, :], eight, ACT.Ln, bias=eps_cols[:, 4:5], after=[t_v])
            t_r = A(BV[:, :], BV[:, :], ACT.Exp, scale=-0.5)
            V("tensor_tensor", KK[:, :], Vr, psum[:, 4:8, :].rearrange("p b n -> p (b n)"), ALU.mult, after=[t_b])
            b.wait("pe", t)
            for k in range(DT):
                ins = mm(bank(k // 2, (k % 2) * T, T), g2[:, k * P:k * P + P], gl, True, True)
            t_g = b.pe(ins)
            ms.set(mix[:, :])
            V("tensor_tensor", Y, Y, BV[:, :], ALU.mult, after=[t_r])
            t = b.c["dve"].here()
            for k in range(DT):
                yk = Y[:, k * T:k * T + T]
                if k % 2:
                    t_a = A(yk, yk, ACT.Identity, scale=vv("lnx_g", k, 1), bias=vv("lnx_b", k, 1), after=[t], chain=False)
                else:
                    V("tensor_scalar", yk, yk, vv("lnx_g", k, 1), vv("lnx_b", k, 1), ALU.mult, ALU.add, after=[t], chain=False)
            V("tensor_tensor", Y, Y, KK[:, :], ALU.add, after=[t_a])
            t = V("tensor_tensor", Y, Y, eight, ALU.mult, after=[t_g])
            tap("yrwkv", Y)
            ms.set(Y, DT * T, after=[t])
            residual_linear(M_MIX0, feature(ms, T), M_KV[0])

    Kall = sb(DT * T, FB, "mem_k")
    Vall = sb(2 * D, FB, "mem_v")
    Mx = Split(DT * T, FB, "mem")
    b.join()
    raw_mem = load(Kall[:, :], dram["mem"], "mem")

    def ev_kv(j, ap, tok):
        A(at(Kall, j, T), ap[:, 0:T], ACT.Copy, after=[tok], chain=False)
        d = tiles(Vall[:, :], D)[:, :, bass.ds(j * P, P)]
        leave("act", nc.scalar.activation, d, tiles(ap[:, T:2 * T], P), ACT.Copy)

    def after_mix(layer, after_=None):
        with ExitStack() as s:
            Q, O, xs_ = sb(DT * T, s, "q"), Split(DT * T, s, "o"), Split(DT * T, s)
            ready = layer_norm("mix_g", "mix_b", layer, xs_,
                               meanwhile=None if layer else lambda: Mx.set(Kall[:, :], after=[raw_mem]))
            tap(f"mix{layer}", X[:, :])
            b.join()
            linear(M_KV[layer], feature(Mx, T), T, ev_kv, M_XQ[layer], product=multiply_kv, mid={"act": 1})
            linear(M_XQ[layer], feature(xs_, T), T, copy_out(Q), M_XO[layer])
            b.join()
            S = sb(8 * T, s, "probs")
            PT = sb(8 * T, s, "probs_t")
            st = sb(16, s, "stats")
            groups = ((0, 1), (2, 3))
            t_s, t_e, t_p = [], [], []
            for hs in groups:
                for h in hs:
                    for qt in range(2):
                        for dd in range(2):
                            k = 2 * h + dd
                            ins = mm(bank(h, qt * T, T), Q[:, k * T + qt * P:k * T + qt * P + P],
                                     Kall[:, k * T:(k + 1) * T], dd == 0, dd == 1)
                t_s.append(b.pe(ins))
            part = lambda a, g: a[:, g * 4 * T:(g + 1) * 4 * T]
            for g in range(2):
                t = V("tensor_copy", part(S, g), psum[:, 2 * g:2 * g + 2, :].rearrange("p b n -> p (b n)"), after=[t_s[g]])
                t_e.append(softmax_exp(tiles(part(S, g), T), 4, 256 ** -0.5, st[:, 4 * g:4 * g + 4], st[:, 8 + 4 * g:12 + 4 * g], [t]))
            for g, hs in enumerate(groups):
                t = softmax_divide(tiles(part(S, g), T), T, st[:, 8 + 4 * g:12 + 4 * g], [t_e[g]])
                t_p.append(transpose_probs(S, PT, hs, t))
            for g, hs in enumerate(groups):
                b.wait("pe", t_p[g])
                for k in range(4 * g, 4 * g + 4):
                    for kt in range(2):
                        v = Vall[:, kt * D + k * P:kt * D + k * P + P]
                        ins = mm(bank(k // 2, (k % 2) * T, T), v, PT[:, (2 * (k // 2) + kt) * T:(2 * (k // 2) + kt + 1) * T],
                                 kt == 0, kt == 1)
            O.set(psum[:, 0:4, :].rearrange("p b n -> p (b n)"), after=[b.pe(ins)])
            residual_linear(M_XO[layer], feature(O, T), M_W13[layer])
        with ExitStack() as s:
            xs_ = Split(DT * T, s)
            ready = layer_norm("xa_g", "xa_b", layer, xs_)
            tap(f"xa{layer}", X[:, :])
            ffn([M_W13[layer]], xs_, T, [M_W2[layer]],
                lambda w2, h, then: residual_linear(w2, feature(h, T), then, halves=2), (M_Q, M_C1)[layer], ready)
        layer_norm("ffn_g", "ffn_b", layer, after_)
        b.join()
        tap(f"ffn{layer}", X[:, :])

    L1 = ExitStack()
    xs_ = Split(DT * T, L1)
    after_mix(0, xs_)

    with L1 as s:
        Q, K, O = (sb(DT * T, s, n) for n in ("q", "k", "o"))
        Vt = sb(2 * D, s, "v_tok")
        am = sb(2 * T, s, "causal")
        b.join()
        tm = load(am[:, :], dram["causal"], "causal")
        linear(M_Q, feature(xs_, T), T, copy_out(Q), M_K)
        linear(M_K, feature(xs_, T), T, copy_out(K), M_V)
        linear(M_V, feature(xs_, T), T, copy_tokens(Vt[:, :], 2, D), M_AOUT, product=multiply_tokens)
        b.join()
        Qs, Ks, Vs = sb(2 * T, s, "q_heads"), sb(2 * T, s, "k_heads"), sb(2 * 2 * P, s, "v_heads")
        S, PT = sb(8 * T, s, "probs"), sb(8 * T, s, "probs_t")
        st = sb(16, s, "stats")
        b.wait("dve", tm)
        S3 = S[:, :].rearrange("p (h q k) -> p h q k", h=4, q=2)
        groups = ((0, 1), (2, 3))
        warm(ACT.Exp)
        with b.loop(4, {b.c["pe"]: 5, b.c["act"]: 13, b.c["dve"]: 14}) as i:
            t1 = A(Qs[:, :], at(Q, i, 2 * T), ACT.Copy, chain=False, after=[b.before("pe")])
            t2 = A(tiles(Vs[:, :], 256), tiles(Vt[:, :], D)[:, :, bass.ds(i * 256, 256)], ACT.Copy, chain=False)
            t3 = V("tensor_copy", Ks[:, :], at(K, i, 2 * T), after=[b.before("pe")], chain=False)
            b.wait("pe", t1, t2, t3, b.before("dve"))
            t_s, t_e, t_p = [], [], []
            for hs in groups:
                for h in hs:
                    p_ = slice(64 * (h % 2), 64 * (h % 2) + 64)
                    for qt in range(2):
                        ins = mm(bank(h, qt * T, T), Qs[p_, (h // 2) * T + qt * P:(h // 2) * T + qt * P + P],
                                 Ks[p_, (h // 2) * T:(h // 2) * T + T], True, True)
                t_s.append(b.pe(ins))
            part = lambda a, g: a[:, g * 4 * T:(g + 1) * 4 * T]
            for g, hs in enumerate(groups):
                for h in hs:
                    t = V("tensor_tensor", S[:, h * 2 * T:(h + 1) * 2 * T], bank(h), am[:, :], ALU.add, after=[t_s[g], t2], chain=False)
                t_e.append(softmax_exp(tiles(part(S, g), T), 4, HD ** -0.5, st[:, 4 * g:4 * g + 4], st[:, 8 + 4 * g:12 + 4 * g], [t]))
            for g, hs in enumerate(groups):
                t = softmax_divide(tiles(part(S, g), T), T, st[:, 8 + 4 * g:12 + 4 * g], [t_e[g]])
                t_p.append(transpose_probs(S, PT, hs, t))
            for g, hs in enumerate(groups):
                b.wait("pe", t_p[g])
                for h in hs:
                    for kt in range(2):
                        ins = mm(bank(h, 0, T), Vs[:, kt * 256 + (h // 2) * P:kt * 256 + (h // 2) * P + P],
                                 PT[:, (2 * h + kt) * T:(2 * h + kt + 1) * T], kt == 0, kt == 1)
            t = b.pe(ins)
            Oi = tiles(at(O, i, 2 * T), T)
            for hh in range(2):
                p_ = slice(64 * hh, 64 * hh + 64)
                src = psum[p_, 0:4, 0:T].rearrange("p (a e) n -> p a e n", e=2)[:, :, hh, :]
                if hh == 0:
                    t_o = V("tensor_copy", Oi[p_, :, :], src, after=[t], chain=False)
                else:
                    A(Oi[p_, :, :], src, ACT.Copy, after=[t, t_o], chain=False)
        b.join()
        xs_.set(O[:, :])
        residual_linear(M_AOUT, feature(xs_, T), M_KV[1])
    after_mix(1)

    FB.close()
    R = sb(DT * 2 * T, name="streams")
    r4 = R[:, :].rearrange("p (t s n) -> p t s n", s=2, n=T)
    b.join()
    t = load(r4[:, :, 0, :], dram["ctx"].rearrange("p (t n) -> p t n", n=T), "ctx")
    V("tensor_copy", r4[:, :, 1, :], tiles(X[:, :], T))
    for e in ("act", "dve"):
        b.wait(e, t)
    b.join()

    def mod(layer, part, lo=0, n=16):
        o = layer * 96 + part * 16 + lo
        return mods[:, o:o + n]

    def modulate(src, dst, ns, layer, gain, part, work=None):
        with ExitStack() as s:
            gm = sb(16, s, "gain")
            b.join()
            V("tensor_scalar", gm[:, :], mod(layer, part + 1), 1.0, None, ALU.add)
            t = V("tensor_tensor", tiles(gm[:, :], 2), tiles(gm[:, :], 2), cols(vv(gain, 8 * layer, 8), 2), ALU.mult)
            col = (lambda k: k) if ns == 2 else (lambda k: 2 * k + 1)
            return norm(src, None, ns * T, EPS6, lambda k: gm[:, col(k):col(k) + 1], lambda k: mod(layer, part, col(k), 1),
                 dst, work=work)

    def gated_linear(m, x, then, layer, part, follows_norm=False):
        if not follows_norm:
            b.join()
        width, mo = m.mo * 2 * T, m.mo
        with ExitStack() as s:
            tmp = sb(4 * width, s)

            def evac(j, ap, tok):
                tm = tmp[:, 0:width]
                gates = mods[:, bass.ds(layer * 96 + part * 16 + j * (2 * mo), 2 * mo)]
                t = V("tensor_tensor", tiles(tm, T), tiles(ap, T), cols(gates, T), ALU.mult,
                      after=[tok, b.slab_out.here()], chain=False)
                leave("dve", nc.vector.tensor_tensor, at(R, j, width), at(R, j, width), tm, ALU.add, after=[t])
            linear(m, x, 2 * T, evac, then, mid={"dve": 1})
            b.join()


    with ExitStack() as s:
        W2 = 2 * T
        PW = T + 2 * PAD
        hm = Split(DT * W2, s, "modulated")
        YP = sb(DT * 2 * PW, s, "glu_padded")
        sg = sb(4 * W2, s, "sig")
        acc = sb(DT * W2, s, "conv")
        yp3 = tiles(YP[:, :], PW)
        V("memset", YP[:, :], 0.0)
        ready = modulate(R[:, :], hm, 2, 0, "norm_mix", 0)
        ob = VOFF["conv_b1"][0]

        def ev_glu(j, ap, tok):
            ph = (b.piece_done.n // 2 - 1) % 4
            gt = sg[:, ph * W2:ph * W2 + W2]
            n = b.slab_out.n
            t = A(gt, ap[:, W2:2 * W2], ACT.Sigmoid, bias=vec[:, bass.ds(j + (ob + 8), 1)], chain=False,
                  after=[tok, Tok(b.slab_out, n - 3, b.slab_out.loop)])
            leave("dve", nc.vector.scalar_tensor_tensor, yp3[:, bass.ds(j * 2, 2), PAD:PAD + T],
                  tiles(ap[:, 0:W2], T), vec[:, bass.ds(j + ob, 1)], tiles(gt, T), ALU.add, ALU.mult, after=[t])
        linear(M_C1, feature(hm, W2, ready=ready), W2, ev_glu, M_C2, mid={"act": 1})
        b.join()
        od = VOFF["conv_dw"][0]
        DVE_N, PE_0 = 4, 5
        PE_N = DT - PE_0
        diag = [sb(PE_N * P, s, "diagonals") for _ in range(2)]
        prod = sb(W2, s, "tap_product")

        def taps_of(k, first, last, old):
            d = diag[b.diags % 2]
            b.diags += 1
            w_ = lambda t: vec[:, bass.ds(k * 8 + (od + t), 1)]
            src = lambda t: yp3[:, 2 * t:2 * t + 2, bass.ds(k, T)]
            for q in range(PE_N):
                t = V("tensor_scalar", d[:, q * P:q * P + P], cc("ident"), w_(PE_0 + q), None, ALU.mult,
                      after=[old], chain=False)
            b.wait("pe", t)
            for q in range(PE_N):
                ins = mm(bank(q), d[:, q * P:q * P + P], src(PE_0 + q), first, last)
            b.pe(ins)
            b.wait("dve", None if first else b.dw_sum)
            for t in range(DVE_N):
                a_t = tiles(at(acc, t, W2), T)
                if first:
                    b.dw_sum = V("tensor_scalar", a_t, src(t), w_(t), vv("conv_dw_b", t, 1), ALU.mult, ALU.add, chain=False)
                else:
                    V("scalar_tensor_tensor", a_t, src(t), w_(t), a_t, ALU.mult, ALU.add, chain=False)
            b.dw_sum = b.c["dve"].here()
            t = DVE_N
            a_t = tiles(at(acc, t, W2), T)
            wt = w_(t).rearrange("p (a o) -> p a o", o=1).broadcast_to([P, 2, T])
            if first:
                G("tensor_tensor", a_t, src(t), wt, ALU.mult)
            else:
                G("tensor_tensor", tiles(prod[:, :], T), src(t), wt, ALU.mult)
                G("tensor_tensor", a_t, a_t, tiles(prod[:, :], T), ALU.add)

        b.diags = 0
        taps_of(0, True, False, None)
        taps_of(1, False, False, None)
        n_loop = (CONV_W - 3) // 2
        with b.loop(n_loop, {b.c["dve"]: 2 * (PE_N + DVE_N), b.c["pe"]: 2, b.c["pool"]: 4}) as i:
            for u in range(2):
                b.dw_sum = b.c["dve"].here()
                taps_of(i * 2 + (2 + u), False, False, b.c["pe"].value(b.c["pe"].n - 1))
        for k in range(2 + 2 * n_loop, CONV_W):
            taps_of(k, False, k == CONV_W - 1, b.c["pe"].value(b.c["pe"].n - 1))
        b.join()
        a_g = at(acc, DVE_N, W2)
        V("tensor_scalar", a_g, a_g, vv("conv_dw_b", DVE_N, 1), None, ALU.add, chain=False)
        for q in range(PE_N):
            V("tensor_scalar", at(acc, PE_0 + q, W2), bank(q), vv("conv_dw_b", PE_0 + q, 1), None, ALU.add, chain=False)
        b.join()
        tap("dwconv", acc[:, :])
        ready = norm(acc, acc, W2, EPS6, lambda k: vv("conv_norm", k // 2, 1), lambda k: 0.0, hm, centre=True, func=ACT.Silu)
        gated_linear(M_C2, feature(hm, W2, ready=ready), M_GU0[0], 0, 2, follows_norm=True)
    tap("convout", R[:, :])
    with ExitStack() as s:
        hm = Split(DT * 2 * T, s, "modulated")
        ready = modulate(R[:, :], hm, 2, 0, "norm_ffn", 3)
        ffn(M_GU0, hm, 2 * T, M_DOWN0,
            lambda w2, h, then: gated_linear(w2, feature(h, 2 * T), then, 0, 5), M_RQ, ready)
    tap("l0out", R[:, :])

    def gated_x(m, x, then, layer, part, halves=1):
        b.join()
        def evac(j, ap, tok):
            gate = mods[:, bass.ds(j * 2 + (layer * 96 + part * 16 + 1), 1)]
            leave("dve", nc.vector.scalar_tensor_tensor, at(X, j, T), ap, gate, at(X, j, T), ALU.mult, ALU.add, after=[tok])
        linear(m, x, T, evac, then, halves=halves)
        b.join()

    with ExitStack() as s:
        V("tensor_copy", tiles(X[:, :], T), r4[:, :, 1, :])
        QX, KX = sb(DT * T, s, "q"), sb(DT * 2 * T, s, "k")
        Vt = sb(4 * 2048, s, "v_tok")
        Gt, O = sb(16 * T, s, "gate"), sb(16 * T, s, "o")
        with ExitStack() as s2:
            hm = Split(DT * 2 * T, s2, "modulated")
            ready = modulate(R[:, :], hm, 2, 1, "norm_mix", 0, work=(O, QX))
            xs = feature(hm, 2 * T, T, T, ready=ready)

            def ev_g(j, ap, tok):
                leave("act", nc.scalar.activation, at(Gt, j, 512), ap, ACT.Silu, after=[tok])
            linear(M_RQ, xs, T, copy_out(QX), M_RK)
            linear(M_RK, feature(hm, 2 * T), 2 * T, copy_out(KX, 1024), M_RV)
            linear(M_RV, feature(hm, 2 * T), 2 * T, copy_tokens(Vt[:, :], 4, 2048), M_RG, product=multiply_tokens)
            linear(M_RG, xs, T, ev_g, M_ROUT)
            b.join()
        with ExitStack() as s2:
            dist, rope = sb(12 * T, s2, "dist"), sb(4 * T, s2, "rope")
            t = load(rope[:, :], dram["rope"], "rope")
            t_dist = load(dist[:, :], dram["dist"], "dist")
            b.wait("dve", t)
            tmp = O[:, 0:DT * T]
            tab = rope[:, :].rearrange("p (w m n) -> p w m n", w=2, m=2)
            kx4 = KX[:, :].rearrange("p (h m s n) -> p h m s n", m=2, s=2, n=T)
            for dst, src, width in ((QX[:, :].rearrange("p (h m n) -> p h m n", m=2, n=T), QX, T),
                                    (kx4[:, :, :, 1, :], KX, 2 * T)):
                for k in range(DT):
                    ins = mm(bank(k // 2, (k % 2) * T, T), cc("swap"), src[:, k * width + width - T:(k + 1) * width], True, True)
                t = b.pe(ins)
                tp = tmp.rearrange("p (h m n) -> p h m n", m=2, n=T)
                tb = lambda w: tab[:, w:w + 1, :, :].broadcast_to([P, 4, 2, T])
                V("tensor_tensor", tp, psum[:, 0:4, :].rearrange("p b (m n) -> p b m n", m=2), tb(1), ALU.mult, after=[t])
                V("tensor_tensor", dst, dst, tb(0), ALU.mult)
                V("tensor_tensor", dst, dst, tp, ALU.add)
                b.join()
            dw = sb(5 * 8, s2)
            w_ = [dw[:, i * 8:i * 8 + 8] for i in range(5)]
            log1p_exp_neg_abs(vv("decay"), w_[0], w_[1], w_[2])
            V("tensor_scalar", w_[3], vv("decay"), 0.0, None, ALU.min)
            lg = w_[3]
            t_lg = V("tensor_tensor", lg, lg, w_[2], ALU.subtract)
            WF, WB, SW = sb(4 * T, s2, "w_fwd"), sb(4 * T, s2, "w_bwd"), sb(4 * T, s2, "weights")
            b.wait("act", t_dist)
            b.wait("dve", t_dist)
            rs = sb(2 * T, s2, "rstd")

            def sum_squares(h, t_sq):
                b.wait("pe", t_sq)
                for k in range(4):
                    ins = mm(bank(4 + h % 2, 0, T), cc("ones_half"), R[:, (4 * h + k) * T:(4 * h + k + 1) * T], k == 0, k == 3)
                return b.pe(ins)

            def scale_head(h, t_ss):
                t = A(rs[:, 0:T], bank(4 + h % 2, 0, T), ACT.Sqrt, bias=EPS_COL[EPS6], after=[t_ss, *inverted])
                inverted[:] = [V("reciprocal", rs[:, T:2 * T], rs[:, 0:T], after=[t])]
                oh = slice(h * 4 * T, (h + 1) * 4 * T)
                V("tensor_tensor", tiles(O[:, oh], T), tiles(O[:, oh], T), rows(rs[:, T:2 * T], 4), ALU.mult)
                V("tensor_tensor", O[:, oh], O[:, oh], Gt[:, oh], ALU.mult)

            t_sw = t_o = t_sq = None
            inverted = []
            for h in range(4):
                t = A(WF[:, :], dist[:, 0:4 * T], ACT.Exp, scale=lg[:, h:h + 1], after=[t_lg, t_sw])
                t2 = A(WB[:, :], dist[:, 4 * T:8 * T], ACT.Exp, scale=lg[:, 4 + h:5 + h], chain=False)
                b.wait("pe", t_sw)
                for st_ in range(4):
                    for dd in range(2):
                        k = 2 * h + dd
                        ins = mm(bank(st_ // 2, (st_ % 2) * T, T), KX[:, k * 512 + st_ * P:k * 512 + st_ * P + P],
                                 QX[:, k * T:k * T + T], dd == 0, dd == 1)
                tq = b.pe(ins)
                t_ss = sum_squares(h - 1, t_sq) if h else None
                V("tensor_tensor", WF[:, 2 * T:], WF[:, 2 * T:], dist[:, 8 * T:10 * T], ALU.mult, after=[t])
                V("tensor_tensor", WB[:, 2 * T:], WB[:, 2 * T:], dist[:, 10 * T:12 * T], ALU.mult, after=[t2])
                V("tensor_tensor", WF[:, :], WF[:, :], WB[:, :], ALU.add)
                t_sw = V("scalar_tensor_tensor", SW[:, :], psum[:, 0:2, :].rearrange("p b n -> p (b n)"), 256 ** -0.5, WF[:, :],
                         ALU.mult, ALU.mult, after=[tq])
                b.wait("pe", t_sw, t_o)
                for m in range(4):
                    for st_ in range(4):
                        ins = mm(bank(2 + m // 2, (m % 2) * T, T), Vt[:, st_ * 2048 + h * 512 + m * P:st_ * 2048 + h * 512 + m * P + P],
                                 SW[:, st_ * T:st_ * T + T], st_ == 0, st_ == 3)
                t_pv = b.pe(ins)
                if h:
                    scale_head(h - 1, t_ss)
                oh = slice(h * 4 * T, (h + 1) * 4 * T)
                t_o = A(O[:, oh], psum[:, 2:4, :].rearrange("p b n -> p (b n)"), ACT.Copy, after=[t_pv])
                t_sq = A(R[:, oh], O[:, oh], ACT.Square, after=[t_o])
            scale_head(3, sum_squares(3, t_sq))
            b.join()
        os_ = Split(16 * T, s, "o")
        os_.set(O[:, :])
        gated_x(M_ROUT, feature(os_, T), M_GU1, 1, 2)
    tap("mods", mods[:, :])
    tap("retout", X[:, :])
    with ExitStack() as s:
        hm = Split(DT * T, s, "modulated")
        ready = modulate(X[:, :], hm, 1, 1, "norm_ffn", 3)
        ffn([M_GU1], hm, T, [M_DOWN1], lambda w2, h, then: gated_x(w2, feature(h, T), then, 1, 5, halves=2), None, ready)
    b.wait("sp", *b.all())
    done = load(out, X[:, :], "out")
    b.wait("sp", done)


def slabs(w, kt, groups, by_k=False):
    t = w.reshape(-1, P, w.shape[1] // P, P)
    out = []
    for g in groups:
        for lo in range(0, t.shape[0], kt):
            order = (1, 0, 2, 3) if by_k else (1, 2, 0, 3)
            out.append(t[lo:lo + kt][:, :, list(g), :].transpose(order).reshape(P, -1))
    return np.ascontiguousarray(np.stack(out))


def arrange(inp):
    def feat(x):
        return np.ascontiguousarray(x.T.reshape(DT, P, -1).transpose(1, 0, 2).reshape(P, -1))

    def col(v):
        return np.asarray(v).reshape(-1, P).T
    two = lambda n, o=0: [(o + 2 * i, o + 2 * i + 1) for i in range(n)]
    one = lambda n: [(i,) for i in range(n)]
    pair = lambda n: [(i, n + i) for i in range(n)]
    d = {"x": feat(inp["x"][0]), "mem": feat(inp["mem"][0]), "ctx": feat(inp["ctx_2"][0])}
    w = inp["even_w_in"][0]
    main = np.concatenate([w[:, :2560], w[:, 2576:]], axis=1)
    d["w_in"] = slabs(main, 8, two(23))
    d["w_dt"] = np.ascontiguousarray(w[:, 2560:2576].reshape(DT, P, 16).transpose(1, 0, 2).reshape(P, -1))
    d["w2a2"], d["g2"] = np.concatenate([inp["rwkv_w2"][0], inp["rwkv_a2"][0]], axis=0), inp["rwkv_g2"][0]
    d["w_mix0"] = slabs(inp["even_w_out"][0], 16, one(8))
    kv = inp["xa_wkv"]
    for l in range(2):
        d[f"w_kv{l}"] = slabs(kv[l], 8, pair(8))
    d["w_ada"] = np.concatenate([slabs(inp["ada_w_2"][l], 8, two(24), True) for l in range(2)])
    for l in range(2):
        d[f"w_xq{l}"] = slabs(inp["xa_wq"][l], 8, two(4))
        d[f"w_xo{l}"] = slabs(inp["xa_wo"][l], 8, two(4))
        d[f"w13_{l}"] = slabs(inp["ffn_w13"][l], 8, pair(FFN_T))
        d[f"w2_{l}"] = slabs(inp["ffn_w2"][l], 11, one(8))
        d[f"gu_{l}"] = slabs(inp["ffn_w_gu_2"][l], 8, pair(FFN_T))
        down = inp["ffn_w_down_2"][l]
        d[f"down_{l}"] = slabs(down, 11, one(8)) if l else \
            np.concatenate([slabs(down[:11 * P], 11, one(8)), slabs(down[11 * P:], 11, one(8))])
    qkv = inp["odd_w_qkv"][0]
    d["w_qkv"] = np.concatenate([slabs(qkv[:, :2 * D], 8, two(8)), slabs(qkv[:, 2 * D:], 8, two(4), True)])
    d["w_aout"] = slabs(inp["odd_w_out"][0], 8, two(4))
    d["w_c1"] = slabs(inp["conv_w1_2"][0], 8, pair(8))
    d["w_c2"] = slabs(inp["conv_w2_2"][0], 8, two(4))
    ret = inp["ret_w_in_2"][0]
    d["w_ret"] = np.concatenate([slabs(ret[:, :2 * D], 8, two(8)), slabs(ret[:, 2 * D:4 * D], 8, two(8), True),
                                 slabs(ret[:, 4 * D:], 8, two(8))])
    d["w_rout"] = slabs(inp["ret_w_out_2"][0], 16, one(8))
    heads = np.zeros((P, 2), np.float32)
    heads[:NH, 0], heads[:NH, 1] = inp["ssd_dt_bias"][0], inp["ssd_a_log"][0]
    cond = np.stack([col(inp["c_ctx_2"]), col(inp["c_2"][0])], axis=2).reshape(P, -1)
    decay = np.broadcast_to(np.concatenate([inp["ret_decay_f_2"][0], inp["ret_decay_b_2"][0]]), (P, 8))
    v = {
        "conv_w": np.concatenate([col(inp["ssd_conv_w"][0][k]) for k in range(4)], axis=1),
        "conv_b": col(inp["ssd_conv_b"][0]), "ssd_d": col(np.repeat(inp["ssd_d"][0], HD)),
        "ssd_g": col(inp["ssd_norm_g"][0]), "mu": col(inp["rwkv_mu"][0]), "w0": col(inp["rwkv_w0"][0]),
        "a0": col(inp["rwkv_a0"][0]), "k_k": col(inp["rwkv_k_k"][0]), "k_a": col(inp["rwkv_k_a"][0]),
        "r_k": col(inp["rwkv_r_k"][0].reshape(-1)), "lnx_g": col(inp["rwkv_lnx_g"][0]),
        "lnx_b": col(inp["rwkv_lnx_b"][0]), "mix_g": col(inp["ln_mix_g"]), "mix_b": col(inp["ln_mix_b"]),
        "xa_g": col(inp["ln_xa_g"]), "xa_b": col(inp["ln_xa_b"]), "ffn_g": col(inp["ln_ffn_g"]),
        "ffn_b": col(inp["ln_ffn_b"]), "cond": cond, "ada_b": col(inp["ada_b_2"]),
        "norm_mix": col(inp["norm_mix_2"]), "norm_ffn": col(inp["norm_ffn_2"]), "conv_b1": col(inp["conv_b1_2"]),
        "conv_dw": np.concatenate([col(inp["conv_dw_2"][0][k]) for k in range(CONV_W)], axis=1),
        "conv_dw_b": col(inp["conv_dw_b_2"]), "conv_norm": col(inp["conv_norm_2"]), "heads": heads, "decay": decay,
    }
    d["vectors"] = np.concatenate([v[n] for n, _ in VECTORS], axis=1)
    assert d["vectors"].shape[1] == NVEC
    d["consts"] = shape_constants()
    d["causal"] = attention_masks()
    d["dist"], d["rope"] = retention_constants()
    return {k: np.ascontiguousarray(a, dtype=np.float32) if a.dtype == np.float32 else a for k, a in d.items()}


def build(nc, arrays, tap_shapes=None):
    dram = {n: nc.dram_tensor(f"in_{n}", a.shape, F32, kind="ExternalInput").ap() for n, a in arrays.items()}
    out = nc.dram_tensor("out", (P, DT * T), F32, kind="ExternalOutput").ap()
    taps = {n: nc.dram_tensor(f"tap_{n}", s, F32, kind="ExternalOutput").ap() for n, s in (tap_shapes or {}).items()}
    program(nc, dram, out, taps)


def kernel(**inputs):
    import concourse.bacc as _bacc
    from concourse.bass_utils import run_bass_kernel_spmd as _run

    arrays = arrange({k: np.asarray(v) for k, v in inputs.items()})
    nc = _bacc.Bacc("TRN2", target_bir_lowering=False, num_devices=1)
    build(nc, arrays)
    r = _run(nc, [{f"in_{n}": a for n, a in arrays.items()}], core_ids=[0])
    y = r.results[0]["out"]
    return y.reshape(P, DT, T).transpose(1, 0, 2).reshape(D, T).T.reshape(1, T, D)
```
